# Optimizing a Trainium2 kernel written in Bass

```python
import math
import jax
import jax.numpy as jnp
from jax import lax
import numpy as np

D_MODEL = 1024
BATCH = 1
SEQ = 1024
DEPTH = 2
DEC_BATCH = 8
DEC_SEQ = 8
PAST_LEN = 1024
PAGE_SIZE = 128

N_EVEN = (DEPTH + 1) // 2
N_ODD = DEPTH // 2
MIX_HALF = D_MODEL // 2
HG_HEADS = 4
HG_DK = MIX_HALF // HG_HEADS
HG_DV = MIX_HALF // HG_HEADS
HG_CHUNK = 64
SB_HEADS = 8
SB_HD = MIX_HALF // SB_HEADS
SB_QBLOCK = 128
SB_BIAS_INIT = -7.0
POOL_WINDOWS = (2, 4, 8, 16)
POOL_GROUPS = len(POOL_WINDOWS)
POOL_GC = MIX_HALF // POOL_GROUPS
POOL_HIST = max(POOL_WINDOWS) - 1
CONV_CH = MIX_HALF
CONV_WIDTH = 31
CONV_HIST = CONV_WIDTH - 1
D_FF = 4 * D_MODEL
HG_QK = HG_HEADS * HG_DK
HG_V = HG_HEADS * HG_DV
SB_W = SB_HEADS * SB_HD
EVEN_IN = 2 * HG_QK + 2 * HG_V + 3 * SB_W
ODD_IN = MIX_HALF + 2 * CONV_CH
EPS = 1e-6
F32 = jnp.float32

kernel_name = 'hybrid_hgrn2_stickbreak_pool_conformer_step'

def rms_norm(x, g):
    xf = x.astype(F32)
    y = xf * lax.rsqrt(jnp.mean(xf * xf, axis=-1, keepdims=True) + EPS)
    return (y * g.astype(F32)).astype(x.dtype)

def mlp(h, w1, w2):
    return jnp.square(jax.nn.relu(h @ w1)) @ w2

def stick_breaking(q, k, v, bias, q_start):
    B, Tq, H, d = q.shape
    Tk = k.shape[1]
    blk = math.gcd(Tq, SB_QBLOCK)
    nb = Tq // blk
    qb = q.reshape(B, nb, blk, H, d).transpose(1, 0, 2, 3, 4)
    k_pos = jnp.arange(Tk)
    kf = k.astype(F32)
    vf = v.astype(F32)
    scale = d ** -0.5
    bf = bias.astype(F32)[None, :, None, None]

    def one_block(args):
        qi, bi = args
        q_pos = q_start + bi * blk + jnp.arange(blk)
        z = jnp.einsum('bqhd,bkhd->bhqk', qi.astype(F32), kf) * scale + bf
        mask = k_pos[None, :] < q_pos[:, None]
        log_beta = jax.nn.log_sigmoid(z)
        log_keep = jnp.where(mask, jax.nn.log_sigmoid(-z), 0.0)
        later = lax.cumsum(log_keep, axis=3, reverse=True) - log_keep
        w = jnp.where(mask, jnp.exp(log_beta + later), 0.0)
        return jnp.einsum('bhqk,bkhd->bqhd', w, vf)

    o = lax.map(one_block, (qb, jnp.arange(nb)))
    return o.transpose(1, 0, 2, 3, 4).reshape(B, Tq, H, d).astype(q.dtype)

def hgrn2(q, f_logit, val, lb, S0):
    B, T, H, DK = q.shape
    DV = val.shape[-1]
    C = math.gcd(T, HG_CHUNK)
    n = T // C
    lbf = lb.astype(F32)
    fl = f_logit.astype(F32)
    log_f = jnp.logaddexp(jnp.log(lbf), jnp.log1p(-lbf) + jax.nn.log_sigmoid(fl))
    k = (1.0 - lbf) * jax.nn.sigmoid(-fl)

    def to_chunks(a):
        return a.astype(F32).reshape(B, n, C, H, a.shape[-1]).transpose(1, 0, 3, 2, 4)

    causal = jnp.tril(jnp.ones((C, C), bool))

    def step(S, inp):
        qc, kc, lfc, vc = inp
        b = jnp.cumsum(lfc, axis=2)
        o_inter = jnp.einsum('bhtk,bhkv->bhtv', qc * jnp.exp(b), S)
        diff = jnp.where(causal[:, :, None], b[:, :, :, None, :] - b[:, :, None, :, :], -jnp.inf)
        a = jnp.einsum('bhtk,bhtsk,bhsk->bhts', qc, jnp.exp(diff), kc)
        o = o_inter + jnp.einsum('bhts,bhsv->bhtv', a, vc)
        b_last = b[:, :, -1:, :]
        S_new = jnp.exp(b_last[:, :, 0, :])[..., None] * S + jnp.einsum(
            'bhsk,bhsv->bhkv', kc * jnp.exp(b_last - b), vc)
        return S_new, o

    S_fin, o = lax.scan(step, S0.astype(F32),
                        (to_chunks(q), to_chunks(k), to_chunks(log_f), to_chunks(val)))
    o = o.transpose(1, 0, 3, 2, 4).reshape(B, T, H, DV)
    return o, S_fin

def even_mixer(h, w_in, w_out, sb_bias, lb, hg_g, S0, k_past, v_past, q_start):
    B, T, _ = h.shape
    proj = h @ w_in
    cuts = [HG_QK, 2 * HG_QK, 2 * HG_QK + HG_V, 2 * HG_QK + 2 * HG_V,
            2 * HG_QK + 2 * HG_V + SB_W, 2 * HG_QK + 2 * HG_V + 2 * SB_W]
    q_a, f_a, i_a, g_a, q_b, k_b, v_b = jnp.split(proj, cuts, axis=-1)
    o_a, S_new = hgrn2(q_a.reshape(B, T, HG_HEADS, HG_DK), f_a.reshape(B, T, HG_HEADS, HG_DK),
                       i_a.reshape(B, T, HG_HEADS, HG_DV), lb, S0)
    o_a = o_a * lax.rsqrt(jnp.mean(o_a * o_a, axis=-1, keepdims=True) + EPS) * hg_g.astype(F32)
    o_a = o_a.reshape(B, T, HG_V) * jax.nn.silu(g_a.astype(F32))
    q_b = q_b.reshape(B, T, SB_HEADS, SB_HD)
    k_b = k_b.reshape(B, T, SB_HEADS, SB_HD)
    v_b = v_b.reshape(B, T, SB_HEADS, SB_HD)
    if k_past is None:
        k_all, v_all = k_b, v_b
    else:
        k_all = jnp.concatenate([k_past.astype(k_b.dtype), k_b], axis=1)
        v_all = jnp.concatenate([v_past.astype(v_b.dtype), v_b], axis=1)
    o_b = stick_breaking(q_b, k_all, v_all, sb_bias, q_start).reshape(B, T, SB_W)
    out = jnp.concatenate([o_a.astype(h.dtype), o_b.astype(h.dtype)], axis=-1) @ w_out
    return out, S_new, k_b, v_b

def odd_mixer(h, w_in, w_out, pool_w, pool_scale, conv_w, conv_b, ln_g, ln_b,
              pool_hist, conv_hist, q_start):
    B, T, _ = h.shape
    proj = h @ w_in
    u, a, gt = jnp.split(proj, [MIX_HALF, MIX_HALF + CONV_CH], axis=-1)
    u_ext = jnp.concatenate([pool_hist.astype(u.dtype), u], axis=1)
    cs = jnp.concatenate([jnp.zeros((B, 1, MIX_HALF), F32),
                          jnp.cumsum(u_ext.astype(F32), axis=1)], axis=1)
    pos = q_start + jnp.arange(T)
    end = cs[:, POOL_HIST + 1:POOL_HIST + 1 + T]
    pooled = []
    for gi, w in enumerate(POOL_WINDOWS):
        sl = slice(gi * POOL_GC, (gi + 1) * POOL_GC)
        wsum = end[..., sl] - cs[:, POOL_HIST + 1 - w:POOL_HIST + 1 - w + T, sl]
        cnt = jnp.minimum(w, pos + 1).astype(F32)[None, :, None]
        pooled.append(wsum / cnt)
    pooled = (jnp.concatenate(pooled, axis=-1) - u.astype(F32)).reshape(B, T, POOL_GROUPS, POOL_GC)
    pool_out = jnp.einsum('btgc,gcd->btgd', pooled, pool_w.astype(F32)).reshape(B, T, MIX_HALF)
    pool_out = pool_out * pool_scale.astype(F32)
    glu = a * jax.nn.sigmoid(gt)
    glu_ext = jnp.concatenate([conv_hist.astype(glu.dtype), glu], axis=1)
    cv = lax.conv_general_dilated(glu_ext.astype(F32), conv_w.astype(F32)[:, None, :],
                                  window_strides=(1,), padding='VALID',
                                  dimension_numbers=('NWC', 'WIO', 'NWC'),
                                  feature_group_count=CONV_CH) + conv_b.astype(F32)
    mu = jnp.mean(cv, axis=-1, keepdims=True)
    var = jnp.mean(jnp.square(cv - mu), axis=-1, keepdims=True)
    cv = (cv - mu) * lax.rsqrt(var + EPS) * ln_g.astype(F32) + ln_b.astype(F32)
    conv_out = jax.nn.silu(cv)
    out = jnp.concatenate([pool_out.astype(h.dtype), conv_out.astype(h.dtype)], axis=-1) @ w_out
    return out, u_ext[:, -POOL_HIST:], glu_ext[:, -CONV_HIST:]

def setup_inputs(seed: int = 0) -> dict:
    key = jax.random.key(seed)
    ks = jax.random.split(key, 32)
    n_pages = PAST_LEN // PAGE_SIZE
    n_pool = (DEC_BATCH * n_pages * 5) // 4

    def nrm(k, shape, s):
        return jax.random.normal(k, shape, F32) * s

    page_table = jax.random.permutation(ks[9], n_pool)[:DEC_BATCH * n_pages]
    page_table = page_table.reshape(DEC_BATCH, n_pages).astype(jnp.int32)
    return {
        'x_prompt': nrm(ks[0], (BATCH, SEQ, D_MODEL), 1.0),
        'x_sample': nrm(ks[1], (DEC_BATCH, DEC_SEQ, D_MODEL), 1.0),
        'c_prompt': nrm(ks[2], (BATCH, D_MODEL), 1.0),
        'c_sample': nrm(ks[3], (DEC_BATCH, D_MODEL), 1.0),
        'cache_sb_k': nrm(ks[4], (N_EVEN, n_pool, PAGE_SIZE, SB_HEADS, SB_HD), 1.0),
        'cache_sb_v': nrm(ks[5], (N_EVEN, n_pool, PAGE_SIZE, SB_HEADS, SB_HD), 1.0),
        'state_hgrn': nrm(ks[6], (N_EVEN, DEC_BATCH, HG_HEADS, HG_DK, HG_DV), 0.5),
        'state_pool': nrm(ks[7], (N_ODD, DEC_BATCH, POOL_HIST, MIX_HALF), 1.0),
        'state_conv': nrm(ks[8], (N_ODD, DEC_BATCH, CONV_HIST, CONV_CH), 0.5),
        'page_table': page_table,
        'norm_g': 1.0 + nrm(ks[10], (DEPTH, 4, D_MODEL), 0.05),
        'ada_w': nrm(ks[11], (DEPTH, D_MODEL, 6 * D_MODEL), D_MODEL ** -0.5),
        'ada_b': nrm(ks[12], (DEPTH, 6 * D_MODEL), 0.02),
        'even_w_in': nrm(ks[13], (N_EVEN, D_MODEL, EVEN_IN), D_MODEL ** -0.5),
        'even_w_out': nrm(ks[14], (N_EVEN, HG_V + SB_W, D_MODEL), (HG_V + SB_W) ** -0.5),
        'sb_bias': SB_BIAS_INIT + nrm(ks[27], (N_EVEN, SB_HEADS), 0.1),
        'hgrn_lb_logits': nrm(ks[15], (N_EVEN, HG_QK), 0.5),
        'hgrn_norm_g': 1.0 + nrm(ks[16], (N_EVEN, HG_HEADS, HG_DV), 0.05),
        'odd_w_in': nrm(ks[17], (N_ODD, D_MODEL, ODD_IN), D_MODEL ** -0.5),
        'odd_w_out': nrm(ks[18], (N_ODD, MIX_HALF + CONV_CH, D_MODEL), (MIX_HALF + CONV_CH) ** -0.5),
        'pool_w': nrm(ks[19], (N_ODD, POOL_GROUPS, POOL_GC, POOL_GC), POOL_GC ** -0.5),
        'pool_scale': 1.0 + nrm(ks[20], (N_ODD, MIX_HALF), 0.05),
        'conv_w': nrm(ks[21], (N_ODD, CONV_WIDTH, CONV_CH), CONV_WIDTH ** -0.5),
        'conv_b': nrm(ks[22], (N_ODD, CONV_CH), 0.02),
        'conv_ln_g': 1.0 + nrm(ks[23], (N_ODD, CONV_CH), 0.05),
        'conv_ln_b': nrm(ks[24], (N_ODD, CONV_CH), 0.02),
        'mlp_w1': nrm(ks[25], (DEPTH, D_MODEL, D_FF), D_MODEL ** -0.5),
        'mlp_w2': nrm(ks[26], (DEPTH, D_FF, D_MODEL), D_FF ** -0.5),
    }

def reference(x_prompt, x_sample, c_prompt, c_sample, cache_sb_k, cache_sb_v, state_hgrn,
              state_pool, state_conv, page_table, norm_g, ada_w, ada_b, even_w_in, even_w_out,
              sb_bias, hgrn_lb_logits, hgrn_norm_g, odd_w_in, odd_w_out, pool_w, pool_scale, conv_w,
              conv_b, conv_ln_g, conv_ln_b, mlp_w1, mlp_w2):
    lb_cum = jnp.cumsum(jax.nn.softmax(hgrn_lb_logits.astype(F32), axis=0), axis=0)
    lower_bounds = jnp.maximum(lb_cum - lb_cum[:1], 0.0).reshape(N_EVEN, HG_HEADS, HG_DK)
    n_pages = page_table.shape[1]
    past_len = n_pages * cache_sb_k.shape[2]

    def run(x, c, q_start, is_sample):
        B = x.shape[0]
        S_list, k_list, v_list, p_list, cv_list = [], [], [], [], []
        for l in range(DEPTH):
            mod = (jax.nn.silu(c) @ ada_w[l] + ada_b[l])[:, None, :]
            sh1, sc1, g1, sh2, sc2, g2 = jnp.split(mod, 6, axis=-1)
            h = rms_norm(x, norm_g[l, 0]) * (1 + sc1) + sh1
            if l % 2 == 0:
                ie = l // 2
                if is_sample:
                    S0 = state_hgrn[ie]
                    k_past = cache_sb_k[ie][page_table].reshape(B, past_len, SB_HEADS, SB_HD)
                    v_past = cache_sb_v[ie][page_table].reshape(B, past_len, SB_HEADS, SB_HD)
                else:
                    S0 = jnp.zeros((B, HG_HEADS, HG_DK, HG_DV), F32)
                    k_past = None
                    v_past = None
                m, S_new, k_new, v_new = even_mixer(h, even_w_in[ie], even_w_out[ie], sb_bias[ie],
                                                    lower_bounds[ie], hgrn_norm_g[ie], S0, k_past,
                                                    v_past, q_start)
                S_list.append(S_new)
                k_list.append(k_new)
                v_list.append(v_new)
            else:
                io = l // 2
                if is_sample:
                    ph = state_pool[io]
                    chh = state_conv[io]
                else:
                    ph = jnp.zeros((B, POOL_HIST, MIX_HALF), x.dtype)
                    chh = jnp.zeros((B, CONV_HIST, CONV_CH), x.dtype)
                m, p_new, c_new = odd_mixer(h, odd_w_in[io], odd_w_out[io], pool_w[io], pool_scale[io],
                                            conv_w[io], conv_b[io], conv_ln_g[io], conv_ln_b[io],
                                            ph, chh, q_start)
                p_list.append(p_new)
                cv_list.append(c_new)
            x = x + g1 * rms_norm(m, norm_g[l, 1])
            h = rms_norm(x, norm_g[l, 2]) * (1 + sc2) + sh2
            x = x + g2 * rms_norm(mlp(h, mlp_w1[l], mlp_w2[l]), norm_g[l, 3])
        return (x, jnp.stack(S_list), jnp.stack(k_list), jnp.stack(v_list),
                jnp.stack(p_list), jnp.stack(cv_list))

    y_p, S_p, k_p, v_p, pool_p, conv_p = run(x_prompt, c_prompt, 0, False)
    y_s, S_s, k_s, v_s, pool_s, conv_s = run(x_sample, c_sample, past_len, True)
    return (y_p, y_s, k_p, v_p, k_s, v_s, S_p, S_s, pool_p, pool_s, conv_p, conv_s)


_drawn_inputs = setup_inputs


def setup_inputs(seed=0):
    import zlib

    import numpy as np

    out = dict(_drawn_inputs(seed))
    spreads = {}
    factors = {'sb_bias': 5.423,
     'pool_scale': 3.159,
     'conv_b': 6.967,
     'conv_ln_g': 4.062,
     'conv_ln_b': 8.0}
    for name, (base, spread) in spreads.items():
        noise = np.random.default_rng([zlib.crc32(name.encode()), seed]).standard_normal(out[name].shape)
        drawn = base * np.exp(spread * noise) if base else spread * noise
        out[name] = jnp.asarray(drawn.astype(out[name].dtype))
    for name, factor in factors.items():
        out[name] = (out[name] * factor).astype(out[name].dtype)
    return out
```

```python
from contextlib import ExitStack

import numpy as np
import concourse.bass as bass
from concourse import mybir

F32 = mybir.dt.float32
F32R = mybir.dt.float32r
I32 = mybir.dt.int32
ALU = mybir.AluOpType
ACT = mybir.ActivationFunctionType

P = 128
D = 1024
SEQ = 1024
NSEQ = 8
TQ = 8
NS = NSEQ * TQ
T = SEQ + NS
CW = 364
NC3 = 3
TP = CW * NC3
PAD = TP - T
TB = 91
NBK = TP // TB
KT = D // P
HALF = D // 2
HT = HALF // P
FF = 4 * D
EPS = 1e-6
N_MOD = 6
SEG = 1 + NSEQ
SEGP = 10
PAGE = 128
NPG = 8
SBH = 8
SBD = 64
HGH = 4
CH = 128
LEVELS = 8
WINDOWS = (2, 4, 8, 16)
PH = 15
CWID = 31
CHI = 30
VP = 88
HG_G, POOL_S, CONV_B, LN_G, LN_B, LB = 64, 68, 72, 76, 80, 84

_layout = [("levels", LEVELS * P), ("ones", 1), ("neg_incl", P), ("neg_ones", 1), ("strict", P), ("reset", TP),
           ("blk", NSEQ), ("cnt", 4 * 16), ("eps", 1)]
COL = {}
_at = 0
for _n, _w in _layout:
    COL[_n] = (_at, _at + _w)
    _at += _w
NCONST = _at
COL["ident"] = (0, P)


def constants():
    c = np.zeros((P, NCONST), np.float32)
    r, q = np.arange(P)[:, None], np.arange(P)[None, :]

    def put(name, v):
        c[:, COL[name][0]:COL[name][1]] = v
    put("ones", 1.0)
    put("neg_incl", -8.0 * (r >= q))
    put("neg_ones", -8.0)
    put("strict", r < q)
    lv = [r == q]
    for n in range(1, LEVELS):
        h = 2 ** (n - 1)
        lv.append((r // (2 * h) == q // (2 * h)) & ((r & h) == 0) & ((q & h) != 0))
    put("levels", np.concatenate(lv, 1))
    reset = np.ones(TP, np.float32)
    reset[0:SEQ:CH] = 0
    reset[SEQ:T:TQ] = 0
    put("reset", reset[None])
    put("blk", (np.arange(P)[:, None] // TQ) == np.arange(NSEQ)[None, :])
    put("cnt", np.concatenate([w / np.minimum(w, np.arange(16) + 1.0) for w in WINDOWS])[None])
    put("eps", EPS)
    return c


def open_split(nc, es, core, tag):
    core.XH = es.enter_context(nc.sbuf_tensor(f"{tag}_x_hi", [P, KT, TP], F32R))
    core.XL = es.enter_context(nc.sbuf_tensor(f"{tag}_x_lo", [P, KT, TP], F32R))


class Core:
    pass


def cols(core, name, a=0, b=None):
    lo, hi = COL[name]
    return core.const[:, lo + a:hi if b is None else lo + b]


def scope(nc, es, tag):
    sems = []

    def close():
        nc.clear_and_free_semaphores(sems)
        nc.all_engine_barrier()
    es.callback(close)

    def sb(name, shape, dtype=F32):
        return es.enter_context(nc.sbuf_tensor(f"{tag}_{name}", shape, dtype))

    def sem(name):
        sems.append(nc.alloc_semaphore(name=f"{tag}_{name}"))
        return sems[-1]
    return sb, sem


def chunked(ap):
    return ap.rearrange("p (c n) -> p c n", c=NC3)


def seg_bcast(ap):
    return ap.unsqueeze(2).to_broadcast([P, NSEQ, TQ])


def column_sums(pe, core, bank, n, sq, first):
    for b in range(NBK):
        q = pe.matmul(core.PS[0:TB, bank, n * NBK + b:n * NBK + b + 1], sq[:, b * TB:(b + 1) * TB], cols(core, "ones"),
                      start=(first and b == 0), stop=True, skip_group_check=True)
    return q


def spread(pe, core, bank, r):
    for b in range(NBK):
        q = pe.matmul(core.PS[:, bank + b // 4, (b % 4) * TB:(b % 4 + 1) * TB], r[:, b:b + 1].to_broadcast([TB, P]),
                      cols(core, "ident")[0:TB, 0:TB], start=True, stop=True)
    return q


def samples(ap):
    return ap[:, SEQ:T].rearrange("p (s t) -> p s t", s=NSEQ)


class AdaPart:
    UNITS = 4

    def __init__(self, core, sb, sem, chunks, rows_bank, turned_bank, ring=2):
        self.core, self.chunks, self.ring = core, chunks, ring
        self.bank, self.turned = rows_bank, turned_bank
        self.wa = sb("ada_w", [P, ring, 2, 4 * P])
        self.rows = sb("mod_rows", [SEG, 4 * P])
        self.w_in = [sem(f"ada_w_in{i}") for i in range(ring)]
        self.mm, self.rows_out, self.rows_T, self.step = sem("mod_mm"), sem("mod_rows_out"), sem("mod_turned"), sem("mod_step")
        self.units = self.UNITS * len(chunks)

    def load(self, eng):
        for n in range(self.units):
            l, c = self.chunks[n // 4]
            q = n % 4
            if n >= self.ring:
                eng.wait_ge(self.mm, n - self.ring + 1)
            eng.dma_start(self.wa[:, n % self.ring], self.core.ada_w[l].rearrange("(k p) f -> p k f", p=P)
                          [:, 2 * q:2 * q + 2, c * 4 * P:(c + 1) * 4 * P]).then_inc(self.w_in[n % self.ring], 16)

    def product(self, pe, n):
        c, q = divmod(n, 4)
        if q == 0 and c > 0:
            self.turn(pe, c - 1)
        pe.wait_ge(self.w_in[n % self.ring], 16 * (n // self.ring + 1))
        for i in range(2):
            m = pe.matmul(self.core.PS[0:SEG, self.bank, :], self.core.cT[:, 2 * q + i, 0:SEG], self.wa[:, n % self.ring, i],
                          start=(q == 0 and i == 0), stop=(q == 3 and i == 1))
        m.then_inc(self.mm, 1)

    def turn(self, pe, c):
        pe.wait_ge(self.rows_out, c + 1)
        for f in range(4):
            at = (4 * c + f) * SEGP
            m = pe.transpose(self.core.PS[:, self.turned, at:at + SEG], self.rows[:, f * P:(f + 1) * P],
                             cols(self.core, "ident")[0:SEG, 0:SEG])
        m.then_inc(self.rows_T, 1)

    def copy(self, act, c):
        act.wait_ge(self.mm, 4 * (c + 1))
        if c > 0:
            act.wait_ge(self.rows_T, c)
        act.activation(self.rows[:, :], self.core.PS[0:SEG, self.bank, :], ACT.Copy).then_inc(self.rows_out, 1)

    def products(self, pe):
        for n in range(self.units):
            self.product(pe, n)
        self.turn(pe, len(self.chunks) - 1)

    def copies(self, act):
        for c in range(len(self.chunks)):
            self.copy(act, c)

    def finish(self, dve):
        core = self.core
        dve.wait_ge(self.rows_T, len(self.chunks))
        n = 0
        for i, (l, c) in enumerate(self.chunks):
            mod = core.mod[:, l, c * 4 * SEGP:(c + 1) * 4 * SEGP].rearrange("p (f c) -> p f c", c=SEGP)[:, :, 0:SEG]
            bias = core.ada_bT[:, 48 * l + 4 * c:48 * l + 4 * c + 4].unsqueeze(2).to_broadcast([P, 4, SEG])
            sums = core.PS[:, self.turned, 4 * i * SEGP:4 * (i + 1) * SEGP].rearrange("p (f c) -> p f c", c=SEGP)[:, :, 0:SEG]
            dve.tensor_tensor(mod, sums, bias, ALU.add).then_inc(self.step, 1)
            n += 1
        for l, c in self.chunks:
            for g, (m_at, plus) in enumerate(((1, 1.0), (2, 0.0), (4, 1.0), (5, 0.0))):
                if c != 2 * m_at:
                    continue
                ng = core.vec[:, (l * 4 + g) * KT:(l * 4 + g + 1) * KT].unsqueeze(2).to_broadcast([P, KT, SEG])
                dst = core.coef[:, l, g].rearrange("p (k c) -> p k c", c=SEGP)[:, :, 0:SEG]
                mod = core.mod[:, l, :].rearrange("p (f c) -> p f c", c=SEGP)[:, m_at * KT:(m_at + 1) * KT, 0:SEG]
                dve.wait_ge(self.step, n)
                dve.tensor_scalar(dst, mod, plus, None, ALU.add).then_inc(self.step, 1)
                dve.wait_ge(self.step, n + 1)
                dve.tensor_tensor(dst, dst, ng, ALU.mult).then_inc(self.step, 1)
                n += 2


def setup(nc, core, tag, X):
    with ExitStack() as es:
        sb, sem = scope(nc, es, tag)
        rows_ada = sb("rows_ada", [96, P])
        rows_vec = sb("rows_vec", [VP, P])
        rows_conv = sb("rows_conv", [CWID * HT, P])
        rows_c = sb("rows_c", [SEG, D])
        xt = sb("xt", [P, 4, D])
        ada = AdaPart(core, sb, sem, [(0, c) for c in range(4)], 6, 7, ring=6)
        s_const, s_rows, s_crow, s_c, s_par, s_silu, s_xT, s_xev = (sem(n) for n in (
            "const_in", "rows_in", "c_in", "c_T", "params_T", "silu_out", "x_T", "x_out"))
        s_copy = sem("params_out")
        s_xt = [sem(f"xt_in{i}") for i in range(4)]
        PS = core.PS
        block = es.enter_context(nc.Block())

        @block.sync
        def _(sp):
            sp.dma_start(core.const[:, 0:P], core.const_in[:, 0:P]).then_inc(s_const, 16)
            sp.dma_start(rows_c[0:1, :], core.c_prompt).then_inc(s_crow, 16)
            sp.dma_start(rows_c[1:SEG, :], core.c_sample).then_inc(s_crow, 16)
            for i in range(9):
                if i >= 4:
                    sp.wait_ge(s_xT, i - 3)
                if i < 8:
                    sp.dma_start(xt[:, i % 4, :], core.x_prompt[0, i * P:(i + 1) * P, :]).then_inc(s_xt[i % 4], 16)
                else:
                    sp.dma_start(xt[0:NS, 0, :], core.x_sample.rearrange("b t d -> (b t) d")).then_inc(s_xt[0], 16)
            ada.load(sp)

        @block.scalar
        def _(act):
            act.dma_start(rows_ada[:, :], core.ada_b.rearrange("l (f p) -> (l f) p", p=P)).then_inc(s_rows, 16)
            act.dma_start(rows_vec[0:64, :], core.norm_g.rearrange("l n (f p) -> (l n f) p", p=P)).then_inc(s_rows, 16)
            for at, src in ((HG_G, core.hgrn_norm_g.rearrange("e h p -> (e h) p")),
                            (POOL_S, core.pool_scale.rearrange("o (f p) -> (o f) p", p=P)),
                            (CONV_B, core.conv_b.rearrange("o (f p) -> (o f) p", p=P)),
                            (LN_G, core.conv_ln_g.rearrange("o (f p) -> (o f) p", p=P)),
                            (LN_B, core.conv_ln_b.rearrange("o (f p) -> (o f) p", p=P)),
                            (LB, core.hgrn_lb_logits.rearrange("e (f p) -> (e f) p", p=P))):
                act.dma_start(rows_vec[at:at + 4, :], src).then_inc(s_rows, 16)
            act.dma_start(rows_conv[:, :], core.conv_w.rearrange("o w (f p) -> (o w f) p", p=P)).then_inc(s_rows, 16)
            act.dma_start(core.sb_bias_bc[:, :], core.sb_bias[0:1, :].to_broadcast([P, SBH])).then_inc(s_rows, 16)
            act.dma_start(core.const[:, P:], core.const_in[:, P:]).then_inc(s_rows, 16)
            act.wait_ge(s_c, 1)
            act.activation(core.cT[:, :, 0:SEG], PS[:, 0, 0:KT * 16].rearrange("p (k c) -> p k c", k=KT)[:, :, 0:SEG],
                           ACT.Silu).then_inc(s_silu, 1)
            ada.copies(act)

        @block.tensor
        def _(pe):
            pe.wait_ge(s_const, 16)
            pe.wait_ge(s_crow, 32)
            ident = cols(core, "ident")
            for k in range(KT):
                m = pe.transpose(PS[:, 0, 16 * k:16 * k + SEG], rows_c[:, k * P:(k + 1) * P], ident[0:SEG, 0:SEG])
            m.then_inc(s_c, 1)
            for i in range(9):
                pe.wait_ge(s_xt[i % 4], 16 * (i // 4 + 1))
                if i >= 2:
                    pe.wait_ge(s_xev, i - 1)
                n = P if i < 8 else NS
                for k in range(KT):
                    m = pe.transpose(PS[:, 2 + 2 * (i % 2) + k // 4, (k % 4) * P:(k % 4) * P + n],
                                     xt[0:n, i % 4, k * P:(k + 1) * P], ident[0:n, 0:n])
                m.then_inc(s_xT, 1)
            pe.wait_ge(s_rows, 16 * 11)
            pe.transpose(PS[:, 1, 0:96], rows_ada[:, :], ident[0:96, 0:96])
            pe.transpose(PS[:, 1, 96:96 + VP], rows_vec[:, :], ident[0:VP, 0:VP])
            pe.transpose(PS[:, 1, 256:256 + CWID * HT], rows_conv[:, :], ident[0:CWID * HT, 0:CWID * HT]).then_inc(s_par, 1)
            pe.wait_ge(s_silu, 1)
            ada.products(pe)

        @block.vector
        def _(dve):
            for k in range(KT):
                dve.memset(X[:, k, T:TP], 0.0)
            for i in range(9):
                dve.wait_ge(s_xT, i + 1)
                n = P if i < 8 else NS
                b = 2 + 2 * (i % 2)
                for h in range(2):
                    m = dve.tensor_copy(X[:, 4 * h:4 * h + 4, i * P:i * P + n],
                                        PS[:, b + h, :].rearrange("p (k t) -> p k t", k=4)[:, :, 0:n])
                m.then_inc(s_xev, 1)
            dve.wait_ge(s_par, 1)
            dve.tensor_copy(core.ada_bT[:, :], PS[:, 1, 0:96])
            dve.tensor_copy(core.vec[:, :], PS[:, 1, 96:96 + VP])
            dve.tensor_copy(core.convw[:, :], PS[:, 1, 256:256 + CWID * HT]).then_inc(s_copy, 1)
            dve.wait_ge(s_copy, 1)
            ada.finish(dve)


def residual_norm(nc, core, tag, X, load, m, gate, scale, shift, store, final=False,
                  chunks=()):
    with ExitStack() as es:
        sb, sem = scope(nc, es, tag)
        sq = sb("sq", [P, 2, TP])
        total = sb("total", [P, TP])
        rt = sb("rt", [TB, 2, NBK])
        rstd = sb("rstd", [TB, 2, NBK])
        y = sb("y", [P, 2, TP])
        y2 = sb("y2", [P, 2, TP])
        PS = core.PS
        s_x, s_store, s_sq, s_ss, s_rt, s_rs = (sem(n) for n in ("x_in", "x_stored", "sq_out", "sumsq", "root", "rstd"))
        s_bc, s_sum = sem("rstd_spread"), [sem(f"squares{n}_added") for n in range(2)]
        ada = AdaPart(core, sb, sem, chunks, 7, 6) if chunks else None
        s_y, s_res, s_y2p, s_y2s, s_hi, s_lo, s_pad, s_ys = (sem(n) for n in ("y_out", "x_new", "y2_prompt", "y2_samples", "hi_out", "lo_out", "pads", "y_small"))
        norms = ([m] if m is not None else []) + ([] if final else [X])
        two = m is not None
        coef = lambda i: core.coef[:, i[0], i[1]].rearrange("p (k c) -> p k c", c=SEGP)
        block = es.enter_context(nc.Block())

        @block.sync
        def _(sp):
            if load:
                sp.dma_start(X[:, :, :], core.x_dram.rearrange("p (k t) -> p k t", k=KT)).then_inc(s_x, 16)
            if store:
                if two:
                    sp.wait_ge(s_res, KT)
                sp.dma_start(core.x_dram.rearrange("p (k t) -> p k t", k=KT), X[:, :, :]).then_inc(s_store, 16)
                if ada:
                    ada.load(sp)
                sp.wait_ge(s_store, 16)

        @block.scalar
        def _(act):
            for n, src in enumerate(norms):
                for k in range(KT):
                    i = n * KT + k
                    if src is X and two:
                        act.wait_ge(s_res, k + 1)
                    if k >= 3:
                        act.wait_ge(s_sum[n], k - 2)
                    if k == 0 and n:
                        act.wait_ge(s_ss, n)
                    act.activation(sq[:, i % 2, :] if k else total[:, :], src[:, k, :], ACT.Square).then_inc(s_sq, 1)
                act.wait_ge(s_ss, n + 1)
                act.activation(rt[:, n, :], PS[0:TB, 6 + n, 0:NBK], ACT.Sqrt, scale=1.0 / D,
                               bias=cols(core, "eps")[0:TB, :]).then_inc(s_rt, 1)
            if final:
                return
            for k in range(KT):
                i = (KT if two else 0) + k
                act.wait_ge(s_y, i + 1)
                if k >= 2:
                    act.wait_ge(s_lo, k - 1)
                act.activation(y2[:, k % 2, 0:SEQ], y[:, i % 2, 0:SEQ], ACT.Identity,
                               scale=coef(scale)[:, k, 0:1],
                               bias=core.mod[:, shift[0], (shift[1] + k) * SEGP:(shift[1] + k) * SEGP + 1]).then_inc(s_y2p, 1)
                act.wait_ge(s_y2p, k + 1)
                act.wait_ge(s_y2s, k + 1)
                act.activation(core.XH[:, k, :], y2[:, k % 2, :], ACT.Copy).then_inc(s_hi, 1)
                if k % 2 == 1 and k // 2 < len(chunks):
                    ada.copy(act, k // 2)

        @block.tensor
        def _(pe):
            for n in range(len(norms)):
                pe.wait_ge(s_sum[n], KT - 1)
                column_sums(pe, core, 6 + n, 0, total, True).then_inc(s_ss, 1)
                pe.wait_ge(s_rs, n + 1)
                spread(pe, core, 3 * n, rstd[:, n, :]).then_inc(s_bc, 1)
            if ada:
                ada.products(pe)

        def add_squares(eng, n):
            for k in range(1, KT):
                i = n * KT + k
                eng.wait_ge(s_sq, i + 1)
                if k >= 2:
                    eng.wait_ge(s_sum[n], k - 1)
                eng.tensor_tensor(total[:, :], total[:, :], sq[:, i % 2, :], ALU.add).then_inc(s_sum[n], 1)

        @block.vector
        def _(dve):
            if not final:
                dve.memset(y2[:, 0, T:TP], 0.0)
                dve.memset(y2[:, 1, T:TP], 0.0).then_inc(s_pad, 1)
            small = 0
            add_squares(dve, 0)
            if two:
                if load:
                    dve.wait_ge(s_x, 16)
                dve.wait_ge(s_rt, 1)
                dve.reciprocal(rstd[:, 0, :], rt[:, 0, :]).then_inc(s_rs, 1)
                dve.wait_ge(s_bc, 1)
                for k in range(KT):
                    dve.tensor_tensor(chunked(y[:, k % 2, :]), chunked(m[:, k, :]), PS[:, 0:NC3, 0:CW],
                                      ALU.mult).then_inc(s_y, 1)
                    dve.wait_ge(s_y, k + 1)
                    dve.scalar_tensor_tensor(out=X[:, k, 0:SEQ], in0=y[:, k % 2, 0:SEQ], scalar=coef(gate)[:, k, 0:1],
                                             in1=X[:, k, 0:SEQ], op0=ALU.mult, op1=ALU.add)
                    dve.tensor_tensor(samples(y[:, k % 2, :]), samples(y[:, k % 2, :]),
                                      seg_bcast(coef(gate)[:, k, 1:SEG]), ALU.mult).then_inc(s_ys, 1)
                    small += 1
                    dve.wait_ge(s_ys, small)
                    dve.tensor_tensor(X[:, k, SEQ:T], X[:, k, SEQ:T], y[:, k % 2, SEQ:T], ALU.add).then_inc(s_res, 1)
            if final:
                return
            n = len(norms) - 1
            dve.wait_ge(s_rt, n + 1)
            dve.reciprocal(rstd[:, n, :], rt[:, n, :]).then_inc(s_rs, 1)
            dve.wait_ge(s_bc, n + 1)
            for k in range(KT):
                i = (KT if two else 0) + k
                if k >= 2:
                    dve.wait_ge(s_y2p, k - 1)
                dve.tensor_tensor(chunked(y[:, i % 2, :]), chunked(X[:, k, :]), PS[:, 3 * n:3 * n + NC3, 0:CW],
                                  ALU.mult).then_inc(s_y, 1)
                dve.wait_ge(s_y, i + 1)
                dve.tensor_tensor(samples(y[:, i % 2, :]), samples(y[:, i % 2, :]),
                                  seg_bcast(coef(scale)[:, k, 1:SEG]), ALU.mult).then_inc(s_ys, 1)
                small += 1
                dve.wait_ge(s_ys, small)
                if k >= 2:
                    dve.wait_ge(s_lo, k - 1)
                sh = core.mod[:, shift[0], :].rearrange("p (f c) -> p f c", c=SEGP)[:, shift[1] + k, 1:SEG]
                dve.tensor_tensor(samples(y2[:, k % 2, :]), samples(y[:, i % 2, :]), seg_bcast(sh),
                                  ALU.add).then_inc(s_y2s, 1)
            if ada:
                ada.finish(dve)

        @block.gpsimd
        def _(pool):
            if final:
                return
            if two:
                add_squares(pool, 1)
            pool.wait_ge(s_pad, 1)
            for k in range(KT):
                pool.wait_ge(s_hi, k + 1)
                pool.tensor_tensor(core.XL[:, k, :], y2[:, k % 2, :], core.XH[:, k, :].bitcast(F32),
                                   ALU.subtract).then_inc(s_lo, 1)


def split(nc, core, tag, src):
    with ExitStack() as es:
        _, sem = scope(nc, es, tag)
        s_hi = sem("hi_out")
        block = es.enter_context(nc.Block())

        @block.scalar
        def _(act):
            for k in range(KT):
                act.activation(core.XH[:, k, :], src[:, k, :], ACT.Copy).then_inc(s_hi, 1)

        @block.vector
        def _(dve):
            for k in range(KT):
                dve.wait_ge(s_hi, k + 1)
                dve.tensor_tensor(core.XL[:, k, :], src[:, k, :], core.XH[:, k, :].bitcast(F32), ALU.subtract)


def product(pe, out, hi, lo, xh, xl, first, last):
    pe.matmul(out, hi, xh, start=first, stop=False)
    pe.matmul(out, hi, xl, start=False, stop=False)
    return pe.matmul(out, lo, xh, start=False, stop=last)


def dense(nc, core, tag, w, jobs):
    with ExitStack() as es:
        sb, sem = scope(nc, es, tag)
        raw = sb("w_raw", [P, 2, KT, P])
        wh = sb("w_hi", [P, 2, KT, P], F32R)
        wl = sb("w_lo", [P, 2, KT, P], F32R)
        s_raw = [sem(f"w_in{i}") for i in range(2)]
        s_hi, s_lo, s_mm, s_ev = (sem(n) for n in ("w_hi_out", "w_lo_out", "mm_done", "out_copied"))
        w_v = w.rearrange("(k p) f -> p k f", p=P)
        PS = core.PS
        base = []
        n = 0
        for _, tiles, _ in jobs:
            base.append(n)
            n += tiles
        block = es.enter_context(nc.Block())

        @block.sync
        def _(sp):
            for (c0, tiles, _), b in zip(jobs, base):
                with sp.Fori(0, tiles // 2) as j:
                    for s in range(2):
                        sp.wait_ge(s_lo, j * 2 + (b + s + 1))
                        sp.dma_start(raw[:, s, :, :], w_v[:, :, bass.ds(j * (2 * P) + (s * P + c0), P)]).then_inc(s_raw[s], 16)

        @block.scalar
        def _(act):
            for (_, tiles, _), b in zip(jobs, base):
                with act.Fori(0, tiles // 2) as j:
                    for s in range(2):
                        act.wait_ge(s_raw[s], j * 16 + 16 * (b // 2 + 1))
                        act.wait_ge(s_mm, j * 2 + (b + s + 1))
                        act.activation(wh[:, s, :, :], raw[:, s, :, :], ACT.Copy).then_inc(s_hi, 1)

        @block.gpsimd
        def _(pool):
            pool.sem_inc(s_lo, 2)
            for (_, tiles, _), b in zip(jobs, base):
                with pool.Fori(0, tiles // 2) as j:
                    for s in range(2):
                        pool.wait_ge(s_hi, j * 2 + (b + s + 1))
                        pool.tensor_tensor(wl[:, s, :, :], raw[:, s, :, :], wh[:, s, :, :].bitcast(F32),
                                           ALU.subtract).then_inc(s_lo, 1)

        @block.tensor
        def _(pe):
            pe.sem_inc(s_mm, 2)
            for (_, tiles, _), b in zip(jobs, base):
                with pe.Fori(0, tiles // 2) as j:
                    for s in range(2):
                        pe.wait_ge(s_lo, j * 2 + (b + s + 3))
                        pe.wait_ge(s_ev, j * 2 + (b + s + 1))
                        for k in range(KT):
                            for c in range(NC3):
                                q = product(pe, PS[:, 3 * s + c, 0:CW], wh[:, s, k, :], wl[:, s, k, :],
                                            core.XH[:, k, c * CW:(c + 1) * CW], core.XL[:, k, c * CW:(c + 1) * CW],
                                            k == 0, k == KT - 1)
                        q.then_inc(s_mm, 1)

        @block.vector
        def _(dve):
            dve.sem_inc(s_ev, 2)
            for (_, tiles, dst), b in zip(jobs, base):
                with dve.Fori(0, tiles // 2) as j:
                    for s in range(2):
                        dve.wait_ge(s_mm, j * 2 + (b + s + 3))
                        o = dst[:, bass.ds(j * 2 + s, 1), :].rearrange("p a (c n) -> p (a c) n", c=NC3)
                        dve.tensor_copy(o, PS[:, 3 * s:3 * s + 3, 0:CW]).then_inc(s_ev, 1)


def mlp(nc, core, tag, w1, w2, M):
    G = FF // (4 * P)
    SETS = 12
    with ExitStack() as es:
        sb, sem = scope(nc, es, tag)
        raw = sb("w_raw", [P, 2, 8 * P])
        wh = sb("w_hi", [P, 2, 8 * P], F32R)
        wl = sb("w_lo", [P, 2, 8 * P], F32R)
        HH = sb("h_hi", [P, 4, TP], F32R)
        HL = sb("h_lo", [P, 4, TP], F32R)
        r = sb("relu", [P, 2, TP])
        s_raw = [sem(f"w_in{i}") for i in range(2)]
        s_hi, s_lo, s_mm, s_ev = (sem(n) for n in ("w_hi_out", "w_lo_out", "mm_done", "out_copied"))
        s_r, s_hh, s_sq, s_h, s_m0 = (sem(n) for n in ("relu_out", "h_hi_out", "sq_out", "h_lo_out", "m_zero"))
        w1_v = w1.rearrange("(k p) f -> p k f", p=P)
        w2_v = w2.rearrange("(g k p) f -> p g k f", p=P, k=4)
        PS = core.PS
        block = es.enter_context(nc.Block())
        released = [1, 2, 3, 4, 6, 8, 10, 12]

        @block.sync
        def _(sp):
            with sp.Fori(0, G) as g:
                for u in range(8):
                    sp.wait_ge(s_lo, g * 8 + (u + 1))
                    if u < 4:
                        sp.dma_start(raw[:, u % 2, :].rearrange("p (k f) -> p k f", k=8),
                                     w1_v[:, :, bass.ds(g * (4 * P) + u * P, P)]).then_inc(s_raw[u % 2], 16)
                    else:
                        sp.dma_start(raw[:, u % 2, :].rearrange("p (k f) -> p k f", k=4),
                                     w2_v[:, bass.ds(g, 1), :, (u - 4) * 2 * P:(u - 3) * 2 * P]
                                     .rearrange("p a k f -> p (a k) f")).then_inc(s_raw[u % 2], 16)

        @block.scalar
        def _(act):
            def weights(g, u):
                act.wait_ge(s_raw[u % 2], g * 64 + 16 * (u // 2 + 1))
                act.wait_ge(s_mm, g * SETS + (released[u - 2] + (SETS if u >= 2 else 0)))
                act.activation(wh[:, u % 2, :], raw[:, u % 2, :], ACT.Copy).then_inc(s_hi, 1)

            def hidden(g, i):
                act.wait_ge(s_mm, g * SETS + (SETS + i + 1))
                if i >= 2:
                    act.wait_ge(s_h, g * 4 + (i - 1))
                act.activation(chunked(r[:, i % 2, :]), PS[:, 3 * (i % 2):3 * (i % 2) + 3, 0:CW],
                               ACT.Relu).then_inc(s_r, 1)
                act.wait_ge(s_r, g * 4 + (i + 1))
                act.activation(HH[:, i, :], r[:, i % 2, :], ACT.Square).then_inc(s_hh, 1)

            with act.Fori(0, G) as g:
                for u in range(8):
                    weights(g, u)
                    if u in (1, 2, 3, 4):
                        hidden(g, u - 1)

        @block.gpsimd
        def _(pool):
            pool.sem_inc(s_lo, 2)
            with pool.Fori(0, G) as g:
                for u in range(8):
                    pool.wait_ge(s_hi, g * 8 + (u + 1))
                    pool.tensor_tensor(wl[:, u % 2, :], raw[:, u % 2, :], wh[:, u % 2, :].bitcast(F32),
                                       ALU.subtract).then_inc(s_lo, 1)

        @block.tensor
        def _(pe):
            pe.sem_inc(s_mm, SETS)
            with pe.Fori(0, G) as g:
                for i in range(4):
                    pe.wait_ge(s_lo, g * 8 + (i + 3))
                    if i < 2:
                        pe.wait_ge(s_ev, g * 8 + (i + 1))
                    else:
                        pe.wait_ge(s_r, g * 4 + (i - 1))
                    for k in range(KT):
                        for c in range(NC3):
                            q = product(pe, PS[:, 3 * (i % 2) + c, 0:CW], wh[:, i % 2, k * P:(k + 1) * P],
                                        wl[:, i % 2, k * P:(k + 1) * P],
                                        core.XH[:, k, c * CW:(c + 1) * CW], core.XL[:, k, c * CW:(c + 1) * CW],
                                        k == 0, k == KT - 1)
                    q.then_inc(s_mm, 1)
                for f in range(8):
                    u = 4 + f // 2
                    pe.wait_ge(s_lo, g * 8 + (u + 3))
                    if f < 2:
                        pe.wait_ge(s_r, g * 4 + (f + 3))
                    else:
                        pe.wait_ge(s_ev, g * 8 + (f + 1))
                    for k in range(4):
                        if f == 0:
                            pe.wait_ge(s_h, g * 4 + (k + 1))
                        at = k * 2 * P + (f % 2) * P
                        for c in range(NC3):
                            q = product(pe, PS[:, 3 * (f % 2) + c, 0:CW], wh[:, u % 2, at:at + P],
                                        wl[:, u % 2, at:at + P],
                                        HH[:, k, c * CW:(c + 1) * CW], HL[:, k, c * CW:(c + 1) * CW],
                                        k == 0, k == 3)
                    q.then_inc(s_mm, 1)

        @block.vector
        def _(dve):
            dve.sem_inc(s_ev, 2)
            dve.memset(M[:, :, :], 0.0).then_inc(s_m0, 1)
            dve.wait_ge(s_m0, 1)
            with dve.Fori(0, G) as g:
                for i in range(4):
                    dve.wait_ge(s_hh, g * 4 + (i + 1))
                    dve.tensor_tensor(r[:, i % 2, :], r[:, i % 2, :], r[:, i % 2, :], ALU.mult).then_inc(s_sq, 1)
                    dve.wait_ge(s_sq, g * 4 + (i + 1))
                    dve.tensor_tensor(HL[:, i, :], r[:, i % 2, :], HH[:, i, :].bitcast(F32), ALU.subtract).then_inc(s_h, 1)
                for f in range(8):
                    dve.wait_ge(s_mm, g * SETS + (SETS + 4 + f + 1))
                    dve.tensor_tensor(chunked(M[:, f, :]), chunked(M[:, f, :]),
                                      PS[:, 3 * (f % 2):3 * (f % 2) + 3, 0:CW], ALU.add).then_inc(s_ev, 1)


def kv_rows(nc, core, tag, KV, VT):
    with ExitStack() as es:
        sb, sem = scope(nc, es, tag)
        kt = sb("k_rows", [P, 2, HALF])
        vs = sb("v_rows", [NS, HALF])
        s_T, s_cp = sem("turned"), sem("copied")
        s_out = [sem(f"stored{i}") for i in range(3)]
        PS = core.PS
        rows = lambda i: P if i < 8 else NS
        block = es.enter_context(nc.Block())

        @block.tensor
        def _(pe):
            for u in range(18):
                i, n = u // 2, rows(u // 2)
                if u >= 4:
                    pe.wait_ge(s_cp, u - 3)
                for f in range(4):
                    q = pe.transpose(PS[0:n, u % 4, f * P:(f + 1) * P], KV[:, 4 * (u % 2) + f, i * P:i * P + n],
                                     cols(core, "ident"))
                q.then_inc(s_T, 1)

        @block.vector
        def _(dve):
            for u in range(18):
                i, n = u // 2, rows(u // 2)
                dve.wait_ge(s_T, u + 1)
                if u % 2 == 0 and i >= 2:
                    dve.wait_ge(s_out[i % 2], 16 * (i // 2))
                dst = kt[0:n, i % 2, :] if u % 2 == 0 else VT[:, i, :] if i < 8 else vs[:, :]
                dve.tensor_copy(dst, PS[0:n, u % 4, :]).then_inc(s_cp, 1)

        @block.sync
        def _(sp):
            kp = core.o_k_p.rearrange("e b (i p) h d -> (e b i) p (h d)", p=P)
            for i in range(9):
                sp.wait_ge(s_cp, 2 * i + 1)
                dst = kp[i] if i < 8 else core.o_k_s.rearrange("e b t h d -> (e b t) (h d)")
                sp.dma_start(dst, kt[0:rows(i), i % 2, :]).then_inc(s_out[i % 2], 16)
            sp.wait_ge(s_cp, 18)
            sp.dma_start(core.o_v_p.rearrange("e b (i p) h d -> p (e b i) (h d)", p=P), VT[:, 0:8, :]).then_inc(s_out[2], 16)
            sp.dma_start(core.o_v_s.rearrange("e b t h d -> (e b t) (h d)"), vs[:, :]).then_inc(s_out[2], 16)
            sp.wait_ge(s_out[0], 16 * 5)
            sp.wait_ge(s_out[1], 16 * 4)
            sp.wait_ge(s_out[2], 32)


def sb_prompt(nc, core, tag, KV, VT):
    tiles = []
    for h in range(SBH):
        for g in range(2):
            for kt in range(4 * g + 3, -1, -1):
                tiles.append((h, g, kt, max(0, kt - 4 * g) * P))
    NT = len(tiles)
    LACC, LOUT = 3, 5
    first = lambda n: tiles[n][2] == 4 * tiles[n][1] + 3
    diag = lambda n: tiles[n][2] >= 4 * tiles[n][1]
    run = lambda n: sum(first(i) for i in range(n + 1)) - 1
    last = lambda n: tiles[n][2] == 0
    with ExitStack() as es:
        sb, sem = scope(nc, es, tag)
        zb = sb("z", [P, 2, 512])
        a = sb("a", [P, 2, 512])
        e = sb("e", [P, 2, 512])
        sp_ = sb("softplus", [P, 4, 512])
        R = sb("later", [P, 4, 512])
        w = sb("w", [P, 3, 512])
        names = ("z_mm", "zb_out", "abs_out", "exp_out", "ln_out", "sp_out", "sp_masked", "later_out", "acc_mm",
                 "w_out", "w_masked", "o_mm", "o_out")
        s_z, s_zb, s_a, s_e, s_l, s_sp, s_spm, s_R, s_acc, s_w, s_wm, s_o, s_oc = (sem(n) for n in names)
        PS = core.PS
        NB = 6
        block = es.enter_context(nc.Block())
        n_diag = lambda n: sum(diag(i) for i in range(n + 1))

        @block.tensor
        def _(pe):
            for t in range(NT + LOUT):
                if t < NT:
                    h, g, kt, c = tiles[t]
                    r = 64 * (h % 2)
                    if t >= NB:
                        pe.wait_ge(s_w, t - NB + 1)
                    pe.matmul(PS[:, t % NB, c:512], KV[r:r + 64, h // 2, kt * P:(kt + 1) * P],
                              core.M[r:r + 64, 4 + h // 2, g * 512 + c:(g + 1) * 512], start=True, stop=True)\
                      .then_inc(s_z, 1)
                n = t - LACC
                if 0 <= n < NT:
                    h, g, kt, c = tiles[n]
                    pe.wait_ge(s_sp, n + 1)
                    if diag(n):
                        pe.wait_ge(s_spm, n_diag(n))
                    pe.wait_ge(s_zb, n + 1)
                    q = pe.matmul(PS[:, n % NB, c:512], cols(core, "neg_incl"), sp_[:, n % 4, c:512],
                                  start=False, stop=first(n), skip_group_check=True)
                    if not first(n):
                        pe.wait_ge(s_R, n)
                        q = pe.matmul(PS[:, n % NB, c:512], cols(core, "neg_ones").to_broadcast([P, P]), R[:, n % 4, c:512],
                                      start=False, stop=True, skip_group_check=True)
                    q.then_inc(s_acc, 1)
                n = t - LOUT
                if 0 <= n < NT:
                    h, g, kt, c = tiles[n]
                    r = 64 * (h % 2)
                    pe.wait_ge(s_w, n + 1)
                    if diag(n):
                        pe.wait_ge(s_wm, n_diag(n))
                    if first(n) and run(n) >= 2:
                        pe.wait_ge(s_oc, run(n) - 1)
                    q = pe.matmul(PS[r:r + 64, 6 + run(n) % 2, c:512], VT[:, kt, h * 64:(h + 1) * 64],
                                  w[:, n % 3, c:512], start=first(n), stop=last(n), skip_group_check=True)
                    q.then_inc(s_o, 1)

        @block.scalar
        def _(act):
            act.preload_act_table_set("natural_log_exp_and_others")
            for t in range(NT + LACC):
                if t < NT:
                    h, g, kt, c = tiles[t]
                    act.wait_ge(s_zb, t + 1)
                    if t >= 2:
                        act.wait_ge(s_l, t - 1)
                    act.activation(a[:, t % 2, c:512], zb[:, t % 2, c:512], ACT.Abs).then_inc(s_a, 1)
                    act.wait_ge(s_a, t + 1)
                    act.activation(a[:, t % 2, c:512], a[:, t % 2, c:512], ACT.Exp, scale=-1.0).then_inc(s_e, 1)
                    act.wait_ge(s_e, t + 1)
                    if t >= 2:
                        act.wait_ge(s_sp, t - 1)
                    act.activation(e[:, t % 2, c:512], a[:, t % 2, c:512], ACT.Ln, bias=1.0).then_inc(s_l, 1)
                n = t - LACC
                if 0 <= n < NT:
                    h, g, kt, c = tiles[n]
                    act.wait_ge(s_acc, n + 1)
                    if n >= 3:
                        act.wait_ge(s_o, n - 2)
                    act.activation(w[:, n % 3, c:512], PS[:, n % NB, c:512], ACT.Exp, scale=0.125,
                                   bias=core.sb_bias_bc[:, h:h + 1]).then_inc(s_w, 1)

        @block.vector
        def _(dve):
            def scores(t):
                h, g, kt, c = tiles[t]
                dve.wait_ge(s_z, t + 1)
                if t >= 2:
                    dve.wait_ge(s_sp, t - 1)
                    dve.wait_ge(s_a, t - 1)
                dve.tensor_scalar(zb[:, t % 2, c:512], PS[:, t % NB, c:512], 0.125, core.sb_bias_bc[:, h:h + 1],
                                  ALU.mult, ALU.add).then_inc(s_zb, 1)

            def sums(t):
                h, g, kt, c = tiles[t]
                dve.wait_ge(s_zb, t + 1)
                dve.wait_ge(s_l, t + 1)
                if t >= 4:
                    dve.wait_ge(s_acc, t - 3)
                    dve.wait_ge(s_R, t - 3)
                dve.scalar_tensor_tensor(out=sp_[:, t % 4, c:512], in0=zb[:, t % 2, c:512], scalar=0.0,
                                         in1=e[:, t % 2, c:512], op0=ALU.max, op1=ALU.add).then_inc(s_sp, 1)
                dve.wait_ge(s_sp, t + 1)
                if diag(t):
                    dve.wait_ge(s_spm, n_diag(t))
                if t >= 3:
                    dve.wait_ge(s_acc, t - 2)
                if t >= 1:
                    dve.wait_ge(s_R, t)
                nx = (t + 1) % 4
                if c:
                    dve.memset(R[:, nx, 0:c], 0.0)
                if first(t):
                    dve.tensor_copy(R[:, nx, c:512], sp_[:, t % 4, c:512]).then_inc(s_R, 1)
                else:
                    dve.tensor_tensor(R[:, nx, c:512], R[:, t % 4, c:512], sp_[:, t % 4, c:512], ALU.add).then_inc(s_R, 1)

            for t in range(NT + LOUT + 1):
                if t < NT:
                    scores(t)
                if 1 <= t <= NT:
                    sums(t - 1)
                n = t - LOUT - 1
                if n >= 0 and last(n):
                    h, g = tiles[n][:2]
                    r = 64 * (h % 2)
                    dve.wait_ge(s_o, n + 1)
                    dve.tensor_copy(core.M[r:r + 64, 4 + h // 2, g * 512:(g + 1) * 512],
                                    PS[r:r + 64, 6 + run(n) % 2, :]).then_inc(s_oc, 1)

        @block.gpsimd
        def _(pool):
            for t in range(NT + LACC):
                if t < NT and diag(t):
                    c = tiles[t][3]
                    pool.wait_ge(s_sp, t + 1)
                    pool.tensor_tensor(sp_[:, t % 4, c:c + P], sp_[:, t % 4, c:c + P], cols(core, "strict"),
                                       ALU.mult).then_inc(s_spm, 1)
                n = t - LACC
                if 0 <= n < NT and diag(n):
                    c = tiles[n][3]
                    pool.wait_ge(s_w, n + 1)
                    pool.tensor_tensor(w[:, n % 3, c:c + P], w[:, n % 3, c:c + P], cols(core, "strict"),
                                       ALU.mult).then_inc(s_wm, 1)


def sb_sample(nc, core, tag, KV, kp, vp):
    W64 = SBH * TQ
    KRING, VRING = kp.shape[1], vp.shape[1]
    NPAGES = NSEQ * NPG
    with ExitStack() as es:
        sb, sem = scope(nc, es, tag)
        pages = sb("pages", [1, NPAGES], I32)
        qb = sb("q_blocks", [P, 4, NSEQ, 2 * TQ])
        kT = sb("k_T", [P, 2, HALF])
        vn = sb("v_new", [TQ, 2, HALF])
        a = sb("a", [P, 512])
        l = sb("l", [P, 512])
        zb = sb("z", [P, 512])
        sp_ = sb("softplus", [P, 512])
        spn = sb("softplus_new", [TQ, 512])
        wn = sb("w_new", [TQ, 512])
        R = sb("later", [P, 512])
        w = sb("w", [P, 512])
        s_pt, s_qb, s_T, s_kT, s_z, s_vn, s_vnc = (sem(n) for n in ("pages_in", "q_ready", "k_turned", "kT_out", "z_mm", "v_new_T", "v_new_out"))
        s_k = [sem(f"k_in{i}") for i in range(KRING)]
        s_v = [sem(f"v_in{i}") for i in range(VRING)]
        t = sb("exponent", [P, 512])
        bt = sb("bias", [P, W64])
        s_q0, s_zn, s_t = sem("zeroed"), sem("z_new_mm"), sem("exponent_out")
        s_zb, s_a, s_e, s_l, s_sp, s_R, s_acc, s_w, s_o, s_oc, s_m, s_m2 = (sem(n) for n in (
            "zb_out", "abs_out", "exp_out", "ln_out", "sp_out", "later_out", "acc_mm", "w_out", "o_mm", "o_out", "masked", "w_masked"))
        PS = core.PS
        block = es.enter_context(nc.Block())

        @block.sync
        def _(sp):
            sp.dma_start(pages[:, :], core.page_table.rearrange("(a b) g -> a (b g)", a=1)).then_inc(s_pt, 16)
            sp.wait_ge(s_pt, 16)
            for i in range(NPAGES):
                page = sp.value_load(pages[0:1, i:i + 1], min_val=0, max_val=core.cache_k.shape[1] - 1)
                if i >= KRING:
                    sp.wait_ge(s_T, i - KRING + 1)
                sp.dma_start(kp[:, i % KRING, :], core.cache_k[0, bass.ds(page, 1)].rearrange("a p h d -> p (a h d)"))\
                  .then_inc(s_k[i % KRING], 16)

        @block.gpsimd
        def _(pool):
            pool.wait_ge(s_pt, 16)
            for i in range(NPAGES):
                page = pool.value_load(pages[0:1, i:i + 1], min_val=0, max_val=core.cache_k.shape[1] - 1)
                if i >= VRING:
                    pool.wait_ge(s_o, (i - VRING) // NPG + 1)
                pool.dma_start(vp[:, i % VRING, :], core.cache_v[0, bass.ds(page, 1)].rearrange("a p h d -> p (a h d)"))\
                    .then_inc(s_v[i % VRING], 16)

        @block.tensor
        def _(pe):
            pe.wait_ge(s_qb, 1)
            for j in range(NSEQ):
                for p in range(4):
                    q = pe.matmul(PS[0:TQ, 4, j * W64 + p * 16:j * W64 + p * 16 + 16],
                                  KV[:, p, SEQ + j * TQ:SEQ + (j + 1) * TQ], qb[:, p, j, :],
                                  start=(j == 0 and p == 0), stop=True, skip_group_check=True)
            q.then_inc(s_zn, 1)
            pe.wait_ge(s_zb, 1)
            pe.wait_ge(s_a, 1)
            pe.wait_ge(s_m, 1)
            pe.matmul(PS[0:TQ, 4, :], cols(core, "neg_incl")[0:TQ, 0:TQ], spn[:, :], start=False, stop=True,
                      skip_group_check=True).then_inc(s_acc, 1)

            def turn(i):
                pe.wait_ge(s_k[i % KRING], 16 * (i // KRING + 1))
                if i >= 2:
                    pe.wait_ge(s_kT, i - 1)
                for p in range(4):
                    q = pe.transpose(PS[:, i % 2, p * P:(p + 1) * P], kp[:, i % KRING, p * P:(p + 1) * P],
                                     cols(core, "ident"))
                q.then_inc(s_T, 1)

            def scores(j):
                for g in range(NPG):
                    i = j * NPG + g
                    if i + 1 < NPAGES:
                        turn(i + 1)
                    pe.wait_ge(s_kT, i + 1)
                    if g == 0 and j >= 2:
                        pe.wait_ge(s_w, j)
                    for p in range(4):
                        at = g * W64 + p * 16
                        q = pe.matmul(PS[:, 2 + j % 2, at:at + 16], kT[:, i % 2, p * P:(p + 1) * P], qb[:, p, j, :],
                                      start=(g == 0 and p == 0), stop=True, skip_group_check=True)
                    q.then_inc(s_z, 1)

            def values(j):
                pe.wait_ge(s_w, j + 2)
                for i in range(j * NPG, (j + 1) * NPG):
                    pe.wait_ge(s_v[i % VRING], 16 * (i // VRING + 1))
                if j >= 1:
                    pe.wait_ge(s_vnc, j)
                for p in range(4):
                    q = pe.transpose(PS[0:TQ, 5, p * P:(p + 1) * P], KV[:, 4 + p, SEQ + j * TQ:SEQ + (j + 1) * TQ],
                                     cols(core, "ident"))
                q.then_inc(s_vn, 1)
                pe.wait_ge(s_vnc, j + 1)
                pe.wait_ge(s_m2, 1)
                if j >= 2:
                    pe.wait_ge(s_oc, j - 1)
                for p in range(4):
                    o = PS[:, 6 + j % 2, p * 16:p * 16 + 16]
                    for g in range(NPG):
                        pe.matmul(o, vp[:, (j * NPG + g) % VRING, p * P:(p + 1) * P], w[:, g * W64 + p * 16:g * W64 + p * 16 + 16],
                                  start=(g == 0), stop=False)
                    q = pe.matmul(o, vn[:, j % 2, p * P:(p + 1) * P], wn[:, j * W64 + p * 16:j * W64 + p * 16 + 16],
                                  start=False, stop=True)
                q.then_inc(s_o, 1)

            turn(0)
            for j in range(NSEQ + 1):
                if j < NSEQ:
                    scores(j)
                if j >= 1:
                    n = j - 1
                    pe.wait_ge(s_sp, n + 2)
                    pe.wait_ge(s_R, (NPG + 1) * (n + 1))
                    pe.matmul(PS[:, 2 + n % 2, :], cols(core, "neg_incl"), sp_[:, :], start=False, stop=False,
                              skip_group_check=True)
                    pe.matmul(PS[:, 2 + n % 2, :], cols(core, "neg_ones").to_broadcast([P, P]), R[:, :], start=False, stop=True,
                              skip_group_check=True).then_inc(s_acc, 1)
                    values(n)

        @block.scalar
        def _(act):
            act.preload_act_table_set("natural_log_exp_and_others")
            def soft(n, rows):
                act.wait_ge(s_zb, n + 1)
                if n:
                    act.wait_ge(s_l, n)
                act.activation(a[0:rows, :], zb[0:rows, :], ACT.Abs).then_inc(s_a, 1)
                act.wait_ge(s_a, n + 1)
                act.activation(a[0:rows, :], a[0:rows, :], ACT.Exp, scale=-1.0).then_inc(s_e, 1)
                act.wait_ge(s_e, n + 1)
                if n:
                    act.wait_ge(s_sp, n)
                act.activation(l[0:rows, :], a[0:rows, :], ACT.Ln, bias=1.0).then_inc(s_l, 1)

            soft(0, TQ)
            act.wait_ge(s_t, 1)
            act.activation(wn[:, :], t[0:TQ, :], ACT.Exp).then_inc(s_w, 1)
            for j in range(NSEQ + 1):
                if j < NSEQ:
                    for g in range(NPG):
                        i = j * NPG + g
                        act.wait_ge(s_T, i + 1)
                        if i >= 2:
                            act.wait_ge(s_z, i)
                        act.activation(kT[:, i % 2, :], PS[:, i % 2, :], ACT.Copy).then_inc(s_kT, 1)
                if j >= 1:
                    act.wait_ge(s_t, j + 1)
                    if j >= 2:
                        act.wait_ge(s_o, j - 1)
                    act.activation(w[:, :], t[:, :], ACT.Exp).then_inc(s_w, 1)
                if j < NSEQ:
                    soft(j + 1, P)

        @block.vector
        def _(dve):
            dve.memset(qb[:, :, :, :], 0.0).then_inc(s_q0, 1)
            dve.wait_ge(s_q0, 1)
            for hh in range(2):
                r = 64 * hh
                q = dve.tensor_copy(qb[r:r + 64, :, :, hh * TQ:(hh + 1) * TQ],
                                    core.M[r:r + 64, 4:8, SEQ:T].rearrange("p k (s t) -> p k s t", s=NSEQ))
            q.then_inc(s_qb, 1)
            bias = core.sb_bias_bc[:, :].unsqueeze(2).to_broadcast([P, SBH, TQ])
            dve.tensor_copy(bt[:, :].rearrange("p (h q) -> p h q", h=SBH), bias).then_inc(s_q0, 1)
            dve.wait_ge(s_q0, 2)
            page_cols = lambda ap: ap.rearrange("p (g c) -> p g c", c=W64)
            bt_all = lambda rows: bt[0:rows, :].unsqueeze(1).to_broadcast([rows, NPG, W64])
            strict = cols(core, "strict")[0:TQ, 0:TQ].unsqueeze(1).to_broadcast([TQ, W64, TQ])
            by_query = lambda ap: ap.rearrange("p (c q) -> p c q", q=TQ)

            def scaled(dst, bank, rows):
                return dve.scalar_tensor_tensor(out=page_cols(dst[0:rows, :]), in0=page_cols(PS[0:rows, bank, :]),
                                                scalar=0.125, in1=bt_all(rows), op0=ALU.mult, op1=ALU.add)

            def softplus(n, dst, rows):
                dve.wait_ge(s_zb, n + 1)
                dve.wait_ge(s_l, n + 1)
                dve.scalar_tensor_tensor(out=dst, in0=zb[0:rows, :], scalar=0.0, in1=l[0:rows, :],
                                         op0=ALU.max, op1=ALU.add).then_inc(s_sp, 1)

            dve.wait_ge(s_zn, 1)
            scaled(zb, 4, TQ).then_inc(s_zb, 1)
            softplus(0, spn[:, :], TQ)
            dve.wait_ge(s_sp, 1)
            dve.tensor_tensor(by_query(spn[:, :]), by_query(spn[:, :]), strict, ALU.mult).then_inc(s_m, 1)
            dve.wait_ge(s_acc, 1)
            scaled(t, 4, TQ).then_inc(s_t, 1)
            dve.wait_ge(s_w, 1)
            dve.tensor_tensor(by_query(wn[:, :]), by_query(wn[:, :]), strict, ALU.mult).then_inc(s_m2, 1)
            for j in range(NSEQ + 1):
                if j >= 1:
                    dve.wait_ge(s_acc, j + 1)
                    dve.wait_ge(s_w, j)
                    scaled(t, 2 + (j - 1) % 2, P).then_inc(s_t, 1)
                    dve.wait_ge(s_vn, j)
                    if j >= 3:
                        dve.wait_ge(s_o, j - 2)
                    dve.tensor_copy(vn[:, (j - 1) % 2, :], PS[0:TQ, 5, :]).then_inc(s_vnc, 1)
                if j < NSEQ:
                    dve.wait_ge(s_z, NPG * (j + 1))
                    dve.wait_ge(s_sp, j + 1)
                    dve.wait_ge(s_a, j + 1)
                    scaled(zb, 2 + j % 2, P).then_inc(s_zb, 1)
                    if j >= 1:
                        dve.wait_ge(s_R, (NPG + 1) * j)
                    softplus(j + 1, sp_[:, :], P)
                    dve.memset(R[:, :], 0.0).then_inc(s_R, 1)
                    dve.wait_ge(s_R, (NPG + 1) * j + 1)
                    dve.wait_ge(s_m, 1)
                    dve.wait_ge(s_sp, j + 2)
                    dve.tensor_copy(R[0:TQ, (NPG - 1) * W64:NPG * W64], spn[:, j * W64:(j + 1) * W64]).then_inc(s_R, 1)
                    for g in range(NPG - 2, -1, -1):
                        dve.wait_ge(s_R, (NPG + 1) * j + NPG - g)
                        dve.tensor_tensor(R[:, g * W64:(g + 1) * W64], R[:, (g + 1) * W64:(g + 2) * W64],
                                          sp_[:, (g + 1) * W64:(g + 2) * W64], ALU.add).then_inc(s_R, 1)
                if j >= 1:
                    n = j - 1
                    dve.wait_ge(s_o, n + 1)
                    for hh in range(2):
                        r = 64 * hh
                        o = PS[r:r + 64, 6 + n % 2, 0:64].rearrange("p (k c) -> p k c", k=4)
                        q = dve.tensor_copy(core.M[r:r + 64, 4:8, SEQ + n * TQ:SEQ + (n + 1) * TQ],
                                            o[:, :, hh * TQ:(hh + 1) * TQ])
                    q.then_inc(s_oc, 1)


def hgrn_prepare(nc, core, tag, B, QE, KK):
    with ExitStack() as es:
        sb, sem = scope(nc, es, tag)
        lb = sb("lower", [P, 5, HGH])
        ada = AdaPart(core, sb, sem, [(0, c) for c in range(4, 10)], 6, 7, ring=4)
        s_a, s_d, s_g = sem("act_step"), sem("dve_step"), sem("scan")
        F = core.BIG[:, 0:HGH, :]
        block = es.enter_context(nc.Block())

        @block.sync
        def _(sp):
            ada.load(sp)

        @block.tensor
        def _(pe):
            ada.products(pe)

        @block.scalar
        def _(act):
            act.activation(KK[:, :, :], F, ACT.Sigmoid, scale=-1.0).then_inc(s_a, 1)
            act.preload_act_table_set("natural_log_exp_and_others")
            act.activation(QE[:, :, :], F, ACT.Abs).then_inc(s_a, 1)
            act.wait_ge(s_a, 2)
            act.activation(QE[:, :, :], QE[:, :, :], ACT.Exp, scale=-1.0).then_inc(s_a, 1)
            act.wait_ge(s_a, 3)
            act.activation(QE[:, :, :], QE[:, :, :], ACT.Ln, bias=1.0).then_inc(s_a, 1)
            ada.copy(act, 0)
            ada.copy(act, 1)
            act.wait_ge(s_d, 1)
            act.activation(lb[:, 1, :], lb[:, 0, :], ACT.Exp).then_inc(s_a, 1)
            for h in range(HGH):
                act.wait_ge(s_g, h + 1)
                act.wait_ge(s_d, 3)
                act.activation(QE[:, h, :], B[:, h, :], ACT.Exp).then_inc(s_a, 1)
                ada.copy(act, 2 + h)
            act.wait_ge(s_d, 9)
            act.activation(F, F, ACT.Exp).then_inc(s_a, 1)

        @block.vector
        def _(dve):
            x = core.vec[:, LB:LB + HGH]
            dve.tensor_tensor(lb[:, 0, :], x, x, ALU.subtract).then_inc(s_d, 1)
            dve.wait_ge(s_a, 5)
            dve.reciprocal(lb[:, 2, :], lb[:, 1, :]).then_inc(s_d, 1)
            dve.scalar_tensor_tensor(out=F, in0=F, scalar=0.0, in1=QE[:, :, :], op0=ALU.min,
                                     op1=ALU.subtract).then_inc(s_d, 1)
            dve.wait_ge(s_d, 3)
            dve.tensor_tensor(lb[:, 3, :], lb[:, 1, :], lb[:, 2, :], ALU.mult).then_inc(s_d, 1)
            dve.wait_ge(s_d, 4)
            dve.tensor_tensor(lb[:, 4, :], lb[:, 3, :], lb[:, 3, :], ALU.subtract).then_inc(s_d, 1)
            dve.wait_ge(s_d, 5)
            dve.tensor_scalar(lb[:, 4, :], lb[:, 4, :], 0.0, None, ALU.max).then_inc(s_d, 1)
            dve.wait_ge(s_d, 6)
            dve.tensor_scalar(lb[:, 4, :], lb[:, 4, :], -1.0, 1.0, ALU.mult, ALU.add).then_inc(s_d, 1)
            dve.wait_ge(s_d, 7)
            for h in range(HGH):
                q = dve.tensor_scalar(KK[:, h, :], KK[:, h, :], lb[:, 4, h:h + 1], None, ALU.mult)
                dve.tensor_tensor_scan(B[:, h, :], cols(core, "reset"), F[:, h, :], 0.0, ALU.mult, ALU.add)\
                   .then_inc(s_g, 1)
            dve.wait_ge(s_g, HGH)
            ends = B[:, :, 0:SEQ].rearrange("p h (c t) -> p h c t", t=CH)[:, :, :, CH - 1:CH]
            for h in range(HGH):
                d = dve.tensor_tensor(F[:, h, 0:SEQ].rearrange("p (c t) -> p c t", t=CH),
                                      ends[:, h].to_broadcast([P, SEQ // CH, CH]),
                                      B[:, h, 0:SEQ].rearrange("p (c t) -> p c t", t=CH), ALU.subtract)
            d.then_inc(s_d, 1)
            for h in range(HGH):
                bs = samples(B[:, h, :])
                d = dve.tensor_tensor(samples(F[:, h, :]), bs[:, :, TQ - 1:TQ].to_broadcast([P, NSEQ, TQ]), bs,
                                      ALU.subtract)
            d.then_inc(s_d, 1)
            for h in range(HGH):
                dve.wait_ge(s_a, 6 + h)
                dve.tensor_tensor(QE[:, h, :], QE[:, h, :], core.M[:, h, :], ALU.mult).then_inc(s_d, 1)
            dve.wait_ge(s_a, 10)
            for h in range(HGH):
                dve.tensor_tensor(F[:, h, :], F[:, h, :], KK[:, h, :], ALU.mult)
            ada.finish(dve)


def hgrn_pairs(nc, core, tag, B, KK, A):
    with ExitStack() as es:
        sb, sem = scope(nc, es, tag)
        E = sb("decay", [P, 2, TP])
        Qt = sb("q_scaled", [P, 2, TP])
        Kt = sb("k_scaled", [P, 2, TP])
        ada = AdaPart(core, sb, sem, [(0, 10), (0, 11)] + [(1, c) for c in range(4)], 6, 7)
        s_d, s_a, s_e, s_q, s_k, s_mm, s_A, s_A0 = (sem(n) for n in (
            "diff", "abs_out", "exp_out", "q_out", "k_out", "mm", "kept", "zeroed"))
        PS = core.PS
        units = [(h, l) for h in range(HGH) for l in range(LEVELS)]
        number = lambda u: u - u // LEVELS - 1
        width = lambda l: T if l <= 3 else SEQ
        masks = cols(core, "levels").bitcast(I32).rearrange("p (l t) -> p l t", l=LEVELS)
        block = es.enter_context(nc.Block())

        @block.sync
        def _(sp):
            ada.load(sp)

        @block.vector
        def _(dve):
            dve.memset(A[:, :, :, :], 0.0).then_inc(s_A0, 1)

            def diff(u):
                h, l = units[u]
                if l == 0:
                    return
                e, n, half = number(u), width(l), 2 ** (l - 1)
                if e >= 2:
                    dve.wait_ge(s_q, e - 1)
                    dve.wait_ge(s_k, e - 1)
                b = B[:, h, 0:n].rearrange("p (n t) -> p n t", t=2 * half)
                c = b[:, :, half - 1:half].to_broadcast([P, n // (2 * half), 2 * half])
                dve.tensor_tensor(E[:, e % 2, 0:n].rearrange("p (n t) -> p n t", t=2 * half), b, c,
                                  ALU.subtract).then_inc(s_d, 1)

            def keep(u):
                h, l = units[u]
                dve.wait_ge(s_mm, u + 1)
                dve.wait_ge(s_A0, 1)
                s = 3 * (u % 2)
                if u:
                    dve.wait_ge(s_A, u)
                for b in range(2):
                    q = dve.copy_predicated(A[:, h, 4 * b:4 * b + 4, :], masks[:, l:l + 1, :].to_broadcast([P, 4, P]),
                                            PS[:, s + b, :].rearrange("p (c t) -> p c t", c=4))
                if l <= 3:
                    q = dve.copy_predicated(A[0:NS, h, 8, 0:NS], masks[0:NS, l, 0:NS], PS[0:NS, s + 2, 0:NS])
                q.then_inc(s_A, 1)

            diff(1)
            for u in range(len(units)):
                h, l = units[u]
                e, n = number(u), width(l)
                if l > 0:
                    dve.wait_ge(s_e, e + 1)
                    if e >= 2:
                        dve.wait_ge(s_mm, u - 1)
                    dve.tensor_tensor(Kt[:, e % 2, 0:n], KK[:, h, 0:n], E[:, e % 2, 0:n], ALU.mult).then_inc(s_k, 1)
                if u + 2 < len(units):
                    diff(u + 2)
                if u >= 1:
                    keep(u - 1)
            keep(len(units) - 1)
            ada.finish(dve)

        @block.scalar
        def _(act):
            for u, (h, l) in enumerate(units):
                if u >= 6 and (u - 2) % 4 == 0 and (u - 6) // 4 < len(ada.chunks):
                    ada.copy(act, (u - 6) // 4)
                if l == 0:
                    continue
                e, n = number(u), width(l)
                act.wait_ge(s_d, e + 1)
                act.activation(E[:, e % 2, 0:n], E[:, e % 2, 0:n], ACT.Abs).then_inc(s_a, 1)
                act.wait_ge(s_a, e + 1)
                act.activation(E[:, e % 2, 0:n], E[:, e % 2, 0:n], ACT.Exp, scale=-1.0).then_inc(s_e, 1)

        @block.gpsimd
        def _(pool):
            for u, (h, l) in enumerate(units):
                if l == 0:
                    continue
                e, n = number(u), width(l)
                pool.wait_ge(s_e, e + 1)
                if e >= 2:
                    pool.wait_ge(s_mm, u - 1)
                pool.tensor_tensor(Qt[:, e % 2, 0:n], core.M[:, h, 0:n], E[:, e % 2, 0:n], ALU.mult).then_inc(s_q, 1)

        @block.tensor
        def _(pe):
            for u, (h, l) in enumerate(units):
                e = number(u)
                if l > 0:
                    pe.wait_ge(s_q, e + 1)
                    pe.wait_ge(s_k, e + 1)
                if u >= 2:
                    pe.wait_ge(s_A, u - 1)
                kt = KK[:, h, :] if l == 0 else Kt[:, e % 2, :]
                qt = core.M[:, h, :] if l == 0 else Qt[:, e % 2, :]
                s = 3 * (u % 2)
                for c in range(8):
                    q = pe.matmul(PS[:, s + c // 4, (c % 4) * P:(c % 4 + 1) * P], kt[:, c * P:(c + 1) * P],
                                  qt[:, c * P:(c + 1) * P], start=True, stop=True)
                if l <= 3:
                    q = pe.matmul(PS[0:NS, s + 2, 0:NS], kt[:, SEQ:T], qt[:, SEQ:T], start=True, stop=True)
                q.then_inc(s_mm, 1)
                if u < ada.units:
                    ada.product(pe, u)
            ada.turn(pe, len(ada.chunks) - 1)


def hgrn_states(nc, core, tag, B, QE, A):
    with ExitStack() as es:
        sb, sem = scope(nc, es, tag)
        IT = sb("v_rows", [P, 9, P])
        KH = sb("k_rows", [P, 9, P])
        S = sb("state", [P, 9, P])
        S0 = sb("s_state", [P, NSEQ, P])
        VB = sb("v_blocks", [NS, NSEQ, P])
        eb = sb("decay_end", [P, HGH, 8 + NSEQ])
        s_s0, s_eb, s_T, s_c, s_vb, s_ds, s_S, s_Sz, s_o, s_oc, s_sm, s_ss = (sem(n) for n in (
            "s0_in", "decay_out", "turned", "rows_out", "blocks_out", "ds_mm", "state_out", "state_zero", "o_mm", "o_out",
            "s_scaled", "s_new"))
        s_out = [sem("S_stored"), sem("Ss_stored")]
        PS = core.PS
        block = es.enter_context(nc.Block())

        @block.sync
        def _(sp):
            for h in range(HGH):
                if h:
                    sp.wait_ge(s_out[1], 16 * h)
                    sp.wait_ge(s_o, h)
                sp.dma_start(S0[:, :, :], core.state_hgrn[0, :, h].rearrange("s k v -> k s v")).then_inc(s_s0, 16)
                sp.wait_ge(s_S, 8 * (h + 1))
                sp.dma_start(core.o_S_p[0, 0, h], S[:, 8, :]).then_inc(s_out[0], 16)
                sp.wait_ge(s_ss, h + 1)
                sp.dma_start(core.o_S_s[0, :, h].rearrange("s k v -> k s v"), S0[:, :, :]).then_inc(s_out[1], 16)
            sp.wait_ge(s_out[0], 16 * HGH)
            sp.wait_ge(s_out[1], 16 * HGH)

        @block.scalar
        def _(act):
            for h in range(HGH):
                act.activation(eb[:, h, 0:8], B[:, h, 0:SEQ].rearrange("p (c t) -> p c t", t=CH)[:, :, CH - 1], ACT.Exp)
                q = act.activation(eb[:, h, 8:8 + NSEQ], samples(B[:, h, :])[:, :, TQ - 1], ACT.Exp)
            q.then_inc(s_eb, 1)

        @block.tensor
        def _(pe):
            for h in range(HGH):
                for w, src in enumerate((core.BIG[:, HGH + h, :], core.BIG[:, h, :])):
                    if w:
                        pe.wait_ge(s_c, 2 * h + 1)
                    elif h:
                        pe.wait_ge(s_oc, h)
                    for i in range(9):
                        n = P if i < 8 else NS
                        q = pe.transpose(PS[0:n, i // 4, (i % 4) * P:(i % 4 + 1) * P], src[:, i * P:i * P + n],
                                         cols(core, "ident"))
                    q.then_inc(s_T, 1)
                pe.wait_ge(s_c, 2 * h + 2)
                if h:
                    pe.wait_ge(s_S, 8 * h)
                    pe.wait_ge(s_ss, h)
                for c in range(8):
                    pe.matmul(PS[:, 3 + c // 4, (c % 4) * P:(c % 4 + 1) * P], KH[:, c, :], IT[:, c, :], start=True, stop=True)
                pe.wait_ge(s_vb, h + 1)
                for b in range(2):
                    q = pe.matmul(PS[:, 5 + b, :], KH[0:NS, 8, :], VB[:, 4 * b:4 * b + 4, :].rearrange("p s v -> p (s v)"),
                                  start=True, stop=True)
                q.then_inc(s_ds, 1)
                for c in range(8):
                    o = PS[:, c // 4, (c % 4) * P:(c % 4 + 1) * P]
                    pe.matmul(o, IT[:, c, :], A[:, h, c, :], start=True, stop=(c == 0))
                    if c:
                        pe.wait_ge(s_S, 8 * h + c)
                        pe.matmul(o, S[:, c, :], QE[:, h, c * P:(c + 1) * P], start=False, stop=True)
                pe.wait_ge(s_s0, 16 * (h + 1))
                pe.matmul(PS[:, 2, 0:NS], IT[0:NS, 8, :], A[0:NS, h, 8, 0:NS], start=True, stop=True)
                for j in range(NSEQ):
                    q = pe.matmul(PS[:, 2, j * TQ:(j + 1) * TQ], S0[:, j, :], QE[:, h, SEQ + j * TQ:SEQ + (j + 1) * TQ],
                                  start=False, stop=True, skip_group_check=True)
                q.then_inc(s_o, 1)

        @block.vector
        def _(dve):
            dve.wait_ge(s_eb, 1)
            for h in range(HGH):
                for w, dst in enumerate((IT, KH)):
                    dve.wait_ge(s_T, 2 * h + w + 1)
                    dve.tensor_copy(dst[:, 0:8, :], PS[:, 0:2, :].rearrange("p b (c t) -> p (b c) t", c=4))
                    dve.tensor_copy(dst[0:NS, 8, :], PS[0:NS, 2, 0:P]).then_inc(s_c, 1)
                dve.wait_ge(s_c, 2 * h + 2)
                dve.tensor_tensor(VB[:, :, :], IT[0:NS, 8:9, :].to_broadcast([NS, NSEQ, P]),
                                  cols(core, "blk")[0:NS, :].unsqueeze(2).to_broadcast([NS, NSEQ, P]), ALU.mult)\
                   .then_inc(s_vb, 1)
                dve.wait_ge(s_ds, h + 1)
                if h:
                    dve.wait_ge(s_out[0], 16 * h)
                for c in range(8):
                    ds = PS[:, 3 + c // 4, (c % 4) * P:(c % 4 + 1) * P]
                    if c == 0:
                        dve.tensor_copy(S[:, 1, :], ds).then_inc(s_S, 1)
                    else:
                        dve.wait_ge(s_S, 8 * h + c)
                        dve.scalar_tensor_tensor(out=S[:, c + 1, :], in0=S[:, c, :], scalar=eb[:, h, c:c + 1], in1=ds,
                                                 op0=ALU.mult, op1=ALU.add).then_inc(s_S, 1)
                dve.wait_ge(s_o, h + 1)
                for b in range(2):
                    dve.tensor_copy(core.M[:, h, b * 512:(b + 1) * 512], PS[:, b, :])
                dve.tensor_copy(core.M[:, h, SEQ:T], PS[:, 2, 0:NS]).then_inc(s_oc, 1)
                dve.tensor_tensor(S0[:, :, :], S0[:, :, :], eb[:, h, 8:8 + NSEQ].unsqueeze(2).to_broadcast([P, NSEQ, P]),
                                  ALU.mult).then_inc(s_sm, 1)
                dve.wait_ge(s_sm, h + 1)
                dve.tensor_tensor(S0[:, :, :], S0[:, :, :], PS[:, 5:7, :].rearrange("p b (s v) -> p (b s) v", v=P),
                                  ALU.add).then_inc(s_ss, 1)


def hgrn_gate(nc, core, tag):
    with ExitStack() as es:
        sb, sem = scope(nc, es, tag)
        sq = sb("sq", [P, 2, TP])
        rt = sb("root", [TB, HGH, NBK])
        r = sb("rstd", [TB, HGH, NBK])
        s_sg, s_sq, s_ss, s_rt, s_r, s_bc, s_y, s_z = (sem(n) for n in (
            "silu", "sq_out", "sumsq", "root_out", "rstd", "rstd_spread", "y", "pads"))
        G = core.BIG[:, 2 * HGH:3 * HGH, :]
        ada = AdaPart(core, sb, sem, [(1, c) for c in range(4, 8)], 7, 0, ring=6)
        PS = core.PS
        block = es.enter_context(nc.Block())

        @block.sync
        def _(sp):
            ada.load(sp)

        @block.scalar
        def _(act):
            act.wait_ge(s_z, 1)
            for h in range(HGH):
                if h >= 2:
                    act.wait_ge(s_ss, h - 1)
                act.activation(sq[:, h % 2, :], core.M[:, h, :], ACT.Square).then_inc(s_sq, 1)
            act.wait_ge(s_ss, HGH)
            act.activation(rt[:, :, :].rearrange("p h b -> p (h b)"), PS[0:TB, 6, 0:HGH * NBK], ACT.Sqrt, scale=1.0 / P,
                           bias=cols(core, "eps")[0:TB, :]).then_inc(s_rt, 1)
            for h in range(HGH):
                act.activation(G[:, h, :], G[:, h, :], ACT.Silu).then_inc(s_sg, 1)
            ada.copies(act)

        @block.tensor
        def _(pe):
            for h in range(HGH):
                pe.wait_ge(s_sq, h + 1)
                column_sums(pe, core, 6, h, sq[:, h % 2, :], h == 0).then_inc(s_ss, 1)
            pe.wait_ge(s_r, 1)
            for h in range(HGH):
                if h >= 2:
                    pe.wait_ge(s_y, h - 1)
                spread(pe, core, 3 * (h % 2), r[:, h, :]).then_inc(s_bc, 1)
            pe.wait_ge(s_y, HGH)
            ada.products(pe)

        @block.vector
        def _(dve):
            dve.memset(core.M[:, 0:HGH, T:TP], 0.0).then_inc(s_z, 1)
            dve.wait_ge(s_rt, 1)
            dve.reciprocal(r[:, :, :], rt[:, :, :]).then_inc(s_r, 1)
            for h in range(HGH):
                dve.wait_ge(s_bc, h + 1)
                m = chunked(core.M[:, h, :])
                dve.scalar_tensor_tensor(out=m, in0=m, scalar=core.vec[:, HG_G + h:HG_G + h + 1],
                                         in1=PS[:, 3 * (h % 2):3 * (h % 2) + 3, 0:CW], op0=ALU.mult, op1=ALU.mult)\
                   .then_inc(s_y, 1)
                dve.wait_ge(s_y, h + 1)
                dve.wait_ge(s_sg, h + 1)
                dve.tensor_tensor(core.M[:, h, :], core.M[:, h, :], G[:, h, :], ALU.mult)
            ada.finish(dve)


def hgrn(nc, core, tag):
    with ExitStack() as es:
        sb = lambda name, shape: es.enter_context(nc.sbuf_tensor(f"{tag}_{name}", shape, F32))
        B = sb("log_decay", [P, HGH, TP])
        QE = sb("q_decayed", [P, HGH, TP])
        A = sb("pairs", [P, HGH, 9, P])
        with nc.sbuf_tensor(f"{tag}_k", [P, HGH, TP], F32) as KK:
            hgrn_prepare(nc, core, tag + "_prep", B, QE, KK)
            hgrn_pairs(nc, core, tag + "_pairs", B, KK, A)
        hgrn_states(nc, core, tag + "_states", B, QE, A)
    hgrn_gate(nc, core, tag + "_gate")


UX = PH + SEQ + NSEQ * (PH + TQ)
GX = CHI + SEQ + NSEQ * (CHI + TQ)


def ext_parts(ap, hist):
    return ap[..., hist:hist + SEQ], ap[..., hist + SEQ:]


def odd_prepare(nc, core, tag, U, G):
    with ExitStack() as es:
        sb, sem = scope(nc, es, tag)
        hp = sb("pool_hist", [NSEQ * PH, HALF])
        hc = sb("conv_hist", [NSEQ * CHI // 2, 2, HALF])
        rows = sb("rows", [NS, 4, HALF])
        s_in, s_hist, s_sg, s_glu, s_T, s_ev, s_R, s_rc = (sem(n) for n in (
            "hist_in", "hist_kept", "sigmoid", "glu", "turned", "hist_out", "rows_T", "rows_out"))
        s_out = sem("stored")
        PS = core.PS
        Ut, A_, GT = core.BIG[:, 0:4, :], core.BIG[:, 4:8, :], core.BIG[:, 8:12, :]
        block = es.enter_context(nc.Block())

        @block.sync
        def _(sp):
            sp.dma_start(hp[:, :], core.state_pool.rearrange("o b t f -> (o b t) f")).then_inc(s_in, 16)
            sp.dma_start(hc[:, :, :], core.state_conv.rearrange("o (h b) t f -> (o b t) h f", h=2)).then_inc(s_in, 16)
            sp.dma_start(core.o_pool_s[0, :, 0:PH - TQ, :], core.state_pool[0, :, TQ:PH, :]).then_inc(s_hist, 16)
            sp.dma_start(core.o_conv_s[0, :, 0:CHI - TQ, :], core.state_conv[0, :, TQ:CHI, :]).then_inc(s_hist, 16)
            sp.wait_ge(s_rc, 4)
            sp.dma_start(core.o_pool_p[0, 0], rows[0:PH, 0, :]).then_inc(s_out, 16)
            sp.dma_start(core.o_conv_p[0, 0], rows[0:CHI, 2, :]).then_inc(s_out, 16)
            for i, (dst, n) in enumerate(((core.o_pool_s, PH), (core.o_conv_s, CHI))):
                for b in range(NSEQ):
                    sp.dma_start(dst[0, b, n - TQ:n, :], rows[b * TQ:(b + 1) * TQ, 2 * i + 1, :]).then_inc(s_out, 16)
            sp.wait_ge(s_hist, 32)
            sp.wait_ge(s_out, 16 * (2 + 2 * NSEQ))

        @block.scalar
        def _(act):
            for k in range(HT):
                act.activation(GT[:, k, :], GT[:, k, :], ACT.Sigmoid).then_inc(s_sg, 1)

        @block.tensor
        def _(pe):
            pe.wait_ge(s_in, 32)
            ident = cols(core, "ident")
            for i in range(3):
                n = NSEQ * PH
                for k in range(HT):
                    src = hp[:, k * P:(k + 1) * P] if i == 0 else hc[:, i - 1, k * P:(k + 1) * P]
                    q = pe.transpose(PS[:, i, k * P:k * P + n], src, ident[0:n, 0:n])
                q.then_inc(s_T, 1)
            for i, (src, n) in enumerate(((Ut, PH), (Ut, NS), (A_, CHI), (A_, NS))):
                if i == 2:
                    pe.wait_ge(s_glu, HT)
                at = SEQ - n if n != NS else SEQ
                for k in range(HT):
                    q = pe.transpose(PS[0:n, 4 + i, k * P:(k + 1) * P], src[:, k, at:at + n], ident)
                q.then_inc(s_R, 1)

        @block.vector
        def _(dve):
            dve.memset(U[:, :, 0:PH], 0.0)
            dve.memset(G[:, :, 0:CHI], 0.0)
            dve.wait_ge(s_T, 3)
            for k in range(HT):
                ux = U[:, k, PH + SEQ:].rearrange("p (s t) -> p s t", s=NSEQ)
                dve.tensor_copy(ux[:, :, 0:PH], PS[:, 0, k * P:k * P + NSEQ * PH].rearrange("p (s t) -> p s t", s=NSEQ))
                gx = G[:, k, CHI + SEQ:].rearrange("p (s t) -> p s t", s=NSEQ)
                for h in range(2):
                    dve.tensor_copy(gx[:, 4 * h:4 * h + 4, 0:CHI],
                                    PS[:, 1 + h, k * P:k * P + 4 * CHI].rearrange("p (s t) -> p s t", s=4))
            for k in range(HT):
                dve.wait_ge(s_sg, k + 1)
                dve.tensor_tensor(A_[:, k, :], A_[:, k, :], GT[:, k, :], ALU.mult).then_inc(s_glu, 1)
            for i, n in enumerate((PH, NS, CHI, NS)):
                dve.wait_ge(s_R, i + 1)
                dve.tensor_copy(rows[0:n, i, :], PS[0:n, 4 + i, :]).then_inc(s_rc, 1)

        @block.gpsimd
        def _(pool):
            for k in range(HT):
                pool.tensor_copy(U[:, k, PH:PH + SEQ], Ut[:, k, 0:SEQ])
                pool.tensor_copy(U[:, k, PH + SEQ:].rearrange("p (s t) -> p s t", s=NSEQ)[:, :, PH:], samples(Ut[:, k, :]))
            for k in range(HT):
                pool.wait_ge(s_glu, k + 1)
                pool.tensor_copy(G[:, k, CHI:CHI + SEQ], A_[:, k, 0:SEQ])
                pool.tensor_copy(G[:, k, CHI + SEQ:].rearrange("p (s t) -> p s t", s=NSEQ)[:, :, CHI:], samples(A_[:, k, :]))


def odd_branches(nc, core, tag, U, G, cv):
    with ExitStack() as es:
        sb, sem = scope(nc, es, tag)
        dg = sb("diag", [P, 2, P])
        sm = sb("sums", [P, 2, UX])
        pw = sb("pool_w", [P, HT, P])
        s_in, s_dg, s_tap, s_acc, s_cv, s_sum, s_pl, s_pp, s_pm, s_out = (sem(n) for n in (
            "pool_w_in", "diag_out", "tap_mm", "acc", "conv_out", "sum", "mean", "pooled", "pool_mm", "pool_out"))
        s_z = sem("pads")
        PS = core.PS
        NPE = 2
        ident = cols(core, "ident")
        block = es.enter_context(nc.Block())
        tail = lambda k: G[:, k, CHI + SEQ:].rearrange("p (s t) -> p s t", s=NSEQ)

        @block.sync
        def _(sp):
            sp.dma_start(pw[:, :, :], core.pool_w.rearrange("o g c d -> c (o g) d")).then_inc(s_in, 16)

        @block.scalar
        def _(act):
            for n in range(NPE):
                k = HT - NPE + n
                with act.Fori(0, (CWID - 1) // 2) as j:
                    for s in range(2):
                        act.wait_ge(s_tap, j * 2 + (n * (CWID + 1) + s + 1))
                        act.activation(dg[:, s, :], ident, ACT.Copy,
                                       scale=core.convw[:, bass.ds(j * (2 * HT) + (s * HT + k), 1)]).then_inc(s_dg, 1)
                act.wait_ge(s_tap, n * (CWID + 1) + CWID)
                act.activation(dg[:, 0, :], ident, ACT.Copy,
                               scale=core.convw[:, (CWID - 1) * HT + k:(CWID - 1) * HT + k + 1]).then_inc(s_dg, 1)
            for n in range(NPE):
                k = HT - NPE + n
                act.wait_ge(s_tap, 2 + (n + 1) * (CWID + 1) - 1)
                b = core.vec[:, CONV_B + k:CONV_B + k + 1]
                act.activation(cv[:, k, 0:SEQ], PS[:, 3 * n:3 * n + 2, :].rearrange("p b c -> p (b c)"), ACT.Identity, bias=b)
                act.activation(cv[:, k, SEQ:T], PS[:, 3 * n + 2, 0:NS], ACT.Identity, bias=b).then_inc(s_cv, 1)
            for g in range(HT):
                act.wait_ge(s_pm, g + 1)
                act.activation(chunked(core.M[:, g, :]), PS[:, 3 * (g % 2):3 * (g % 2) + 3, 0:CW], ACT.Copy,
                               scale=core.vec[:, POOL_S + g:POOL_S + g + 1]).then_inc(s_out, 1)

        @block.tensor
        def _(pe):
            pe.sem_inc(s_tap, 2)

            def tap(slot, n, k, at, first):
                b = 3 * n
                fl = dict(start=first, stop=True, skip_group_check=True)
                for h in range(2):
                    pe.matmul(PS[:, b + h, :], dg[:, slot, :], G[:, k, bass.ds(at + h * 512, 512)], **fl)
                return pe.matmul(PS[:, b + 2, 0:NS].rearrange("p (s t) -> p s t", s=NSEQ), dg[:, slot, :],
                                 tail(k)[:, :, bass.ds(at, TQ)], **fl)

            for n in range(NPE):
                k = HT - NPE + n
                base = n * CWID
                for s in range(2):
                    pe.wait_ge(s_dg, base + s + 1)
                    tap(s, n, k, s, s == 0).then_inc(s_tap, 1)
                with pe.Fori(0, (CWID - 3) // 2) as j:
                    for s in range(2):
                        pe.wait_ge(s_dg, j * 2 + (base + s + 3))
                        tap(s, n, k, j * 2 + (s + 2), False).then_inc(s_tap, 1)
                pe.wait_ge(s_dg, base + CWID)
                tap(0, n, k, CWID - 1, False).then_inc(s_tap, 2)
            pe.wait_ge(s_in, 16)
            for g in range(HT):
                pe.wait_ge(s_pp, g + 1)
                if g < 2:
                    pe.wait_ge(s_cv, g + 1)
                else:
                    pe.wait_ge(s_out, g - 1)
                for c in range(NC3):
                    q = pe.matmul(PS[:, 3 * (g % 2) + c, 0:CW], pw[:, g, :], core.BIG[:, g, c * CW:(c + 1) * CW],
                                  start=True, stop=True)
                q.then_inc(s_pm, 1)

        @block.vector
        def _(dve):
            dve.memset(cv[:, :, T:TP], 0.0).then_inc(s_z, 1)
            dve.sem_inc(s_acc, 2)
            for k in range(HT - NPE):
                b, w0 = core.vec[:, CONV_B + k:CONV_B + k + 1], core.convw[:, k:k + 1]
                dve.tensor_scalar(cv[:, k, 0:SEQ], G[:, k, 0:SEQ], w0, b, ALU.mult, ALU.add)
                dve.tensor_scalar(samples(cv[:, k, :]), tail(k)[:, :, 0:TQ], w0, b, ALU.mult, ALU.add).then_inc(s_acc, 1)
            with dve.Fori(1, CWID) as j:
                for k in range(HT - NPE):
                    w = core.convw[:, bass.ds(j * HT + k, 1)]
                    dve.wait_ge(s_acc, j * 2 + (k + 1))
                    dve.scalar_tensor_tensor(out=cv[:, k, 0:SEQ], in0=G[:, k, bass.ds(j, SEQ)], scalar=w,
                                             in1=cv[:, k, 0:SEQ], op0=ALU.mult, op1=ALU.add)
                    dve.scalar_tensor_tensor(out=samples(cv[:, k, :]), in0=tail(k)[:, :, bass.ds(j, TQ)], scalar=w,
                                             in1=samples(cv[:, k, :]), op0=ALU.mult, op1=ALU.add).then_inc(s_acc, 1)

        @block.gpsimd
        def _(pool):
            n = 0
            for g, w in enumerate(WINDOWS):
                src, h = U[:, g, :], 1
                while h < w:
                    if n:
                        pool.wait_ge(s_sum, n)
                    n += 1
                    dst = sm[:, n % 2, :]
                    pool.tensor_tensor(dst[:, 2 * h - 1:UX], src[:, 2 * h - 1:UX], src[:, h - 1:UX - h], ALU.add).then_inc(s_sum, 1)
                    src, h = dst, 2 * h
                pool.wait_ge(s_sum, n)
                u = core.BIG[:, g, :]
                pool.tensor_tensor(src[:, PH:PH + 16], src[:, PH:PH + 16], cols(core, "cnt", 16 * g, 16 * g + 16), ALU.mult)\
                    .then_inc(s_pl, 1)
                pool.wait_ge(s_pl, 2 * g + 1)
                pool.tensor_scalar(src[:, PH:UX], src[:, PH:UX], 1.0 / w, None, ALU.mult).then_inc(s_pl, 1)
                pool.wait_ge(s_pl, 2 * g + 2)
                pool.tensor_tensor(u[:, 0:SEQ], src[:, PH:PH + SEQ], u[:, 0:SEQ], ALU.subtract)
                sx = src[:, PH + SEQ:].rearrange("p (s t) -> p s t", s=NSEQ)[:, :, PH:]
                pool.tensor_tensor(samples(u), sx, samples(u), ALU.subtract).then_inc(s_pp, 1)
                if g + 1 < HT:
                    pool.wait_ge(s_pp, g + 1)


def odd_norm(nc, core, tag, cv):
    with ExitStack() as es:
        sb, sem = scope(nc, es, tag)
        sq = sb("sq", [P, HT, TP])
        mu = sb("mu", [P, TP])
        rt = sb("root", [TB, NBK])
        r = sb("rstd", [TB, NBK])
        s_bc, s_sum = sem("rstd_spread"), sem("squares_added")
        s_mu, s_muc, s_c, s_sq, s_ss, s_rt, s_r, s_y, s_o, s_z = (sem(n) for n in (
            "mean_mm", "mean_out", "centred", "sq_out", "sumsq", "root_out", "rstd", "y", "out", "pads"))
        PS = core.PS
        block = es.enter_context(nc.Block())

        @block.tensor
        def _(pe):
            for k in range(HT):
                for c in range(NC3):
                    q = pe.matmul(PS[:, c, 0:CW], cols(core, "ones").to_broadcast([P, P]), cv[:, k, c * CW:(c + 1) * CW],
                                  start=(k == 0), stop=(k == HT - 1))
            q.then_inc(s_mu, 1)
            pe.wait_ge(s_sum, HT - 1)
            column_sums(pe, core, 6, 0, sq[:, 0, :], True).then_inc(s_ss, 1)
            pe.wait_ge(s_r, 1)
            spread(pe, core, 3, r).then_inc(s_bc, 1)

        @block.scalar
        def _(act):
            act.wait_ge(s_mu, 1)
            act.activation(chunked(mu[:, :]), PS[:, 0:NC3, 0:CW], ACT.Copy, scale=1.0 / HALF).then_inc(s_muc, 1)
            for k in range(HT):
                act.wait_ge(s_c, k + 1)
                act.activation(sq[:, k, :], cv[:, k, :], ACT.Square).then_inc(s_sq, 1)
            act.wait_ge(s_ss, 1)
            act.activation(rt[:, :], PS[0:TB, 6, 0:NBK], ACT.Sqrt, scale=1.0 / HALF,
                           bias=cols(core, "eps")[0:TB, :]).then_inc(s_rt, 1)
            for k in range(HT):
                act.wait_ge(s_y, k + 1)
                act.activation(core.M[:, HT + k, :], cv[:, k, :], ACT.Silu, scale=core.vec[:, LN_G + k:LN_G + k + 1],
                               bias=core.vec[:, LN_B + k:LN_B + k + 1]).then_inc(s_o, 1)

        @block.vector
        def _(dve):
            dve.wait_ge(s_muc, 1)
            for k in range(HT):
                dve.tensor_tensor(cv[:, k, :], cv[:, k, :], mu[:, :], ALU.subtract).then_inc(s_c, 1)
            dve.wait_ge(s_rt, 1)
            dve.reciprocal(r[:, :], rt[:, :]).then_inc(s_r, 1)
            dve.wait_ge(s_bc, 1)
            for k in range(HT):
                dve.tensor_tensor(chunked(cv[:, k, :]), chunked(cv[:, k, :]), PS[:, 3:6, 0:CW], ALU.mult).then_inc(s_y, 1)
            dve.wait_ge(s_o, HT)
            dve.memset(core.M[:, HT:2 * HT, T:TP], 0.0)

        @block.gpsimd
        def _(pool):
            for k in range(1, HT):
                pool.wait_ge(s_sq, k + 1)
                if k >= 2:
                    pool.wait_ge(s_sum, k - 1)
                pool.tensor_tensor(sq[:, 0, :], sq[:, 0, :], sq[:, k, :], ALU.add).then_inc(s_sum, 1)


def odd_mixer(nc, core, tag):
    with ExitStack() as es:
        sb = lambda name, shape: es.enter_context(nc.sbuf_tensor(f"{tag}_{name}", shape, F32))
        G = sb("glu", [P, HT, GX])
        cv = sb("conv", [P, HT, TP])
        U = sb("u", [P, HT, UX])
        odd_prepare(nc, core, tag + "_prep", U, G)
        odd_branches(nc, core, tag + "_branches", U, G, cv)
        odd_norm(nc, core, tag + "_norm", cv)


INPUTS = ["x_prompt", "x_sample", "c_prompt", "c_sample", "cache_sb_k", "cache_sb_v", "state_hgrn", "state_pool",
          "state_conv", "page_table", "norm_g", "ada_w", "ada_b", "even_w_in", "even_w_out", "sb_bias",
          "hgrn_lb_logits", "hgrn_norm_g", "odd_w_in", "odd_w_out", "pool_w", "pool_scale", "conv_w", "conv_b",
          "conv_ln_g", "conv_ln_b", "mlp_w1", "mlp_w2"]

OUTPUTS = [("y_prompt", (1, SEQ, D)), ("y_sample", (NSEQ, TQ, D)),
           ("sb_k_prompt", (1, 1, SEQ, SBH, SBD)), ("sb_v_prompt", (1, 1, SEQ, SBH, SBD)),
           ("sb_k_sample", (1, NSEQ, TQ, SBH, SBD)), ("sb_v_sample", (1, NSEQ, TQ, SBH, SBD)),
           ("hgrn_prompt", (1, 1, HGH, P, P)), ("hgrn_sample", (1, NSEQ, HGH, P, P)),
           ("pool_prompt", (1, 1, PH, HALF)), ("pool_sample", (1, NSEQ, PH, HALF)),
           ("conv_prompt", (1, 1, CHI, HALF)), ("conv_sample", (1, NSEQ, CHI, HALF))]


def open_core(nc, es, ins):
    c = Core()
    (c.x_prompt, c.x_sample, c.c_prompt, c.c_sample, c.cache_k, c.cache_v, c.state_hgrn, c.state_pool,
     c.state_conv, c.page_table, c.norm_g, c.ada_w, c.ada_b, c.even_w_in, c.even_w_out, c.sb_bias,
     c.hgrn_lb_logits, c.hgrn_norm_g, c.odd_w_in, c.odd_w_out, c.pool_w, c.pool_scale, c.conv_w, c.conv_b,
     c.conv_ln_g, c.conv_ln_b, c.mlp_w1, c.mlp_w2) = (ins[n] for n in INPUTS)
    c.even_w_in, c.even_w_out, c.odd_w_in, c.odd_w_out = (w[0] for w in (c.even_w_in, c.even_w_out, c.odd_w_in, c.odd_w_out))
    c.const_in = ins["consts"]
    sb = lambda n, s, d=F32: es.enter_context(nc.sbuf_tensor(n, s, d))
    c.const = sb("const", [P, NCONST])
    c.mod = sb("mod", [P, 2, N_MOD * KT * SEGP])
    c.coef = sb("coef", [P, 2, 4, KT * SEGP])
    c.ada_bT = sb("ada_bT", [P, 96])
    c.vec = sb("vec", [P, VP])
    c.convw = sb("convw", [P, CWID * HT])
    c.sb_bias_bc = sb("sb_bias_bc", [P, SBH])
    c.cT = sb("cT", [P, KT, SEGP])
    c.M = sb("M", [P, KT, TP])
    (c.o_y_p, c.o_y_s, c.o_k_p, c.o_v_p, c.o_k_s, c.o_v_s, c.o_S_p, c.o_S_s, c.o_pool_p, c.o_pool_s, c.o_conv_p,
     c.o_conv_s) = (ins[n] for n, _ in OUTPUTS)
    c.x_dram = nc.dram_tensor("x_scratch", [P, KT * TP], F32, kind="Internal").ap()
    c.PS = es.enter_context(nc.psum_tensor("PS", [P, 8, 512], F32))
    return c


def rows_out(nc, core, tag, X):
    with ExitStack() as es:
        sb, sem = scope(nc, es, tag)
        rows = sb("rows", [P, 2, D])
        s_T, s_cp = sem("turned"), sem("copied")
        s_out = [sem(f"stored{i}") for i in range(2)]
        PS = core.PS
        n_rows = lambda i: P if i < 8 else NS
        block = es.enter_context(nc.Block())

        @block.tensor
        def _(pe):
            for i in range(9):
                if i >= 2:
                    pe.wait_ge(s_cp, i - 1)
                n = n_rows(i)
                for k in range(KT):
                    q = pe.transpose(PS[0:n, 2 * (i % 2) + k // 4, (k % 4) * P:(k % 4 + 1) * P],
                                     X[:, k, i * P:i * P + n], cols(core, "ident"))
                q.then_inc(s_T, 1)

        @block.vector
        def _(dve):
            for i in range(9):
                dve.wait_ge(s_T, i + 1)
                if i >= 2:
                    dve.wait_ge(s_out[i % 2], 16 * (i // 2))
                n = n_rows(i)
                dve.tensor_copy(rows[0:n, i % 2, :], PS[0:n, 2 * (i % 2):2 * (i % 2) + 2, :].rearrange("p b c -> p (b c)"))\
                   .then_inc(s_cp, 1)

        @block.sync
        def _(sp):
            for i in range(9):
                sp.wait_ge(s_cp, i + 1)
                dst = core.o_y_p[0, i * P:(i + 1) * P, :] if i < 8 else core.o_y_s.rearrange("b t d -> (b t) d")
                sp.dma_start(dst, rows[0:n_rows(i), i % 2, :]).then_inc(s_out[i % 2], 16)
            sp.wait_ge(s_out[0], 16 * 5)
            sp.wait_ge(s_out[1], 16 * 4)


def ring_of_pages(tiles):
    return tiles.rearrange("p a b -> p (a b)")[:, 0:8 * HALF].rearrange("p (i f) -> p i f", f=HALF)


def step(nc, ins):
    with ExitStack() as top:
        core = open_core(nc, top, ins)
        M = core.M
        with nc.sbuf_tensor("big0", [P, 3 * HT, TP], F32) as big:
            core.BIG = big
            setup(nc, core, "setup", big[:, 0:KT, :])
            with ExitStack() as es:
                open_split(nc, es, core, "in0")
                residual_norm(nc, core, "norm00", big[:, 0:KT, :], False, None, None, (0, 0), (0, 0), True)
                KV, spare = big[:, 0:KT, :], ring_of_pages(big[:, KT:KT + HT, :])
                sb_at = 4 * HALF
                dense(nc, core, "qkv", core.even_w_in, [(sb_at, HT, M[:, HT:2 * HT, :]), (sb_at + HALF, 2 * HT, KV)])
                kv_rows(nc, core, "kv_rows", KV, spare)
                sb_prompt(nc, core, "sb_prompt", KV, spare)
                sb_sample(nc, core, "sb_sample", KV, ring_of_pages(M[:, 0:HT, :]), spare)
                dense(nc, core, "qfig", core.even_w_in, [(0, HT, M[:, 0:HT, :]), (HALF, 3 * HT, big)])
            hgrn(nc, core, "hgrn")
        mlp_of_layer(nc, core, 0, core.even_w_out, M)
        with nc.sbuf_tensor("big1", [P, 3 * HT, TP], F32) as big:
            core.BIG = big
            with ExitStack() as es:
                open_split(nc, es, core, "in1")
                residual_norm(nc, core, "norm10", big[:, 0:KT, :], True, M, (0, 3), (1, 0), (1, 0), True)
                dense(nc, core, "odd_in", core.odd_w_in, [(0, 3 * HT, big)])
            odd_mixer(nc, core, "odd")
        mlp_of_layer(nc, core, 1, core.odd_w_out, M)
        with nc.sbuf_tensor("x_end", [P, KT, TP], F32) as X:
            residual_norm(nc, core, "norm_end", X, True, M, (1, 3), None, None, False, final=True)
            rows_out(nc, core, "rows", X)


def mlp_of_layer(nc, core, l, w_out, M):
    with ExitStack() as es:
        open_split(nc, es, core, f"mid{l}")
        split(nc, core, f"mixed{l}", M)
        dense(nc, core, f"out{l}", w_out, [(0, KT, M)])
        with nc.sbuf_tensor(f"x_mid{l}", [P, KT, TP], F32) as X:
            residual_norm(nc, core, f"norm{l}1", X, True, M, (l, 1), (l, 2), (l, 3 * KT), True,
                          chunks=[] if l else [(1, c) for c in range(8, 12)])
        mlp(nc, core, f"mlp{l}", core.mlp_w1[l], core.mlp_w2[l], M)


def kernel(**inputs):
    import concourse.bacc as bacc
    from concourse.bass_utils import run_bass_kernel_spmd

    nc = bacc.Bacc("TRN2", target_bir_lowering=False, num_devices=1)
    arrays = {name: np.ascontiguousarray(inputs[name]) for name in INPUTS}
    arrays["consts"] = constants()
    aps = {name: nc.dram_tensor(name, a.shape, mybir.dt.from_np(a.dtype), kind="ExternalInput").ap()
           for name, a in arrays.items()}
    for name, shape in OUTPUTS:
        aps[name] = nc.dram_tensor(name, shape, F32, kind="ExternalOutput").ap()
    step(nc, aps)
    result = run_bass_kernel_spmd(nc, [arrays], core_ids=[0])
    return tuple(result.results[0][name] for name, _ in OUTPUTS)
```

```python
from contextlib import ExitStack

import numpy as np
import concourse.bass as bass
from concourse import mybir

F32 = mybir.dt.float32
F32R = mybir.dt.float32r
I32 = mybir.dt.int32
ALU = mybir.AluOpType
ACT = mybir.ActivationFunctionType

P = 128
D = 1024
SEQ = 1024
NSEQ = 8
TQ = 8
NS = NSEQ * TQ
T = SEQ + NS
CW = 364
NC3 = 3
TP = CW * NC3
PAD = TP - T
TB = 91
NBK = TP // TB
KT = D // P
HALF = D // 2
HT = HALF // P
FF = 4 * D
EPS = 1e-6
N_MOD = 6
SEG = 1 + NSEQ
SEGP = 10
PAGE = 128
NPG = 8
SBH = 8
SBD = 64
HGH = 4
CH = 128
LEVELS = 8
WINDOWS = (2, 4, 8, 16)
PH = 15
CWID = 31
CHI = 30
VP = 88
HG_G, POOL_S, CONV_B, LN_G, LN_B, LB = 64, 68, 72, 76, 80, 84

_layout = [("levels", LEVELS * P), ("ones", 1), ("neg_incl", P), ("neg_ones", 1), ("strict", P), ("reset", TP),
           ("blk", NSEQ), ("head", SBH), ("before", TQ), ("cnt", 4 * 16), ("eps", 1)]
COL = {}
_at = 0
for _n, _w in _layout:
    COL[_n] = (_at, _at + _w)
    _at += _w
NCONST = _at
COL["ident"] = (0, P)


def constants():
    c = np.zeros((P, NCONST), np.float32)
    r, q = np.arange(P)[:, None], np.arange(P)[None, :]

    def put(name, v):
        c[:, COL[name][0]:COL[name][1]] = v
    put("ones", 1.0)
    put("neg_incl", -8.0 * (r >= q))
    put("neg_ones", -8.0)
    put("strict", r < q)
    lv = [r == q]
    for n in range(1, LEVELS):
        h = 2 ** (n - 1)
        lv.append((r // (2 * h) == q // (2 * h)) & ((r & h) == 0) & ((q & h) != 0))
    put("levels", np.concatenate(lv, 1))
    reset = np.ones(TP, np.float32)
    reset[0:SEQ:CH] = 0
    reset[SEQ:T:TQ] = 0
    put("reset", reset[None])
    put("blk", (np.arange(P)[:, None] // TQ) == np.arange(NSEQ)[None, :])
    put("cnt", np.concatenate([w / np.minimum(w, np.arange(16) + 1.0) for w in WINDOWS])[None])
    put("eps", EPS)
    put("head", (r % (SBH * TQ)) // TQ == np.arange(SBH)[None])
    put("before", np.arange(TQ)[None] < r % TQ)
    return c


def open_split(nc, es, core, tag):
    core.XH = es.enter_context(nc.sbuf_tensor(f"{tag}_x_hi", [P, KT, TP], F32R))
    core.XL = es.enter_context(nc.sbuf_tensor(f"{tag}_x_lo", [P, KT, TP], F32R))


class Core:
    pass


def cols(core, name, a=0, b=None):
    lo, hi = COL[name]
    return core.const[:, lo + a:hi if b is None else lo + b]


def scope(nc, es, tag):
    sems = []

    def close():
        nc.clear_and_free_semaphores(sems)
        nc.all_engine_barrier()
    es.callback(close)

    def sb(name, shape, dtype=F32):
        return es.enter_context(nc.sbuf_tensor(f"{tag}_{name}", shape, dtype))

    def sem(name):
        sems.append(nc.alloc_semaphore(name=f"{tag}_{name}"))
        return sems[-1]
    return sb, sem


def chunked(ap):
    return ap.rearrange("p (c n) -> p c n", c=NC3)


def seg_bcast(ap):
    return ap.unsqueeze(2).to_broadcast([P, NSEQ, TQ])


def column_sums(pe, core, bank, n, sq, first):
    for b in range(NBK):
        q = pe.matmul(core.PS[0:TB, bank, n * NBK + b:n * NBK + b + 1], sq[:, b * TB:(b + 1) * TB], cols(core, "ones"),
                      start=(first and b == 0), stop=True, skip_group_check=True)
    return q


def spread(pe, core, bank, r):
    for b in range(NBK):
        q = pe.matmul(core.PS[:, bank + b // 4, (b % 4) * TB:(b % 4 + 1) * TB], r[:, b:b + 1].to_broadcast([TB, P]),
                      cols(core, "ident")[0:TB, 0:TB], start=True, stop=True)
    return q


def samples(ap):
    return ap[:, SEQ:T].rearrange("p (s t) -> p s t", s=NSEQ)


class AdaPart:
    UNITS = 4

    def __init__(self, core, sb, sem, chunks, rows_bank, turned_bank, ring=2):
        self.core, self.chunks, self.ring = core, chunks, ring
        self.bank, self.turned = rows_bank, turned_bank
        self.wa = sb("ada_w", [P, ring, 2, 4 * P])
        self.rows = sb("mod_rows", [SEG, 4 * P])
        self.w_in = [sem(f"ada_w_in{i}") for i in range(ring)]
        self.mm, self.rows_out, self.rows_T, self.step = sem("mod_mm"), sem("mod_rows_out"), sem("mod_turned"), sem("mod_step")
        self.units = self.UNITS * len(chunks)

    def load(self, eng):
        for n in range(self.units):
            l, c = self.chunks[n // 4]
            q = n % 4
            if n >= self.ring:
                eng.wait_ge(self.mm, n - self.ring + 1)
            eng.dma_start(self.wa[:, n % self.ring], self.core.ada_w[l].rearrange("(k p) f -> p k f", p=P)
                          [:, 2 * q:2 * q + 2, c * 4 * P:(c + 1) * 4 * P]).then_inc(self.w_in[n % self.ring], 16)

    def product(self, pe, n):
        c, q = divmod(n, 4)
        if q == 0 and c > 0:
            self.turn(pe, c - 1)
        pe.wait_ge(self.w_in[n % self.ring], 16 * (n // self.ring + 1))
        for i in range(2):
            m = pe.matmul(self.core.PS[0:SEG, self.bank, :], self.core.cT[:, 2 * q + i, 0:SEG], self.wa[:, n % self.ring, i],
                          start=(q == 0 and i == 0), stop=(q == 3 and i == 1))
        m.then_inc(self.mm, 1)

    def turn(self, pe, c):
        pe.wait_ge(self.rows_out, c + 1)
        for f in range(4):
            at = (4 * c + f) * SEGP
            m = pe.transpose(self.core.PS[:, self.turned, at:at + SEG], self.rows[:, f * P:(f + 1) * P],
                             cols(self.core, "ident")[0:SEG, 0:SEG])
        m.then_inc(self.rows_T, 1)

    def copy(self, act, c):
        act.wait_ge(self.mm, 4 * (c + 1))
        if c > 0:
            act.wait_ge(self.rows_T, c)
        act.activation(self.rows[:, :], self.core.PS[0:SEG, self.bank, :], ACT.Copy).then_inc(self.rows_out, 1)

    def products(self, pe):
        for n in range(self.units):
            self.product(pe, n)
        self.turn(pe, len(self.chunks) - 1)

    def copies(self, act):
        for c in range(len(self.chunks)):
            self.copy(act, c)

    def finish(self, dve):
        core = self.core
        dve.wait_ge(self.rows_T, len(self.chunks))
        n = 0
        for i, (l, c) in enumerate(self.chunks):
            mod = core.mod[:, l, c * 4 * SEGP:(c + 1) * 4 * SEGP].rearrange("p (f c) -> p f c", c=SEGP)[:, :, 0:SEG]
            bias = core.ada_bT[:, 48 * l + 4 * c:48 * l + 4 * c + 4].unsqueeze(2).to_broadcast([P, 4, SEG])
            sums = core.PS[:, self.turned, 4 * i * SEGP:4 * (i + 1) * SEGP].rearrange("p (f c) -> p f c", c=SEGP)[:, :, 0:SEG]
            dve.tensor_tensor(mod, sums, bias, ALU.add).then_inc(self.step, 1)
            n += 1
        for l, c in self.chunks:
            for g, (m_at, plus) in enumerate(((1, 1.0), (2, 0.0), (4, 1.0), (5, 0.0))):
                if c != 2 * m_at:
                    continue
                ng = core.vec[:, (l * 4 + g) * KT:(l * 4 + g + 1) * KT].unsqueeze(2).to_broadcast([P, KT, SEG])
                dst = core.coef[:, l, g].rearrange("p (k c) -> p k c", c=SEGP)[:, :, 0:SEG]
                mod = core.mod[:, l, :].rearrange("p (f c) -> p f c", c=SEGP)[:, m_at * KT:(m_at + 1) * KT, 0:SEG]
                dve.wait_ge(self.step, n)
                dve.tensor_scalar(dst, mod, plus, None, ALU.add).then_inc(self.step, 1)
                dve.wait_ge(self.step, n + 1)
                dve.tensor_tensor(dst, dst, ng, ALU.mult).then_inc(self.step, 1)
                n += 2


def setup(nc, core, tag, X):
    with ExitStack() as es:
        sb, sem = scope(nc, es, tag)
        rows_ada = sb("rows_ada", [96, P])
        rows_vec = sb("rows_vec", [VP, P])
        rows_conv = sb("rows_conv", [CWID * HT, P])
        rows_c = sb("rows_c", [SEG, D])
        xt = sb("xt", [P, 4, D])
        ada = AdaPart(core, sb, sem, [(0, c) for c in range(4)], 6, 7, ring=6)
        s_const, s_rows, s_crow, s_c, s_par, s_silu, s_xT, s_xev = (sem(n) for n in (
            "const_in", "rows_in", "c_in", "c_T", "params_T", "silu_out", "x_T", "x_out"))
        s_copy = sem("params_out")
        s_xt = [sem(f"xt_in{i}") for i in range(4)]
        PS = core.PS
        block = es.enter_context(nc.Block())

        @block.sync
        def _(sp):
            sp.dma_start(core.const[:, 0:P], core.const_in[:, 0:P]).then_inc(s_const, 16)
            sp.dma_start(rows_c[0:1, :], core.c_prompt).then_inc(s_crow, 16)
            sp.dma_start(rows_c[1:SEG, :], core.c_sample).then_inc(s_crow, 16)
            for i in range(9):
                if i >= 4:
                    sp.wait_ge(s_xT, i - 3)
                if i < 8:
                    sp.dma_start(xt[:, i % 4, :], core.x_prompt[0, i * P:(i + 1) * P, :]).then_inc(s_xt[i % 4], 16)
                else:
                    sp.dma_start(xt[0:NS, 0, :], core.x_sample.rearrange("b t d -> (b t) d")).then_inc(s_xt[0], 16)
            ada.load(sp)

        @block.scalar
        def _(act):
            act.dma_start(rows_ada[:, :], core.ada_b.rearrange("l (f p) -> (l f) p", p=P)).then_inc(s_rows, 16)
            act.dma_start(rows_vec[0:64, :], core.norm_g.rearrange("l n (f p) -> (l n f) p", p=P)).then_inc(s_rows, 16)
            for at, src in ((HG_G, core.hgrn_norm_g.rearrange("e h p -> (e h) p")),
                            (POOL_S, core.pool_scale.rearrange("o (f p) -> (o f) p", p=P)),
                            (CONV_B, core.conv_b.rearrange("o (f p) -> (o f) p", p=P)),
                            (LN_G, core.conv_ln_g.rearrange("o (f p) -> (o f) p", p=P)),
                            (LN_B, core.conv_ln_b.rearrange("o (f p) -> (o f) p", p=P)),
                            (LB, core.hgrn_lb_logits.rearrange("e (f p) -> (e f) p", p=P))):
                act.dma_start(rows_vec[at:at + 4, :], src).then_inc(s_rows, 16)
            act.dma_start(rows_conv[:, :], core.conv_w.rearrange("o w (f p) -> (o w f) p", p=P)).then_inc(s_rows, 16)
            act.dma_start(core.sb_bias_bc[:, :], core.sb_bias[0:1, :].to_broadcast([P, SBH])).then_inc(s_rows, 16)
            act.dma_start(core.const[:, P:], core.const_in[:, P:]).then_inc(s_rows, 16)
            act.wait_ge(s_c, 1)
            act.activation(core.cT[:, :, 0:SEG], PS[:, 0, 0:KT * 16].rearrange("p (k c) -> p k c", k=KT)[:, :, 0:SEG],
                           ACT.Silu).then_inc(s_silu, 1)
            ada.copies(act)

        @block.tensor
        def _(pe):
            pe.wait_ge(s_const, 16)
            pe.wait_ge(s_crow, 32)
            ident = cols(core, "ident")
            for k in range(KT):
                m = pe.transpose(PS[:, 0, 16 * k:16 * k + SEG], rows_c[:, k * P:(k + 1) * P], ident[0:SEG, 0:SEG])
            m.then_inc(s_c, 1)
            for i in range(9):
                pe.wait_ge(s_xt[i % 4], 16 * (i // 4 + 1))
                if i >= 2:
                    pe.wait_ge(s_xev, i - 1)
                n = P if i < 8 else NS
                for k in range(KT):
                    m = pe.transpose(PS[:, 2 + 2 * (i % 2) + k // 4, (k % 4) * P:(k % 4) * P + n],
                                     xt[0:n, i % 4, k * P:(k + 1) * P], ident[0:n, 0:n])
                m.then_inc(s_xT, 1)
            pe.wait_ge(s_rows, 16 * 11)
            pe.transpose(PS[:, 1, 0:96], rows_ada[:, :], ident[0:96, 0:96])
            pe.transpose(PS[:, 1, 96:96 + VP], rows_vec[:, :], ident[0:VP, 0:VP])
            pe.transpose(PS[:, 1, 256:256 + CWID * HT], rows_conv[:, :], ident[0:CWID * HT, 0:CWID * HT]).then_inc(s_par, 1)
            pe.wait_ge(s_silu, 1)
            ada.products(pe)

        @block.vector
        def _(dve):
            for k in range(KT):
                dve.memset(X[:, k, T:TP], 0.0)
            for i in range(9):
                dve.wait_ge(s_xT, i + 1)
                n = P if i < 8 else NS
                b = 2 + 2 * (i % 2)
                for h in range(2):
                    m = dve.tensor_copy(X[:, 4 * h:4 * h + 4, i * P:i * P + n],
                                        PS[:, b + h, :].rearrange("p (k t) -> p k t", k=4)[:, :, 0:n])
                m.then_inc(s_xev, 1)
            dve.wait_ge(s_par, 1)
            dve.tensor_copy(core.ada_bT[:, :], PS[:, 1, 0:96])
            dve.tensor_copy(core.vec[:, :], PS[:, 1, 96:96 + VP])
            dve.tensor_copy(core.convw[:, :], PS[:, 1, 256:256 + CWID * HT]).then_inc(s_copy, 1)
            dve.wait_ge(s_copy, 1)
            ada.finish(dve)


def residual_norm(nc, core, tag, X, load, m, gate, scale, shift, store, final=False):
    with ExitStack() as es:
        sb, sem = scope(nc, es, tag)
        sq = sb("sq", [P, 2, TP])
        total = sb("total", [P, TP])
        rt = sb("rt", [TB, 2, NBK])
        rstd = sb("rstd", [TB, 2, NBK])
        y = sb("y", [P, 2, TP])
        y2 = sb("y2", [P, 3, TP])
        PS = core.PS
        s_x, s_store, s_sq, s_ss, s_rt, s_rs = (sem(n) for n in ("x_in", "x_stored", "sq_out", "sumsq", "root", "rstd"))
        s_bc, s_sum = sem("rstd_spread"), [sem(f"squares{n}_added") for n in range(2)]
        s_y, s_res, s_y2p, s_y2s, s_hi, s_pad, s_ys = (sem(n) for n in (
            "y_out", "x_new", "y2_prompt", "y2_samples", "hi_out", "pads", "y_small"))
        s_lo = [sem(f"lo_out{i}") for i in range(3)]
        norms = ([m] if m is not None else []) + ([] if final else [X])
        two = m is not None
        coef = lambda i: core.coef[:, i[0], i[1]].rearrange("p (k c) -> p k c", c=SEGP)
        block = es.enter_context(nc.Block())

        @block.sync
        def _(sp):
            if load:
                sp.dma_start(X[:, :, :], core.x_dram.rearrange("p (k t) -> p k t", k=KT)).then_inc(s_x, 16)
            if store:
                if two:
                    sp.wait_ge(s_res, KT)
                sp.dma_start(core.x_dram.rearrange("p (k t) -> p k t", k=KT), X[:, :, :]).then_inc(s_store, 16)
                sp.wait_ge(s_store, 16)

        @block.scalar
        def _(act):
            for n, src in enumerate(norms):
                for k in range(KT):
                    i = n * KT + k
                    if src is X and two:
                        act.wait_ge(s_res, k + 1)
                    if k >= 3:
                        act.wait_ge(s_sum[n], k - 2)
                    if k == 0 and n:
                        act.wait_ge(s_ss, n)
                    act.activation(sq[:, i % 2, :] if k else total[:, :], src[:, k, :], ACT.Square).then_inc(s_sq, 1)
                act.wait_ge(s_ss, n + 1)
                act.activation(rt[:, n, :], PS[0:TB, 6 + n, 0:NBK], ACT.Sqrt, scale=1.0 / D,
                               bias=cols(core, "eps")[0:TB, :]).then_inc(s_rt, 1)
            if final:
                return
            for k in range(KT + 1):
                if k < KT:
                    i = (KT if two else 0) + k
                    act.wait_ge(s_y, i + 1)
                    if k >= 3:
                        act.wait_ge(s_lo[k % 3], k // 3)
                    act.activation(y2[:, k % 3, 0:SEQ], y[:, i % 2, 0:SEQ], ACT.Identity,
                                   scale=coef(scale)[:, k, 0:1],
                                   bias=core.mod[:, shift[0], (shift[1] + k) * SEGP:(shift[1] + k) * SEGP + 1]).then_inc(s_y2p, 1)
                if k >= 1:
                    act.wait_ge(s_y2p, k)
                    act.wait_ge(s_y2s, k)
                    act.activation(core.XH[:, k - 1, :], y2[:, (k - 1) % 3, :], ACT.Copy).then_inc(s_hi, 1)

        @block.tensor
        def _(pe):
            for n in range(len(norms)):
                pe.wait_ge(s_sum[n], KT - 1)
                column_sums(pe, core, 6 + n, 0, total, True).then_inc(s_ss, 1)
                pe.wait_ge(s_rs, n + 1)
                spread(pe, core, 3 * n, rstd[:, n, :]).then_inc(s_bc, 1)

        def add_squares(eng, n):
            for k in range(1, KT):
                i = n * KT + k
                eng.wait_ge(s_sq, i + 1)
                if k >= 2:
                    eng.wait_ge(s_sum[n], k - 1)
                eng.tensor_tensor(total[:, :], total[:, :], sq[:, i % 2, :], ALU.add).then_inc(s_sum[n], 1)

        def low(eng, k):
            eng.wait_ge(s_hi, k + 1)
            eng.tensor_tensor(core.XL[:, k, :], y2[:, k % 3, :], core.XH[:, k, :].bitcast(F32),
                              ALU.subtract).then_inc(s_lo[k % 3], 1)

        @block.vector
        def _(dve):
            if not final:
                dve.memset(y2[:, 0, T:TP], 0.0)
                dve.memset(y2[:, 1, T:TP], 0.0)
                dve.memset(y2[:, 2, T:TP], 0.0).then_inc(s_pad, 1)
            small = 0
            add_squares(dve, 0)
            if two:
                if load:
                    dve.wait_ge(s_x, 16)
                dve.wait_ge(s_rt, 1)
                dve.reciprocal(rstd[:, 0, :], rt[:, 0, :]).then_inc(s_rs, 1)
                dve.wait_ge(s_bc, 1)
                for k in range(KT):
                    dve.tensor_tensor(chunked(y[:, k % 2, :]), chunked(m[:, k, :]), PS[:, 0:NC3, 0:CW],
                                      ALU.mult).then_inc(s_y, 1)
                    dve.wait_ge(s_y, k + 1)
                    dve.scalar_tensor_tensor(out=X[:, k, 0:SEQ], in0=y[:, k % 2, 0:SEQ], scalar=coef(gate)[:, k, 0:1],
                                             in1=X[:, k, 0:SEQ], op0=ALU.mult, op1=ALU.add)
                    dve.tensor_tensor(samples(y[:, k % 2, :]), samples(y[:, k % 2, :]),
                                      seg_bcast(coef(gate)[:, k, 1:SEG]), ALU.mult).then_inc(s_ys, 1)
                    small += 1
                    dve.wait_ge(s_ys, small)
                    dve.tensor_tensor(X[:, k, SEQ:T], X[:, k, SEQ:T], y[:, k % 2, SEQ:T], ALU.add).then_inc(s_res, 1)
            if final:
                return
            n = len(norms) - 1
            dve.wait_ge(s_rt, n + 1)
            dve.reciprocal(rstd[:, n, :], rt[:, n, :]).then_inc(s_rs, 1)
            dve.wait_ge(s_bc, n + 1)
            for k in range(KT):
                i = (KT if two else 0) + k
                if k >= 2:
                    dve.wait_ge(s_y2p, k - 1)
                dve.tensor_tensor(chunked(y[:, i % 2, :]), chunked(X[:, k, :]), PS[:, 3 * n:3 * n + NC3, 0:CW],
                                  ALU.mult).then_inc(s_y, 1)
                dve.wait_ge(s_y, i + 1)
                dve.tensor_tensor(samples(y[:, i % 2, :]), samples(y[:, i % 2, :]),
                                  seg_bcast(coef(scale)[:, k, 1:SEG]), ALU.mult).then_inc(s_ys, 1)
                small += 1
                dve.wait_ge(s_ys, small)
                if k >= 3:
                    dve.wait_ge(s_lo[k % 3], k // 3)
                sh = core.mod[:, shift[0], :].rearrange("p (f c) -> p f c", c=SEGP)[:, shift[1] + k, 1:SEG]
                dve.tensor_tensor(samples(y2[:, k % 3, :]), samples(y[:, i % 2, :]), seg_bcast(sh),
                                  ALU.add).then_inc(s_y2s, 1)
                if k >= 4 and k % 3 == 1:
                    low(dve, k - 2)

        @block.gpsimd
        def _(pool):
            if final:
                return
            if two:
                add_squares(pool, 1)
            pool.wait_ge(s_pad, 1)
            for k in range(KT):
                if k % 3 != 2:
                    low(pool, k)


def product(pe, out, hi, lo, xh, xl, first, last):
    pe.matmul(out, hi, xh, start=first, stop=False)
    pe.matmul(out, hi, xl, start=False, stop=False)
    return pe.matmul(out, lo, xh, start=False, stop=last)


def dense(nc, core, tag, w, jobs, src=None):
    with ExitStack() as es:
        sb, sem = scope(nc, es, tag)
        raw = sb("w_raw", [P, 2, KT, P])
        wh = sb("w_hi", [P, 2, KT, P], F32R)
        wl = sb("w_lo", [P, 2, KT, P], F32R)
        s_raw = [sem(f"w_in{i}") for i in range(2)]
        s_hi, s_lo, s_mm, s_ev = (sem(n) for n in ("w_hi_out", "w_lo_out", "mm_done", "out_copied"))
        s_xhi, s_xlo = sem("x_hi_out"), sem("x_lo_out")
        w_v = w.rearrange("(k p) f -> p k f", p=P)
        PS = core.PS
        base = []
        n = 0
        for _, tiles, _ in jobs:
            base.append(n)
            n += tiles
        block = es.enter_context(nc.Block())

        @block.sync
        def _(sp):
            for (c0, tiles, _), b in zip(jobs, base):
                with sp.Fori(0, tiles // 2) as j:
                    for s in range(2):
                        sp.wait_ge(s_lo, j * 2 + (b + s + 1))
                        sp.dma_start(raw[:, s, :, :], w_v[:, :, bass.ds(j * (2 * P) + (s * P + c0), P)]).then_inc(s_raw[s], 16)

        @block.scalar
        def _(act):
            for k in range(KT if src is not None else 0):
                act.activation(core.XH[:, k, :], src[:, k, :], ACT.Copy).then_inc(s_xhi, 1)
            for (_, tiles, _), b in zip(jobs, base):
                with act.Fori(0, tiles // 2) as j:
                    for s in range(2):
                        act.wait_ge(s_raw[s], j * 16 + 16 * (b // 2 + 1))
                        act.wait_ge(s_mm, j * 2 + (b + s + 1))
                        act.activation(wh[:, s, :, :], raw[:, s, :, :], ACT.Copy).then_inc(s_hi, 1)

        @block.gpsimd
        def _(pool):
            pool.sem_inc(s_lo, 2)
            for (_, tiles, _), b in zip(jobs, base):
                with pool.Fori(0, tiles // 2) as j:
                    for s in range(2):
                        pool.wait_ge(s_hi, j * 2 + (b + s + 1))
                        pool.tensor_tensor(wl[:, s, :, :], raw[:, s, :, :], wh[:, s, :, :].bitcast(F32),
                                           ALU.subtract).then_inc(s_lo, 1)

        @block.tensor
        def _(pe):
            pe.sem_inc(s_mm, 2)
            if src is not None:
                pe.wait_ge(s_xlo, KT)
            for (_, tiles, _), b in zip(jobs, base):
                with pe.Fori(0, tiles // 2) as j:
                    for s in range(2):
                        pe.wait_ge(s_lo, j * 2 + (b + s + 3))
                        pe.wait_ge(s_ev, j * 2 + (b + s + 1))
                        for k in range(KT):
                            for c in range(NC3):
                                q = product(pe, PS[:, 3 * s + c, 0:CW], wh[:, s, k, :], wl[:, s, k, :],
                                            core.XH[:, k, c * CW:(c + 1) * CW], core.XL[:, k, c * CW:(c + 1) * CW],
                                            k == 0, k == KT - 1)
                        q.then_inc(s_mm, 1)

        @block.vector
        def _(dve):
            dve.sem_inc(s_ev, 2)
            for k in range(KT if src is not None else 0):
                dve.wait_ge(s_xhi, k + 1)
                dve.tensor_tensor(core.XL[:, k, :], src[:, k, :], core.XH[:, k, :].bitcast(F32), ALU.subtract)\
                   .then_inc(s_xlo, 1)
            for (_, tiles, dst), b in zip(jobs, base):
                with dve.Fori(0, tiles // 2) as j:
                    for s in range(2):
                        dve.wait_ge(s_mm, j * 2 + (b + s + 3))
                        o = dst[:, bass.ds(j * 2 + s, 1), :].rearrange("p a (c n) -> p (a c) n", c=NC3)
                        dve.tensor_copy(o, PS[:, 3 * s:3 * s + 3, 0:CW]).then_inc(s_ev, 1)


def mlp(nc, core, tag, w1, w2, M):
    G = FF // (4 * P)
    SETS = 12
    with ExitStack() as es:
        sb, sem = scope(nc, es, tag)
        raw = sb("w_raw", [P, 2, 8 * P])
        wh = sb("w_hi", [P, 2, 8 * P], F32R)
        wl = sb("w_lo", [P, 2, 8 * P], F32R)
        HH = sb("h_hi", [P, 4, TP], F32R)
        HL = sb("h_lo", [P, 4, TP], F32R)
        r = sb("relu", [P, 2, TP])
        s_raw = [sem(f"w_in{i}") for i in range(2)]
        s_hi, s_lo, s_mm, s_ev = (sem(n) for n in ("w_hi_out", "w_lo_out", "mm_done", "out_copied"))
        s_r, s_hh, s_sq, s_h, s_m0 = (sem(n) for n in ("relu_out", "h_hi_out", "sq_out", "h_lo_out", "m_zero"))
        w1_v = w1.rearrange("(k p) f -> p k f", p=P)
        w2_v = w2.rearrange("(g k p) f -> p g k f", p=P, k=4)
        PS = core.PS
        block = es.enter_context(nc.Block())
        released = [1, 2, 3, 4, 6, 8, 10, 12]

        @block.sync
        def _(sp):
            with sp.Fori(0, G) as g:
                for u in range(8):
                    sp.wait_ge(s_lo, g * 8 + (u + 1))
                    if u < 4:
                        sp.dma_start(raw[:, u % 2, :].rearrange("p (k f) -> p k f", k=8),
                                     w1_v[:, :, bass.ds(g * (4 * P) + u * P, P)]).then_inc(s_raw[u % 2], 16)
                    else:
                        sp.dma_start(raw[:, u % 2, :].rearrange("p (k f) -> p k f", k=4),
                                     w2_v[:, bass.ds(g, 1), :, (u - 4) * 2 * P:(u - 3) * 2 * P]
                                     .rearrange("p a k f -> p (a k) f")).then_inc(s_raw[u % 2], 16)

        @block.scalar
        def _(act):
            def weights(g, u):
                act.wait_ge(s_raw[u % 2], g * 64 + 16 * (u // 2 + 1))
                act.wait_ge(s_mm, g * SETS + (released[u - 2] + (SETS if u >= 2 else 0)))
                act.activation(wh[:, u % 2, :], raw[:, u % 2, :], ACT.Copy).then_inc(s_hi, 1)

            def hidden(g, i):
                act.wait_ge(s_mm, g * SETS + (SETS + i + 1))
                if i >= 2:
                    act.wait_ge(s_h, g * 4 + (i - 1))
                act.activation(chunked(r[:, i % 2, :]), PS[:, 3 * (i % 2):3 * (i % 2) + 3, 0:CW],
                               ACT.Relu).then_inc(s_r, 1)
                act.wait_ge(s_r, g * 4 + (i + 1))
                act.activation(HH[:, i, :], r[:, i % 2, :], ACT.Square).then_inc(s_hh, 1)

            with act.Fori(0, G) as g:
                for u in range(8):
                    weights(g, u)
                    if u in (1, 2, 3, 4):
                        hidden(g, u - 1)

        @block.gpsimd
        def _(pool):
            pool.sem_inc(s_lo, 2)
            with pool.Fori(0, G) as g:
                for u in range(8):
                    pool.wait_ge(s_hi, g * 8 + (u + 1))
                    pool.tensor_tensor(wl[:, u % 2, :], raw[:, u % 2, :], wh[:, u % 2, :].bitcast(F32),
                                       ALU.subtract).then_inc(s_lo, 1)

        @block.tensor
        def _(pe):
            pe.sem_inc(s_mm, SETS)
            with pe.Fori(0, G) as g:
                for i in range(4):
                    pe.wait_ge(s_lo, g * 8 + (i + 3))
                    if i < 2:
                        pe.wait_ge(s_ev, g * 8 + (i + 1))
                    else:
                        pe.wait_ge(s_r, g * 4 + (i - 1))
                    for k in range(KT):
                        for c in range(NC3):
                            q = product(pe, PS[:, 3 * (i % 2) + c, 0:CW], wh[:, i % 2, k * P:(k + 1) * P],
                                        wl[:, i % 2, k * P:(k + 1) * P],
                                        core.XH[:, k, c * CW:(c + 1) * CW], core.XL[:, k, c * CW:(c + 1) * CW],
                                        k == 0, k == KT - 1)
                    q.then_inc(s_mm, 1)
                for f in range(8):
                    u = 4 + f // 2
                    pe.wait_ge(s_lo, g * 8 + (u + 3))
                    if f < 2:
                        pe.wait_ge(s_r, g * 4 + (f + 3))
                    else:
                        pe.wait_ge(s_ev, g * 8 + (f + 1))
                    for k in range(4):
                        if f == 0:
                            pe.wait_ge(s_h, g * 4 + (k + 1))
                        at = k * 2 * P + (f % 2) * P
                        for c in range(NC3):
                            q = product(pe, PS[:, 3 * (f % 2) + c, 0:CW], wh[:, u % 2, at:at + P],
                                        wl[:, u % 2, at:at + P],
                                        HH[:, k, c * CW:(c + 1) * CW], HL[:, k, c * CW:(c + 1) * CW],
                                        k == 0, k == 3)
                    q.then_inc(s_mm, 1)

        @block.vector
        def _(dve):
            dve.sem_inc(s_ev, 2)
            dve.memset(M[:, :, :], 0.0).then_inc(s_m0, 1)
            dve.wait_ge(s_m0, 1)
            with dve.Fori(0, G) as g:
                for i in range(4):
                    dve.wait_ge(s_hh, g * 4 + (i + 1))
                    dve.tensor_tensor(r[:, i % 2, :], r[:, i % 2, :], r[:, i % 2, :], ALU.mult).then_inc(s_sq, 1)
                    dve.wait_ge(s_sq, g * 4 + (i + 1))
                    dve.tensor_tensor(HL[:, i, :], r[:, i % 2, :], HH[:, i, :].bitcast(F32), ALU.subtract).then_inc(s_h, 1)
                for f in range(8):
                    dve.wait_ge(s_mm, g * SETS + (SETS + 4 + f + 1))
                    dve.tensor_tensor(chunked(M[:, f, :]), chunked(M[:, f, :]),
                                      PS[:, 3 * (f % 2):3 * (f % 2) + 3, 0:CW], ALU.add).then_inc(s_ev, 1)


def sb_prompt(nc, core, tag, KV, VT, spare):
    tiles = []
    for h in range(SBH):
        for g in range(2):
            for kt in range(4 * g + 3, -1, -1):
                tiles.append((h, g, kt, max(0, kt - 4 * g) * P))
    NT = len(tiles)
    LACC, LOUT = 3, 5
    first = lambda n: tiles[n][2] == 4 * tiles[n][1] + 3
    diag = lambda n: tiles[n][2] >= 4 * tiles[n][1]
    run = lambda n: sum(first(i) for i in range(n + 1)) - 1
    last = lambda n: tiles[n][2] == 0
    with ExitStack() as es:
        sb, sem = scope(nc, es, tag)
        zb = sb("z", [P, 2, 512])
        a = sb("a", [P, 2, 512])
        e = sb("e", [P, 2, 512])
        sp_ = sb("softplus", [P, 4, 512])
        R = sb("later", [P, 4, 512])
        w = sb("w", [P, 3, 512])
        names = ("z_mm", "zb_out", "abs_out", "exp_out", "ln_out", "sp_out", "sp_masked", "later_out", "acc_mm",
                 "w_out", "w_masked", "o_mm", "o_out")
        s_z, s_zb, s_a, s_e, s_l, s_sp, s_spm, s_R, s_acc, s_w, s_wm, s_o, s_oc = (sem(n) for n in names)
        PS = core.PS
        NB = 6
        k_rows = spare[:, 0:4 * HALF].rearrange("p (i f) -> p i f", i=4)
        v_rows = spare[0:NS, 4 * HALF:5 * HALF]
        s_rT, s_rows = sem("rows_turned"), sem("rows_copied")
        s_out = [sem(f"rows_stored{i}") for i in range(5)]
        n_rows = lambda i: P if i < 8 else NS
        units = [(1, i) for i in range(9)] + [(0, i) for i in range(9)]
        block = es.enter_context(nc.Block())

        @block.sync
        def _(sp):
            sp.wait_ge(s_rows, 9)
            sp.dma_start(core.o_v_p.rearrange("e b (i p) h d -> p (e b i) (h d)", p=P), VT[:, 0:8, :]).then_inc(s_out[4], 16)
            sp.dma_start(core.o_v_s.rearrange("e b t h d -> (e b t) (h d)"), v_rows).then_inc(s_out[4], 16)
            kp = core.o_k_p.rearrange("e b (i p) h d -> (e b i) p (h d)", p=P)
            for i in range(9):
                sp.wait_ge(s_rows, 9 + i + 1)
                dst = kp[i] if i < 8 else core.o_k_s.rearrange("e b t h d -> (e b t) (h d)")
                sp.dma_start(dst, k_rows[0:n_rows(i), i % 4, :]).then_inc(s_out[i % 4], 16)
            for i in range(4):
                sp.wait_ge(s_out[i], 16 * (3 if i == 0 else 2))
            sp.wait_ge(s_out[4], 32)
        n_diag = lambda n: sum(diag(i) for i in range(n + 1))

        @block.tensor
        def _(pe):
            for u, (kv, i) in enumerate(units):
                if u >= 4:
                    pe.wait_ge(s_rows, u - 3)
                n = n_rows(i)
                for f in range(4):
                    q = pe.transpose(PS[0:n, u % 4, f * P:(f + 1) * P], KV[:, 4 * kv + f, i * P:i * P + n],
                                     cols(core, "ident"))
                q.then_inc(s_rT, 1)
            pe.wait_ge(s_rows, len(units))
            for t in range(NT + LOUT):
                if t < NT:
                    h, g, kt, c = tiles[t]
                    r = 64 * (h % 2)
                    if t >= NB:
                        pe.wait_ge(s_w, t - NB + 1)
                    pe.matmul(PS[:, t % NB, c:512], KV[r:r + 64, h // 2, kt * P:(kt + 1) * P],
                              core.M[r:r + 64, 4 + h // 2, g * 512 + c:(g + 1) * 512], start=True, stop=True)\
                      .then_inc(s_z, 1)
                n = t - LACC
                if 0 <= n < NT:
                    h, g, kt, c = tiles[n]
                    pe.wait_ge(s_sp, n + 1)
                    if diag(n):
                        pe.wait_ge(s_spm, n_diag(n))
                    pe.wait_ge(s_zb, n + 1)
                    q = pe.matmul(PS[:, n % NB, c:512], cols(core, "neg_incl"), sp_[:, n % 4, c:512],
                                  start=False, stop=first(n), skip_group_check=True)
                    if not first(n):
                        pe.wait_ge(s_R, n)
                        q = pe.matmul(PS[:, n % NB, c:512], cols(core, "neg_ones").to_broadcast([P, P]), R[:, n % 4, c:512],
                                      start=False, stop=True, skip_group_check=True)
                    q.then_inc(s_acc, 1)
                n = t - LOUT
                if 0 <= n < NT:
                    h, g, kt, c = tiles[n]
                    r = 64 * (h % 2)
                    pe.wait_ge(s_w, n + 1)
                    if diag(n):
                        pe.wait_ge(s_wm, n_diag(n))
                    if first(n) and run(n) >= 2:
                        pe.wait_ge(s_oc, run(n) - 1)
                    q = pe.matmul(PS[r:r + 64, 6 + run(n) % 2, c:512], VT[:, kt, h * 64:(h + 1) * 64],
                                  w[:, n % 3, c:512], start=first(n), stop=last(n), skip_group_check=True)
                    q.then_inc(s_o, 1)

        @block.scalar
        def _(act):
            act.preload_act_table_set("natural_log_exp_and_others")
            for t in range(NT + LACC):
                if t < NT:
                    h, g, kt, c = tiles[t]
                    act.wait_ge(s_zb, t + 1)
                    if t >= 2:
                        act.wait_ge(s_l, t - 1)
                    act.activation(a[:, t % 2, c:512], zb[:, t % 2, c:512], ACT.Abs).then_inc(s_a, 1)
                    act.wait_ge(s_a, t + 1)
                    act.activation(a[:, t % 2, c:512], a[:, t % 2, c:512], ACT.Exp, scale=-1.0).then_inc(s_e, 1)
                    act.wait_ge(s_e, t + 1)
                    if t >= 2:
                        act.wait_ge(s_sp, t - 1)
                    act.activation(e[:, t % 2, c:512], a[:, t % 2, c:512], ACT.Ln, bias=1.0).then_inc(s_l, 1)
                n = t - LACC
                if 0 <= n < NT:
                    h, g, kt, c = tiles[n]
                    act.wait_ge(s_acc, n + 1)
                    if n >= 3:
                        act.wait_ge(s_o, n - 2)
                    act.activation(w[:, n % 3, c:512], PS[:, n % NB, c:512], ACT.Exp, scale=0.125,
                                   bias=core.sb_bias_bc[:, h:h + 1]).then_inc(s_w, 1)

        @block.vector
        def _(dve):
            def scores(t):
                h, g, kt, c = tiles[t]
                dve.wait_ge(s_z, t + 1)
                if t >= 2:
                    dve.wait_ge(s_sp, t - 1)
                    dve.wait_ge(s_a, t - 1)
                dve.tensor_scalar(zb[:, t % 2, c:512], PS[:, t % NB, c:512], 0.125, core.sb_bias_bc[:, h:h + 1],
                                  ALU.mult, ALU.add).then_inc(s_zb, 1)

            def sums(t):
                h, g, kt, c = tiles[t]
                dve.wait_ge(s_zb, t + 1)
                dve.wait_ge(s_l, t + 1)
                if t >= 4:
                    dve.wait_ge(s_acc, t - 3)
                    dve.wait_ge(s_R, t - 3)
                dve.scalar_tensor_tensor(out=sp_[:, t % 4, c:512], in0=zb[:, t % 2, c:512], scalar=0.0,
                                         in1=e[:, t % 2, c:512], op0=ALU.max, op1=ALU.add).then_inc(s_sp, 1)
                dve.wait_ge(s_sp, t + 1)
                if diag(t):
                    dve.wait_ge(s_spm, n_diag(t))
                if t >= 3:
                    dve.wait_ge(s_acc, t - 2)
                if t >= 1:
                    dve.wait_ge(s_R, t)
                nx = (t + 1) % 4
                if c:
                    dve.memset(R[:, nx, 0:c], 0.0)
                if first(t):
                    dve.tensor_copy(R[:, nx, c:512], sp_[:, t % 4, c:512]).then_inc(s_R, 1)
                else:
                    dve.tensor_tensor(R[:, nx, c:512], R[:, t % 4, c:512], sp_[:, t % 4, c:512], ALU.add).then_inc(s_R, 1)

            for u, (kv, i) in enumerate(units):
                dve.wait_ge(s_rT, u + 1)
                if kv == 0 and i >= 4:
                    dve.wait_ge(s_out[i % 4], 16 * (i // 4))
                n = n_rows(i)
                dst = k_rows[0:n, i % 4, :] if kv == 0 else VT[:, i, :] if i < 8 else v_rows
                dve.tensor_copy(dst, PS[0:n, u % 4, :]).then_inc(s_rows, 1)
            for t in range(NT + LOUT + 1):
                if t < NT:
                    scores(t)
                if 1 <= t <= NT:
                    sums(t - 1)
                n = t - LOUT - 1
                if n >= 0 and last(n):
                    h, g = tiles[n][:2]
                    r = 64 * (h % 2)
                    dve.wait_ge(s_o, n + 1)
                    dve.tensor_copy(core.M[r:r + 64, 4 + h // 2, g * 512:(g + 1) * 512],
                                    PS[r:r + 64, 6 + run(n) % 2, :]).then_inc(s_oc, 1)

        @block.gpsimd
        def _(pool):
            for t in range(NT + LACC):
                if t < NT and diag(t):
                    c = tiles[t][3]
                    pool.wait_ge(s_sp, t + 1)
                    pool.tensor_tensor(sp_[:, t % 4, c:c + P], sp_[:, t % 4, c:c + P], cols(core, "strict"),
                                       ALU.mult).then_inc(s_spm, 1)
                n = t - LACC
                if 0 <= n < NT and diag(n):
                    c = tiles[n][3]
                    pool.wait_ge(s_w, n + 1)
                    pool.tensor_tensor(w[:, n % 3, c:c + P], w[:, n % 3, c:c + P], cols(core, "strict"),
                                       ALU.mult).then_inc(s_wm, 1)


def sb_sample(nc, core, tag, KV, spare_k, spare_v):
    W64 = SBH * TQ
    KRING, VRING = 4, 8
    NPAGES = NSEQ * NPG
    NG, NH = NSEQ // 2, NSEQ * 2
    with ExitStack() as es:
        sb, sem = scope(nc, es, tag)
        kp = spare_k[:, 0:KRING * HALF].rearrange("p (i f) -> p i f", i=KRING)
        kT = [spare_k[:, KRING * HALF:8 * HALF].rearrange("p (k t) -> p k t", k=4), sb("k_T", [P, 4, HALF])]
        new_w = spare_k[:, 8 * HALF:8 * HALF + NG * W64]
        vp = spare_v[:, 0:VRING * HALF].rearrange("p (i f) -> p i f", i=VRING)
        pages = sb("pages", [1, NPAGES], I32)
        qb = sb("q_blocks", [P, 4, NSEQ, W64])
        bias = sb("bias", [P, SBH])
        z = sb("z", [P, NPG * PAGE])
        a = sb("a", [P, NPG * PAGE])
        wT = sb("w_T", [P, NPG, P])
        v_new = sb("v_new", [NS, HALF])
        wnT = sb("w_new_T", [NS, NG * P])
        o = sb("o_rows", [P, HALF])
        zn, an, sn = (sb(f"{n}_new", [P, NG * TQ]) for n in "zas")
        (s_pt, s_q0, s_q, s_bias, s_zn, s_an, s_dn, s_wn, s_wnT, s_wnTc, s_vn, s_vnc) = (sem(n) for n in (
            "pages_in", "zeroed", "q_ready", "bias", "z_new_mm", "act_new", "dve_new", "w_new", "w_new_T", "w_new_T_out",
            "v_new_T", "v_new_out"))
        s_k = [sem(f"k_in{i}") for i in range(KRING)]
        s_v = [sem(f"v_in{i}") for i in range(VRING)]
        (s_T, s_kT, s_z, s_zb, s_a, s_e, s_l, s_sp, s_sp2, s_S, s_t, s_w, s_wT, s_wTc, s_o, s_og, s_oc, s_oT, s_ox) = (
            sem(n) for n in ("k_turned", "kT_out", "z_mm", "z_out", "abs_out", "exp_out", "ln_out", "softplus",
                             "softplus_new_added", "scan", "exponent", "w_out", "w_turned", "wT_out", "page_used",
                             "o_mm", "o_out", "o_turned", "o_placed"))
        PS = core.PS
        zbanks = lambda g: PS[:, 2 * (g % 2):2 * (g % 2) + 2, :].rearrange("p b c -> p (b c)")
        ident = cols(core, "ident")
        block = es.enter_context(nc.Block())

        @block.sync
        def _(sp):
            sp.dma_start(pages[:, :], core.page_table.rearrange("(a b) g -> a (b g)", a=1)).then_inc(s_pt, 16)
            sp.wait_ge(s_pt, 16)
            for i in range(NPAGES):
                page = sp.value_load(pages[0:1, i:i + 1], min_val=0, max_val=core.cache_k.shape[1] - 1)
                if i >= KRING:
                    sp.wait_ge(s_T, i - KRING + 1)
                sp.dma_start(kp[:, i % KRING, :], core.cache_k[0, bass.ds(page, 1)].rearrange("a p h d -> p (a h d)"))\
                  .then_inc(s_k[i % KRING], 16)

        @block.gpsimd
        def _(pool):
            pool.wait_ge(s_pt, 16)
            for i in range(NPAGES):
                page = pool.value_load(pages[0:1, i:i + 1], min_val=0, max_val=core.cache_k.shape[1] - 1)
                if i >= VRING:
                    pool.wait_ge(s_o, i - VRING + 1)
                pool.dma_start(vp[:, i % VRING, :], core.cache_v[0, bass.ds(page, 1)].rearrange("a p h d -> p (a h d)"))\
                    .then_inc(s_v[i % VRING], 16)

        @block.tensor
        def _(pe):
            def turn(i):
                pe.wait_ge(s_k[i % KRING], 16 * (i // KRING + 1))
                if i >= 2:
                    pe.wait_ge(s_kT, i - 1)
                for p in range(4):
                    q = pe.transpose(PS[:, 4 + i % 2, p * P:(p + 1) * P], kp[:, i % KRING, p * P:(p + 1) * P], ident)
                q.then_inc(s_T, 1)

            def scores(h):
                j, g = h // 2, h // 4
                pe.wait_ge(s_kT, 4 * h + 4)
                if h % 4 == 0 and g >= 2:
                    pe.wait_ge(s_wTc, g - 1)
                r = W64 * (j % 2)
                for p in range(4):
                    q = pe.matmul(PS[r:r + W64, 2 * (g % 2) + h % 2, :], qb[:, p, j, :], kT[h % 2][:, p, :],
                                  start=(p == 0), stop=(p == 3))
                q.then_inc(s_z, 1)

            def turn_weights(g):
                pe.wait_ge(s_w, g + 1)
                for i in range(NPG):
                    q = pe.transpose(PS[:, 2 * (g % 2) + i // 4, (i % 4) * P:(i % 4 + 1) * P], a[:, i * P:(i + 1) * P], ident)
                q.then_inc(s_wT, 1)

            def values(g, par):
                if par == 0:
                    pe.wait_ge(s_wTc, g + 1)
                    if g:
                        pe.wait_ge(s_oc, g)
                r = W64 * par
                for i in range(NPG):
                    n = (2 * g + par) * NPG + i
                    pe.wait_ge(s_v[n % VRING], 16 * (n // VRING + 1))
                    pe.matmul(PS[r:r + W64, 6, :], wT[:, i, r:r + W64], vp[:, n % VRING, :], start=(i == 0), stop=False)\
                      .then_inc(s_o, 1)
                q = pe.matmul(PS[r:r + W64, 6, :], wnT[:, g * P + r:g * P + r + W64], v_new[:, :], start=False, stop=True)
                if par == 1:
                    q.then_inc(s_og, 1)

            def turn_outputs(g):
                pe.wait_ge(s_oc, g + 1)
                if g:
                    pe.wait_ge(s_ox, g)
                for p in range(4):
                    q = pe.transpose(PS[:, 7, p * P:(p + 1) * P], o[:, p * P:(p + 1) * P], ident)
                q.then_inc(s_oT, 1)

            pe.wait_ge(s_q, 1)
            for j in range(NSEQ):
                r = W64 * (j % 2)
                for p in range(4):
                    q = pe.matmul(PS[r:r + W64, 7, (j // 2) * TQ:(j // 2 + 1) * TQ], qb[:, p, j, :],
                                  KV[:, p, SEQ + j * TQ:SEQ + (j + 1) * TQ], start=(p == 0), stop=(p == 3))
            q.then_inc(s_zn, 1)
            for p in range(4):
                q = pe.transpose(PS[0:NS, 6, p * P:(p + 1) * P], KV[:, 4 + p, SEQ:T], ident)
            q.then_inc(s_vn, 1)
            for h in range(NH + 4):
                g = h // 4 - 1
                for i in range(4):
                    if h < NH:
                        turn(4 * h + i)
                    if i == 0 and 1 <= h <= NH:
                        scores(h - 1)
                    if i == 0 and g >= 0:
                        if h % 4 == 2:
                            values(g, 0)
                        if h % 4 == 3:
                            turn_outputs(g)
                    if i == 2 and g >= 0 and h % 4 == 2:
                        values(g, 1)
                if h % 4 == 1 and g >= 0:
                    turn_weights(g)
                if h == 2:
                    pe.wait_ge(s_wn, 1)
                    pe.wait_ge(s_vnc, 1)
                    for k in range(NG):
                        q = pe.transpose(PS[0:NS, 7, k * P:(k + 1) * P], new_w[:, k * W64:(k + 1) * W64], ident)
                    q.then_inc(s_wnT, 1)
                    pe.wait_ge(s_wnTc, 1)

        @block.scalar
        def _(act):
            act.preload_act_table_set("natural_log_exp_and_others")
            act.wait_ge(s_dn, 1)
            act.activation(an[:, :], zn[:, :], ACT.Abs).then_inc(s_an, 1)
            act.wait_ge(s_an, 1)
            act.activation(an[:, :], an[:, :], ACT.Exp, scale=-1.0).then_inc(s_an, 1)
            act.wait_ge(s_an, 2)
            act.activation(an[:, :], an[:, :], ACT.Ln, bias=1.0).then_inc(s_an, 1)

            def soft(g):
                act.wait_ge(s_zb, g + 1)
                if g:
                    act.wait_ge(s_wT, g)
                act.activation(a[:, :], z[:, :], ACT.Abs).then_inc(s_a, 1)
                act.wait_ge(s_a, g + 1)
                act.activation(a[:, :], a[:, :], ACT.Exp, scale=-1.0).then_inc(s_e, 1)
                act.wait_ge(s_e, g + 1)
                act.activation(a[:, :], a[:, :], ACT.Ln, bias=1.0).then_inc(s_l, 1)

            for h in range(NH + 2):
                if h < NH:
                    for i in range(4 * h, 4 * h + 4):
                        act.wait_ge(s_T, i + 1)
                        if h >= 2:
                            act.wait_ge(s_z, h - 1)
                        act.activation(kT[h % 2][:, :, (i % 4) * P:(i % 4 + 1) * P],
                                       PS[:, 4 + i % 2, :].rearrange("p (k t) -> p k t", k=4), ACT.Copy).then_inc(s_kT, 1)
                if h == 0:
                    act.wait_ge(s_dn, 6)
                    act.activation(an[:, :], zn[:, :], ACT.Exp).then_inc(s_an, 1)
                if h >= 4 and h % 4 == 0:
                    soft(h // 4 - 1)
                if h >= 4 and h % 4 == 1:
                    act.wait_ge(s_t, h // 4)
                    act.activation(a[:, :], z[:, :], ACT.Exp).then_inc(s_w, 1)

        @block.vector
        def _(dve):
            dve.memset(qb[:, :, :, :], 0.0).then_inc(s_q0, 1)
            dve.wait_ge(s_q0, 1)
            for hh in range(2):
                r = 64 * hh
                for p in range(4):
                    at = (2 * p + hh) * TQ
                    q = dve.tensor_copy(qb[r:r + 64, p, :, at:at + TQ],
                                        core.M[r:r + 64, 4 + p, SEQ:T].rearrange("p (s t) -> p s t", s=NSEQ))
            q.then_inc(s_q, 1)
            dve.tensor_tensor(bias[:, :], core.sb_bias_bc[:, :], cols(core, "head"), ALU.mult).then_inc(s_bias, 1)
            dve.wait_ge(s_bias, 1)
            dve.tensor_tensor_scan(bias[:, :], cols(core, "ones").to_broadcast([P, SBH]), bias[:, :], 0.0, ALU.mult, ALU.add)\
               .then_inc(s_bias, 1)
            dve.wait_ge(s_bias, 2)
            b = bias[:, SBH - 1:SBH]
            by_group = lambda t: t.rearrange("p (g t) -> p g t", t=TQ)
            before = cols(core, "before").unsqueeze(1).to_broadcast([P, NG, TQ])
            dve.wait_ge(s_zn, 1)
            dve.tensor_scalar(zn[:, :], PS[:, 7, 0:NG * TQ], 0.125, b, ALU.mult, ALU.add).then_inc(s_dn, 1)
            dve.wait_ge(s_an, 3)
            dve.wait_ge(s_dn, 1)
            dve.scalar_tensor_tensor(out=sn[:, :], in0=zn[:, :], scalar=0.0, in1=an[:, :], op0=ALU.max, op1=ALU.add)\
               .then_inc(s_dn, 1)
            dve.wait_ge(s_dn, 2)
            dve.tensor_tensor(by_group(sn[:, :]), by_group(sn[:, :]), before, ALU.mult).then_inc(s_dn, 1)
            dve.wait_ge(s_dn, 3)
            dve.tensor_tensor_scan(an[:, ::-1], cols(core, "reset", SEQ, SEQ + NG * TQ), sn[:, ::-1], 0.0, ALU.mult, ALU.add)\
               .then_inc(s_dn, 1)
            dve.wait_ge(s_dn, 4)
            dve.tensor_copy(sn[:, :], an[:, :]).then_inc(s_dn, 1)
            dve.tensor_tensor(zn[:, :], zn[:, :], an[:, :], ALU.subtract).then_inc(s_dn, 1)
            dve.memset(new_w, 0.0).then_inc(s_dn, 1)
            dve.wait_ge(s_an, 4)
            dve.wait_ge(s_dn, 7)
            for j in range(NSEQ):
                r, g = W64 * (j % 2), j // 2
                q = dve.tensor_tensor(new_w[r:r + W64, g * W64 + j * TQ:g * W64 + (j + 1) * TQ],
                                      an[r:r + W64, g * TQ:(g + 1) * TQ], cols(core, "before")[r:r + W64, :], ALU.mult)
            q.then_inc(s_wn, 1)
            dve.wait_ge(s_vn, 1)
            dve.tensor_copy(v_new[:, :], PS[0:NS, 6, :]).then_inc(s_vnc, 1)
            dve.wait_ge(s_wnT, 1)
            dve.tensor_copy(wnT[:, :], PS[0:NS, 7, :]).then_inc(s_wnTc, 1)
            for g in range(NG):
                dve.wait_ge(s_z, 4 * g + 4)
                if g:
                    dve.wait_ge(s_w, g)
                dve.tensor_scalar(z[:, :], zbanks(g), 0.125, b, ALU.mult, ALU.add).then_inc(s_zb, 1)
                dve.wait_ge(s_zb, g + 1)
                dve.wait_ge(s_l, g + 1)
                dve.scalar_tensor_tensor(out=a[:, :], in0=z[:, :], scalar=0.0, in1=a[:, :], op0=ALU.max, op1=ALU.add)\
                   .then_inc(s_sp, 1)
                dve.wait_ge(s_sp, g + 1)
                e = NPG * PAGE - 1
                dve.tensor_tensor(a[:, e:e + 1], a[:, e:e + 1], sn[:, g * TQ:g * TQ + 1], ALU.add).then_inc(s_sp2, 1)
                dve.wait_ge(s_sp2, g + 1)
                dve.tensor_tensor_scan(zbanks(g)[:, ::-1], cols(core, "ones").to_broadcast([P, NPG * PAGE]), a[:, ::-1], 0.0,
                                       ALU.mult, ALU.add).then_inc(s_S, 1)
                dve.wait_ge(s_S, g + 1)
                dve.tensor_tensor(z[:, :], z[:, :], zbanks(g), ALU.subtract).then_inc(s_t, 1)
                dve.wait_ge(s_wT, g + 1)
                if g:
                    dve.wait_ge(s_og, g)
                dve.tensor_copy(wT[:, :, :].rearrange("p i r -> p (i r)"), zbanks(g)).then_inc(s_wTc, 1)
                dve.wait_ge(s_og, g + 1)
                if g:
                    dve.wait_ge(s_oT, g)
                dve.tensor_copy(o[:, :], PS[:, 6, :]).then_inc(s_oc, 1)
                dve.wait_ge(s_oT, g + 1)
                for hh in range(2):
                    r = 64 * hh
                    for p in range(4):
                        src = PS[r:r + 64, 7, p * P:(p + 1) * P].rearrange("p (s h q) -> p s h q", s=2, h=SBH)[:, :, 2 * p + hh, :]
                        at = SEQ + 2 * g * TQ
                        q = dve.tensor_copy(core.M[r:r + 64, 4 + p, at:at + 2 * TQ].rearrange("p (s q) -> p s q", s=2), src)
                q.then_inc(s_ox, 1)


def hgrn_prepare(nc, core, tag, B, QE, KK):
    with ExitStack() as es:
        sb, sem = scope(nc, es, tag)
        lb = sb("lower", [P, 5, HGH])
        ada = AdaPart(core, sb, sem, [(0, c) for c in range(4, 10)], 6, 7, ring=4)
        s_a, s_d, s_g = sem("act_step"), sem("dve_step"), sem("scan")
        F = core.BIG[:, 0:HGH, :]
        block = es.enter_context(nc.Block())

        @block.sync
        def _(sp):
            ada.load(sp)

        @block.tensor
        def _(pe):
            ada.products(pe)

        @block.scalar
        def _(act):
            act.activation(KK[:, :, :], F, ACT.Sigmoid, scale=-1.0).then_inc(s_a, 1)
            act.preload_act_table_set("natural_log_exp_and_others")
            act.activation(QE[:, :, :], F, ACT.Abs).then_inc(s_a, 1)
            act.wait_ge(s_a, 2)
            act.activation(QE[:, :, :], QE[:, :, :], ACT.Exp, scale=-1.0).then_inc(s_a, 1)
            act.wait_ge(s_a, 3)
            act.activation(QE[:, :, :], QE[:, :, :], ACT.Ln, bias=1.0).then_inc(s_a, 1)
            ada.copy(act, 0)
            ada.copy(act, 1)
            act.wait_ge(s_d, 1)
            act.activation(lb[:, 1, :], lb[:, 0, :], ACT.Exp).then_inc(s_a, 1)
            for h in range(HGH):
                act.wait_ge(s_g, h + 1)
                act.wait_ge(s_d, 3)
                act.activation(QE[:, h, :], B[:, h, :], ACT.Exp).then_inc(s_a, 1)
                ada.copy(act, 2 + h)
            act.wait_ge(s_d, 9)
            act.activation(F, F, ACT.Exp).then_inc(s_a, 1)

        @block.vector
        def _(dve):
            x = core.vec[:, LB:LB + HGH]
            dve.tensor_tensor(lb[:, 0, :], x, x, ALU.subtract).then_inc(s_d, 1)
            dve.wait_ge(s_a, 5)
            dve.reciprocal(lb[:, 2, :], lb[:, 1, :]).then_inc(s_d, 1)
            dve.scalar_tensor_tensor(out=F, in0=F, scalar=0.0, in1=QE[:, :, :], op0=ALU.min,
                                     op1=ALU.subtract).then_inc(s_d, 1)
            dve.wait_ge(s_d, 3)
            dve.tensor_tensor(lb[:, 3, :], lb[:, 1, :], lb[:, 2, :], ALU.mult).then_inc(s_d, 1)
            dve.wait_ge(s_d, 4)
            dve.tensor_tensor(lb[:, 4, :], lb[:, 3, :], lb[:, 3, :], ALU.subtract).then_inc(s_d, 1)
            dve.wait_ge(s_d, 5)
            dve.tensor_scalar(lb[:, 4, :], lb[:, 4, :], 0.0, None, ALU.max).then_inc(s_d, 1)
            dve.wait_ge(s_d, 6)
            dve.tensor_scalar(lb[:, 4, :], lb[:, 4, :], -1.0, 1.0, ALU.mult, ALU.add).then_inc(s_d, 1)
            dve.wait_ge(s_d, 7)
            for h in range(HGH):
                q = dve.tensor_scalar(KK[:, h, :], KK[:, h, :], lb[:, 4, h:h + 1], None, ALU.mult)
                dve.tensor_tensor_scan(B[:, h, :], cols(core, "reset"), F[:, h, :], 0.0, ALU.mult, ALU.add)\
                   .then_inc(s_g, 1)
            dve.wait_ge(s_g, HGH)
            ends = B[:, :, 0:SEQ].rearrange("p h (c t) -> p h c t", t=CH)[:, :, :, CH - 1:CH]
            for h in range(HGH):
                d = dve.tensor_tensor(F[:, h, 0:SEQ].rearrange("p (c t) -> p c t", t=CH),
                                      ends[:, h].to_broadcast([P, SEQ // CH, CH]),
                                      B[:, h, 0:SEQ].rearrange("p (c t) -> p c t", t=CH), ALU.subtract)
            d.then_inc(s_d, 1)
            for h in range(HGH):
                bs = samples(B[:, h, :])
                d = dve.tensor_tensor(samples(F[:, h, :]), bs[:, :, TQ - 1:TQ].to_broadcast([P, NSEQ, TQ]), bs,
                                      ALU.subtract)
            d.then_inc(s_d, 1)
            for h in range(HGH):
                dve.wait_ge(s_a, 6 + h)
                dve.tensor_tensor(QE[:, h, :], QE[:, h, :], core.M[:, h, :], ALU.mult).then_inc(s_d, 1)
            dve.wait_ge(s_a, 10)
            for h in range(HGH):
                dve.tensor_tensor(F[:, h, :], F[:, h, :], KK[:, h, :], ALU.mult)
            ada.finish(dve)


def hgrn_pairs(nc, core, tag, B, KK, A):
    with ExitStack() as es:
        sb, sem = scope(nc, es, tag)
        E = sb("decay", [P, 2, TP])
        Qt = sb("q_scaled", [P, 2, TP])
        Kt = sb("k_scaled", [P, 2, TP])
        ada = AdaPart(core, sb, sem, [(0, 10), (0, 11)] + [(1, c) for c in range(4)], 6, 7)
        s_d, s_a, s_e, s_q, s_k, s_mm, s_A, s_A0 = (sem(n) for n in (
            "diff", "abs_out", "exp_out", "q_out", "k_out", "mm", "kept", "zeroed"))
        PS = core.PS
        units = [(h, l) for h in range(HGH) for l in range(LEVELS)]
        number = lambda u: u - u // LEVELS - 1
        width = lambda l: T if l <= 3 else SEQ
        masks = cols(core, "levels").bitcast(I32).rearrange("p (l t) -> p l t", l=LEVELS)
        block = es.enter_context(nc.Block())

        @block.sync
        def _(sp):
            ada.load(sp)

        @block.vector
        def _(dve):
            dve.memset(A[:, :, :, :], 0.0).then_inc(s_A0, 1)

            def diff(u):
                h, l = units[u]
                if l == 0:
                    return
                e, n, half = number(u), width(l), 2 ** (l - 1)
                if e >= 2:
                    dve.wait_ge(s_q, e - 1)
                    dve.wait_ge(s_k, e - 1)
                b = B[:, h, 0:n].rearrange("p (n t) -> p n t", t=2 * half)
                c = b[:, :, half - 1:half].to_broadcast([P, n // (2 * half), 2 * half])
                dve.tensor_tensor(E[:, e % 2, 0:n].rearrange("p (n t) -> p n t", t=2 * half), b, c,
                                  ALU.subtract).then_inc(s_d, 1)

            def keep(u):
                h, l = units[u]
                dve.wait_ge(s_mm, u + 1)
                dve.wait_ge(s_A0, 1)
                s = 3 * (u % 2)
                if u:
                    dve.wait_ge(s_A, u)
                for b in range(2):
                    q = dve.copy_predicated(A[:, h, 4 * b:4 * b + 4, :], masks[:, l:l + 1, :].to_broadcast([P, 4, P]),
                                            PS[:, s + b, :].rearrange("p (c t) -> p c t", c=4))
                if l <= 3:
                    q = dve.copy_predicated(A[0:NS, h, 8, 0:NS], masks[0:NS, l, 0:NS], PS[0:NS, s + 2, 0:NS])
                q.then_inc(s_A, 1)

            diff(1)
            for u in range(len(units)):
                h, l = units[u]
                e, n = number(u), width(l)
                if l > 0:
                    dve.wait_ge(s_e, e + 1)
                    if e >= 2:
                        dve.wait_ge(s_mm, u - 1)
                    dve.tensor_tensor(Kt[:, e % 2, 0:n], KK[:, h, 0:n], E[:, e % 2, 0:n], ALU.mult).then_inc(s_k, 1)
                if u + 2 < len(units):
                    diff(u + 2)
                if u >= 1:
                    keep(u - 1)
            keep(len(units) - 1)
            ada.finish(dve)

        @block.scalar
        def _(act):
            for u, (h, l) in enumerate(units):
                if u >= 6 and (u - 2) % 4 == 0 and (u - 6) // 4 < len(ada.chunks):
                    ada.copy(act, (u - 6) // 4)
                if l == 0:
                    continue
                e, n = number(u), width(l)
                act.wait_ge(s_d, e + 1)
                act.activation(E[:, e % 2, 0:n], E[:, e % 2, 0:n], ACT.Abs).then_inc(s_a, 1)
                act.wait_ge(s_a, e + 1)
                act.activation(E[:, e % 2, 0:n], E[:, e % 2, 0:n], ACT.Exp, scale=-1.0).then_inc(s_e, 1)

        @block.gpsimd
        def _(pool):
            for u, (h, l) in enumerate(units):
                if l == 0:
                    continue
                e, n = number(u), width(l)
                pool.wait_ge(s_e, e + 1)
                if e >= 2:
                    pool.wait_ge(s_mm, u - 1)
                pool.tensor_tensor(Qt[:, e % 2, 0:n], core.M[:, h, 0:n], E[:, e % 2, 0:n], ALU.mult).then_inc(s_q, 1)

        @block.tensor
        def _(pe):
            for u, (h, l) in enumerate(units):
                e = number(u)
                if l > 0:
                    pe.wait_ge(s_q, e + 1)
                    pe.wait_ge(s_k, e + 1)
                if u >= 2:
                    pe.wait_ge(s_A, u - 1)
                kt = KK[:, h, :] if l == 0 else Kt[:, e % 2, :]
                qt = core.M[:, h, :] if l == 0 else Qt[:, e % 2, :]
                s = 3 * (u % 2)
                for c in range(8):
                    q = pe.matmul(PS[:, s + c // 4, (c % 4) * P:(c % 4 + 1) * P], kt[:, c * P:(c + 1) * P],
                                  qt[:, c * P:(c + 1) * P], start=True, stop=True)
                if l <= 3:
                    q = pe.matmul(PS[0:NS, s + 2, 0:NS], kt[:, SEQ:T], qt[:, SEQ:T], start=True, stop=True)
                q.then_inc(s_mm, 1)
                if u < ada.units:
                    ada.product(pe, u)
            ada.turn(pe, len(ada.chunks) - 1)


def hgrn_states(nc, core, tag, B, QE, A):
    with ExitStack() as es:
        sb, sem = scope(nc, es, tag)
        IT = sb("v_rows", [P, 9, P])
        KH = sb("k_rows", [P, 9, P])
        S = sb("state", [P, 9, P])
        S0 = sb("s_state", [P, NSEQ, P])
        VB = sb("v_blocks", [NS, NSEQ, P])
        eb = sb("decay_end", [P, HGH, 8 + NSEQ])
        s_s0, s_eb, s_T, s_c, s_vb, s_ds, s_S, s_Sz, s_o, s_oc, s_sm, s_ss = (sem(n) for n in (
            "s0_in", "decay_out", "turned", "rows_out", "blocks_out", "ds_mm", "state_out", "state_zero", "o_mm", "o_out",
            "s_scaled", "s_new"))
        s_out = [sem("S_stored"), sem("Ss_stored")]
        PS = core.PS
        block = es.enter_context(nc.Block())

        @block.sync
        def _(sp):
            for h in range(HGH):
                if h:
                    sp.wait_ge(s_out[1], 16 * h)
                    sp.wait_ge(s_o, h)
                sp.dma_start(S0[:, :, :], core.state_hgrn[0, :, h].rearrange("s k v -> k s v")).then_inc(s_s0, 16)
                sp.wait_ge(s_S, 8 * (h + 1))
                sp.dma_start(core.o_S_p[0, 0, h], S[:, 8, :]).then_inc(s_out[0], 16)
                sp.wait_ge(s_ss, h + 1)
                sp.dma_start(core.o_S_s[0, :, h].rearrange("s k v -> k s v"), S0[:, :, :]).then_inc(s_out[1], 16)
            sp.wait_ge(s_out[0], 16 * HGH)
            sp.wait_ge(s_out[1], 16 * HGH)

        @block.scalar
        def _(act):
            for h in range(HGH):
                act.activation(eb[:, h, 0:8], B[:, h, 0:SEQ].rearrange("p (c t) -> p c t", t=CH)[:, :, CH - 1], ACT.Exp)
                q = act.activation(eb[:, h, 8:8 + NSEQ], samples(B[:, h, :])[:, :, TQ - 1], ACT.Exp)
            q.then_inc(s_eb, 1)

        @block.tensor
        def _(pe):
            for h in range(HGH):
                for w, src in enumerate((core.BIG[:, HGH + h, :], core.BIG[:, h, :])):
                    if w:
                        pe.wait_ge(s_c, 2 * h + 1)
                    elif h:
                        pe.wait_ge(s_oc, h)
                    for i in range(9):
                        n = P if i < 8 else NS
                        q = pe.transpose(PS[0:n, i // 4, (i % 4) * P:(i % 4 + 1) * P], src[:, i * P:i * P + n],
                                         cols(core, "ident"))
                    q.then_inc(s_T, 1)
                pe.wait_ge(s_c, 2 * h + 2)
                if h:
                    pe.wait_ge(s_S, 8 * h)
                    pe.wait_ge(s_ss, h)
                for c in range(8):
                    pe.matmul(PS[:, 3 + c // 4, (c % 4) * P:(c % 4 + 1) * P], KH[:, c, :], IT[:, c, :], start=True, stop=True)
                pe.wait_ge(s_vb, h + 1)
                for b in range(2):
                    q = pe.matmul(PS[:, 5 + b, :], KH[0:NS, 8, :], VB[:, 4 * b:4 * b + 4, :].rearrange("p s v -> p (s v)"),
                                  start=True, stop=True)
                q.then_inc(s_ds, 1)
                for c in range(8):
                    o = PS[:, c // 4, (c % 4) * P:(c % 4 + 1) * P]
                    pe.matmul(o, IT[:, c, :], A[:, h, c, :], start=True, stop=(c == 0))
                    if c:
                        pe.wait_ge(s_S, 8 * h + c)
                        pe.matmul(o, S[:, c, :], QE[:, h, c * P:(c + 1) * P], start=False, stop=True)
                pe.wait_ge(s_s0, 16 * (h + 1))
                pe.matmul(PS[:, 2, 0:NS], IT[0:NS, 8, :], A[0:NS, h, 8, 0:NS], start=True, stop=True)
                for j in range(NSEQ):
                    q = pe.matmul(PS[:, 2, j * TQ:(j + 1) * TQ], S0[:, j, :], QE[:, h, SEQ + j * TQ:SEQ + (j + 1) * TQ],
                                  start=False, stop=True, skip_group_check=True)
                q.then_inc(s_o, 1)

        @block.vector
        def _(dve):
            dve.wait_ge(s_eb, 1)
            for h in range(HGH):
                for w, dst in enumerate((IT, KH)):
                    dve.wait_ge(s_T, 2 * h + w + 1)
                    dve.tensor_copy(dst[:, 0:8, :], PS[:, 0:2, :].rearrange("p b (c t) -> p (b c) t", c=4))
                    dve.tensor_copy(dst[0:NS, 8, :], PS[0:NS, 2, 0:P]).then_inc(s_c, 1)
                dve.wait_ge(s_c, 2 * h + 2)
                dve.tensor_tensor(VB[:, :, :], IT[0:NS, 8:9, :].to_broadcast([NS, NSEQ, P]),
                                  cols(core, "blk")[0:NS, :].unsqueeze(2).to_broadcast([NS, NSEQ, P]), ALU.mult)\
                   .then_inc(s_vb, 1)
                dve.wait_ge(s_ds, h + 1)
                if h:
                    dve.wait_ge(s_out[0], 16 * h)
                for c in range(8):
                    ds = PS[:, 3 + c // 4, (c % 4) * P:(c % 4 + 1) * P]
                    if c == 0:
                        dve.tensor_copy(S[:, 1, :], ds).then_inc(s_S, 1)
                    else:
                        dve.wait_ge(s_S, 8 * h + c)
                        dve.scalar_tensor_tensor(out=S[:, c + 1, :], in0=S[:, c, :], scalar=eb[:, h, c:c + 1], in1=ds,
                                                 op0=ALU.mult, op1=ALU.add).then_inc(s_S, 1)
                dve.wait_ge(s_o, h + 1)
                for b in range(2):
                    dve.tensor_copy(core.M[:, h, b * 512:(b + 1) * 512], PS[:, b, :])
                dve.tensor_copy(core.M[:, h, SEQ:T], PS[:, 2, 0:NS]).then_inc(s_oc, 1)
                dve.tensor_tensor(S0[:, :, :], S0[:, :, :], eb[:, h, 8:8 + NSEQ].unsqueeze(2).to_broadcast([P, NSEQ, P]),
                                  ALU.mult).then_inc(s_sm, 1)
                dve.wait_ge(s_sm, h + 1)
                dve.tensor_tensor(S0[:, :, :], S0[:, :, :], PS[:, 5:7, :].rearrange("p b (s v) -> p (b s) v", v=P),
                                  ALU.add).then_inc(s_ss, 1)


def hgrn_gate(nc, core, tag):
    with ExitStack() as es:
        sb, sem = scope(nc, es, tag)
        sq = sb("sq", [P, 2, TP])
        r = sb("rstd", [P, TP])
        s_sg, s_sq, s_ss, s_rt, s_r, s_bc, s_y, s_z = (sem(n) for n in (
            "silu", "sq_out", "sumsq", "root_out", "rstd", "rstd_spread", "y", "pads"))
        G = core.BIG[:, 2 * HGH:3 * HGH, :]
        PS = core.PS
        block = es.enter_context(nc.Block())

        @block.scalar
        def _(act):
            act.wait_ge(s_z, 1)
            for h in range(HGH):
                if h >= 2:
                    act.wait_ge(s_ss, h - 1)
                act.activation(sq[:, h % 2, :], core.M[:, h, :], ACT.Square).then_inc(s_sq, 1)
            for h in range(HGH):
                act.wait_ge(s_ss, HGH)
                act.activation(chunked(r[32 * h:32 * h + 1, :]), PS[32 * h:32 * h + 1, 0:NC3, 0:CW], ACT.Sqrt, scale=1.0 / P,
                               bias=cols(core, "eps")[32 * h:32 * h + 1, :]).then_inc(s_rt, 1)
            for h in range(HGH):
                act.activation(G[:, h, :], G[:, h, :], ACT.Silu).then_inc(s_sg, 1)

        @block.tensor
        def _(pe):
            for h in range(HGH):
                pe.wait_ge(s_sq, h + 1)
                for c in range(NC3):
                    q = pe.matmul(PS[32 * h:32 * h + 1, c, 0:CW], cols(core, "ones"), sq[:, h % 2, c * CW:(c + 1) * CW],
                                  start=True, stop=True)
                q.then_inc(s_ss, 1)
            pe.wait_ge(s_r, 1)
            for h in range(HGH):
                if h >= 2:
                    pe.wait_ge(s_y, h - 1)
                b = 3 * ((h + 1) % 2)
                for c in range(NC3):
                    q = pe.matmul(PS[:, b + c, 0:CW], cols(core, "ones")[32 * h:32 * h + 1, :].to_broadcast([1, P]),
                                  r[32 * h:32 * h + 1, c * CW:(c + 1) * CW], start=True, stop=True)
                q.then_inc(s_bc, 1)

        @block.vector
        def _(dve):
            dve.memset(core.M[:, 0:HGH, T:TP], 0.0)
            dve.memset(r[:, :], 1.0).then_inc(s_z, 1)
            dve.wait_ge(s_rt, HGH)
            dve.reciprocal(r[:, :], r[:, :]).then_inc(s_r, 1)
            for h in range(HGH):
                dve.wait_ge(s_bc, h + 1)
                b = 3 * ((h + 1) % 2)
                m = chunked(core.M[:, h, :])
                dve.scalar_tensor_tensor(out=m, in0=m, scalar=core.vec[:, HG_G + h:HG_G + h + 1],
                                         in1=PS[:, b:b + 3, 0:CW], op0=ALU.mult, op1=ALU.mult).then_inc(s_y, 1)
                dve.wait_ge(s_y, h + 1)
                dve.wait_ge(s_sg, h + 1)
                dve.tensor_tensor(core.M[:, h, :], core.M[:, h, :], G[:, h, :], ALU.mult)


def hgrn(nc, core, tag):
    with ExitStack() as es:
        sb = lambda name, shape: es.enter_context(nc.sbuf_tensor(f"{tag}_{name}", shape, F32))
        B = sb("log_decay", [P, HGH, TP])
        QE = sb("q_decayed", [P, HGH, TP])
        A = sb("pairs", [P, HGH, 9, P])
        with nc.sbuf_tensor(f"{tag}_k", [P, HGH, TP], F32) as KK:
            hgrn_prepare(nc, core, tag + "_prep", B, QE, KK)
            hgrn_pairs(nc, core, tag + "_pairs", B, KK, A)
        hgrn_states(nc, core, tag + "_states", B, QE, A)
    hgrn_gate(nc, core, tag + "_gate")


UX = PH + SEQ + NSEQ * (PH + TQ)
GX = CHI + SEQ + NSEQ * (CHI + TQ)


def ext_parts(ap, hist):
    return ap[..., hist:hist + SEQ], ap[..., hist + SEQ:]


def odd_prepare(nc, core, tag, U, G):
    with ExitStack() as es:
        sb, sem = scope(nc, es, tag)
        hp = sb("pool_hist", [NSEQ * PH, HALF])
        hc = sb("conv_hist", [NSEQ * CHI // 2, 2, HALF])
        rows = sb("rows", [NS, 4, HALF])
        s_in, s_hist, s_sg, s_glu, s_T, s_ev, s_R, s_rc, s_kept = (sem(n) for n in (
            "hist_in", "hist_kept", "sigmoid", "glu", "turned", "hist_out", "rows_T", "rows_out", "hist_laid_out"))
        s_out = sem("stored")
        ada = AdaPart(core, sb, sem, [(1, c) for c in range(4, 8)], 3, 2, ring=4)
        PS = core.PS
        Ut, A_, GT = core.BIG[:, 0:4, :], core.BIG[:, 4:8, :], core.BIG[:, 8:12, :]
        block = es.enter_context(nc.Block())

        @block.sync
        def _(sp):
            sp.dma_start(hp[:, :], core.state_pool.rearrange("o b t f -> (o b t) f")).then_inc(s_in, 16)
            sp.dma_start(hc[:, :, :], core.state_conv.rearrange("o (h b) t f -> (o b t) h f", h=2)).then_inc(s_in, 16)
            sp.dma_start(core.o_pool_s[0, :, 0:PH - TQ, :], core.state_pool[0, :, TQ:PH, :]).then_inc(s_hist, 16)
            sp.dma_start(core.o_conv_s[0, :, 0:CHI - TQ, :], core.state_conv[0, :, TQ:CHI, :]).then_inc(s_hist, 16)
            ada.load(sp)
            sp.wait_ge(s_rc, 4)
            sp.dma_start(core.o_pool_p[0, 0], rows[0:PH, 0, :]).then_inc(s_out, 16)
            sp.dma_start(core.o_conv_p[0, 0], rows[0:CHI, 2, :]).then_inc(s_out, 16)
            for i, (dst, n) in enumerate(((core.o_pool_s, PH), (core.o_conv_s, CHI))):
                for b in range(NSEQ):
                    sp.dma_start(dst[0, b, n - TQ:n, :], rows[b * TQ:(b + 1) * TQ, 2 * i + 1, :]).then_inc(s_out, 16)
            sp.wait_ge(s_hist, 32)
            sp.wait_ge(s_out, 16 * (2 + 2 * NSEQ))

        @block.scalar
        def _(act):
            for k in range(HT):
                act.activation(GT[:, k, :], GT[:, k, :], ACT.Sigmoid).then_inc(s_sg, 1)
            ada.copies(act)

        @block.tensor
        def _(pe):
            pe.wait_ge(s_in, 32)
            ident = cols(core, "ident")
            for i in range(3):
                n = NSEQ * PH
                for k in range(HT):
                    src = hp[:, k * P:(k + 1) * P] if i == 0 else hc[:, i - 1, k * P:(k + 1) * P]
                    q = pe.transpose(PS[:, i, k * P:k * P + n], src, ident[0:n, 0:n])
                q.then_inc(s_T, 1)
            for i, (src, n) in enumerate(((Ut, PH), (Ut, NS), (A_, CHI), (A_, NS))):
                if i == 2:
                    pe.wait_ge(s_glu, HT)
                at = SEQ - n if n != NS else SEQ
                for k in range(HT):
                    q = pe.transpose(PS[0:n, 4 + i, k * P:(k + 1) * P], src[:, k, at:at + n], ident)
                q.then_inc(s_R, 1)
            pe.wait_ge(s_kept, 1)
            ada.products(pe)

        @block.vector
        def _(dve):
            dve.memset(U[:, :, 0:PH], 0.0)
            dve.memset(G[:, :, 0:CHI], 0.0)
            dve.wait_ge(s_T, 3)
            for k in range(HT):
                ux = U[:, k, PH + SEQ:].rearrange("p (s t) -> p s t", s=NSEQ)
                dve.tensor_copy(ux[:, :, 0:PH], PS[:, 0, k * P:k * P + NSEQ * PH].rearrange("p (s t) -> p s t", s=NSEQ))
                gx = G[:, k, CHI + SEQ:].rearrange("p (s t) -> p s t", s=NSEQ)
                for h in range(2):
                    q = dve.tensor_copy(gx[:, 4 * h:4 * h + 4, 0:CHI],
                                        PS[:, 1 + h, k * P:k * P + 4 * CHI].rearrange("p (s t) -> p s t", s=4))
            q.then_inc(s_kept, 1)
            for k in range(HT):
                dve.wait_ge(s_sg, k + 1)
                dve.tensor_tensor(A_[:, k, :], A_[:, k, :], GT[:, k, :], ALU.mult).then_inc(s_glu, 1)
            for i, n in enumerate((PH, NS, CHI, NS)):
                dve.wait_ge(s_R, i + 1)
                dve.tensor_copy(rows[0:n, i, :], PS[0:n, 4 + i, :]).then_inc(s_rc, 1)
            ada.finish(dve)

        @block.gpsimd
        def _(pool):
            for k in range(HT):
                pool.tensor_copy(U[:, k, PH:PH + SEQ], Ut[:, k, 0:SEQ])
                pool.tensor_copy(U[:, k, PH + SEQ:].rearrange("p (s t) -> p s t", s=NSEQ)[:, :, PH:], samples(Ut[:, k, :]))
            for k in range(HT):
                pool.wait_ge(s_glu, k + 1)
                pool.tensor_copy(G[:, k, CHI:CHI + SEQ], A_[:, k, 0:SEQ])
                pool.tensor_copy(G[:, k, CHI + SEQ:].rearrange("p (s t) -> p s t", s=NSEQ)[:, :, CHI:], samples(A_[:, k, :]))


def odd_branches(nc, core, tag, U, G, cv):
    with ExitStack() as es:
        sb, sem = scope(nc, es, tag)
        dg = sb("diag", [P, 2, P])
        sm = sb("sums", [P, 2, UX])
        pw = sb("pool_w", [P, HT, P])
        s_in, s_dg, s_tap, s_acc, s_cv, s_sum, s_pl, s_pp, s_pm, s_out = (sem(n) for n in (
            "pool_w_in", "diag_out", "tap_mm", "acc", "conv_out", "sum", "mean", "pooled", "pool_mm", "pool_out"))
        s_z = sem("pads")
        PS = core.PS
        NPE = 2
        ident = cols(core, "ident")
        block = es.enter_context(nc.Block())
        tail = lambda k: G[:, k, CHI + SEQ:].rearrange("p (s t) -> p s t", s=NSEQ)

        @block.sync
        def _(sp):
            sp.dma_start(pw[:, :, :], core.pool_w.rearrange("o g c d -> c (o g) d")).then_inc(s_in, 16)

        @block.scalar
        def _(act):
            for n in range(NPE):
                k = HT - NPE + n
                with act.Fori(0, (CWID - 1) // 2) as j:
                    for s in range(2):
                        act.wait_ge(s_tap, j * 2 + (n * (CWID + 1) + s + 1))
                        act.activation(dg[:, s, :], ident, ACT.Copy,
                                       scale=core.convw[:, bass.ds(j * (2 * HT) + (s * HT + k), 1)]).then_inc(s_dg, 1)
                act.wait_ge(s_tap, n * (CWID + 1) + CWID)
                act.activation(dg[:, 0, :], ident, ACT.Copy,
                               scale=core.convw[:, (CWID - 1) * HT + k:(CWID - 1) * HT + k + 1]).then_inc(s_dg, 1)
            for n in range(NPE):
                k = HT - NPE + n
                act.wait_ge(s_tap, 2 + (n + 1) * (CWID + 1) - 1)
                b = core.vec[:, CONV_B + k:CONV_B + k + 1]
                act.activation(cv[:, k, 0:SEQ], PS[:, 3 * n:3 * n + 2, :].rearrange("p b c -> p (b c)"), ACT.Identity, bias=b)
                act.activation(cv[:, k, SEQ:T], PS[:, 3 * n + 2, 0:NS], ACT.Identity, bias=b).then_inc(s_cv, 1)
            for g in range(HT):
                act.wait_ge(s_pm, g + 1)
                act.activation(chunked(core.M[:, g, :]), PS[:, 3 * (g % 2):3 * (g % 2) + 3, 0:CW], ACT.Copy,
                               scale=core.vec[:, POOL_S + g:POOL_S + g + 1]).then_inc(s_out, 1)

        @block.tensor
        def _(pe):
            pe.sem_inc(s_tap, 2)

            def tap(slot, n, k, at, first):
                b = 3 * n
                fl = dict(start=first, stop=True, skip_group_check=True)
                for h in range(2):
                    pe.matmul(PS[:, b + h, :], dg[:, slot, :], G[:, k, bass.ds(at + h * 512, 512)], **fl)
                return pe.matmul(PS[:, b + 2, 0:NS].rearrange("p (s t) -> p s t", s=NSEQ), dg[:, slot, :],
                                 tail(k)[:, :, bass.ds(at, TQ)], **fl)

            for n in range(NPE):
                k = HT - NPE + n
                base = n * CWID
                for s in range(2):
                    pe.wait_ge(s_dg, base + s + 1)
                    tap(s, n, k, s, s == 0).then_inc(s_tap, 1)
                with pe.Fori(0, (CWID - 3) // 2) as j:
                    for s in range(2):
                        pe.wait_ge(s_dg, j * 2 + (base + s + 3))
                        tap(s, n, k, j * 2 + (s + 2), False).then_inc(s_tap, 1)
                pe.wait_ge(s_dg, base + CWID)
                tap(0, n, k, CWID - 1, False).then_inc(s_tap, 2)
            pe.wait_ge(s_in, 16)
            for g in range(HT):
                pe.wait_ge(s_pp, g + 1)
                if g < 2:
                    pe.wait_ge(s_cv, g + 1)
                else:
                    pe.wait_ge(s_out, g - 1)
                for c in range(NC3):
                    q = pe.matmul(PS[:, 3 * (g % 2) + c, 0:CW], pw[:, g, :], core.BIG[:, g, c * CW:(c + 1) * CW],
                                  start=True, stop=True)
                q.then_inc(s_pm, 1)

        @block.vector
        def _(dve):
            dve.memset(cv[:, :, T:TP], 0.0).then_inc(s_z, 1)
            dve.sem_inc(s_acc, 2)
            for k in range(HT - NPE):
                b, w0 = core.vec[:, CONV_B + k:CONV_B + k + 1], core.convw[:, k:k + 1]
                dve.tensor_scalar(cv[:, k, 0:SEQ], G[:, k, 0:SEQ], w0, b, ALU.mult, ALU.add)
                dve.tensor_scalar(samples(cv[:, k, :]), tail(k)[:, :, 0:TQ], w0, b, ALU.mult, ALU.add).then_inc(s_acc, 1)
            with dve.Fori(1, CWID) as j:
                for k in range(HT - NPE):
                    w = core.convw[:, bass.ds(j * HT + k, 1)]
                    dve.wait_ge(s_acc, j * 2 + (k + 1))
                    dve.scalar_tensor_tensor(out=cv[:, k, 0:SEQ], in0=G[:, k, bass.ds(j, SEQ)], scalar=w,
                                             in1=cv[:, k, 0:SEQ], op0=ALU.mult, op1=ALU.add)
                    dve.scalar_tensor_tensor(out=samples(cv[:, k, :]), in0=tail(k)[:, :, bass.ds(j, TQ)], scalar=w,
                                             in1=samples(cv[:, k, :]), op0=ALU.mult, op1=ALU.add).then_inc(s_acc, 1)

        @block.gpsimd
        def _(pool):
            n = 0
            for g, w in enumerate(WINDOWS):
                src, h = U[:, g, :], 1
                while h < w:
                    if n:
                        pool.wait_ge(s_sum, n)
                    n += 1
                    dst = sm[:, n % 2, :]
                    pool.tensor_tensor(dst[:, 2 * h - 1:UX], src[:, 2 * h - 1:UX], src[:, h - 1:UX - h], ALU.add).then_inc(s_sum, 1)
                    src, h = dst, 2 * h
                pool.wait_ge(s_sum, n)
                u = core.BIG[:, g, :]
                pool.tensor_tensor(src[:, PH:PH + 16], src[:, PH:PH + 16], cols(core, "cnt", 16 * g, 16 * g + 16), ALU.mult)\
                    .then_inc(s_pl, 1)
                pool.wait_ge(s_pl, 2 * g + 1)
                pool.tensor_scalar(src[:, PH:UX], src[:, PH:UX], 1.0 / w, None, ALU.mult).then_inc(s_pl, 1)
                pool.wait_ge(s_pl, 2 * g + 2)
                pool.tensor_tensor(u[:, 0:SEQ], src[:, PH:PH + SEQ], u[:, 0:SEQ], ALU.subtract)
                sx = src[:, PH + SEQ:].rearrange("p (s t) -> p s t", s=NSEQ)[:, :, PH:]
                pool.tensor_tensor(samples(u), sx, samples(u), ALU.subtract).then_inc(s_pp, 1)
                if g + 1 < HT:
                    pool.wait_ge(s_pp, g + 1)


def odd_norm(nc, core, tag, cv):
    SUMS = 40
    with ExitStack() as es:
        sb, sem = scope(nc, es, tag)
        sq = sb("sq", [P, HT, TP])
        mu = sb("mu", [P, TP])
        rt = sb("root", [TB, NBK])
        r = sb("rstd", [TB, NBK])
        s_bc, s_sum = sem("rstd_spread"), sem("squares_added")
        s_mu, s_muc, s_c, s_sq, s_ss, s_rt, s_r, s_y, s_o, s_z = (sem(n) for n in (
            "mean_mm", "mean_out", "centred", "sq_out", "sumsq", "root_out", "rstd", "y", "out", "pads"))
        ada = AdaPart(core, sb, sem, [(1, c) for c in range(8, 12)], 7, 6)
        PS = core.PS
        block = es.enter_context(nc.Block())

        @block.sync
        def _(sp):
            ada.load(sp)

        @block.tensor
        def _(pe):
            for k in range(HT):
                for c in range(NC3):
                    q = pe.matmul(PS[:, c, 0:CW], cols(core, "ones").to_broadcast([P, P]), cv[:, k, c * CW:(c + 1) * CW],
                                  start=(k == 0), stop=(k == HT - 1))
            q.then_inc(s_mu, 1)
            for n in range(8):
                ada.product(pe, n)
            pe.wait_ge(s_sum, HT - 1)
            column_sums(pe, core, 6, SUMS, sq[:, 0, :], True).then_inc(s_ss, 1)
            pe.wait_ge(s_r, 1)
            spread(pe, core, 3, r).then_inc(s_bc, 1)
            for n in range(8, ada.units):
                ada.product(pe, n)
            ada.turn(pe, len(ada.chunks) - 1)

        @block.scalar
        def _(act):
            act.wait_ge(s_mu, 1)
            act.activation(chunked(mu[:, :]), PS[:, 0:NC3, 0:CW], ACT.Copy, scale=1.0 / HALF).then_inc(s_muc, 1)
            for k in range(HT):
                act.wait_ge(s_c, k + 1)
                act.activation(sq[:, k, :], cv[:, k, :], ACT.Square).then_inc(s_sq, 1)
                if k >= 2:
                    ada.copy(act, k - 2)
            act.wait_ge(s_ss, 1)
            act.activation(rt[:, :], PS[0:TB, 6, SUMS * NBK:(SUMS + 1) * NBK], ACT.Sqrt, scale=1.0 / HALF,
                           bias=cols(core, "eps")[0:TB, :]).then_inc(s_rt, 1)
            for k in range(HT):
                act.wait_ge(s_y, k + 1)
                act.activation(core.M[:, HT + k, :], cv[:, k, :], ACT.Silu, scale=core.vec[:, LN_G + k:LN_G + k + 1],
                               bias=core.vec[:, LN_B + k:LN_B + k + 1]).then_inc(s_o, 1)
                if k >= 2:
                    ada.copy(act, k)

        @block.vector
        def _(dve):
            dve.wait_ge(s_muc, 1)
            for k in range(HT):
                dve.tensor_tensor(cv[:, k, :], cv[:, k, :], mu[:, :], ALU.subtract).then_inc(s_c, 1)
            dve.wait_ge(s_rt, 1)
            dve.reciprocal(r[:, :], rt[:, :]).then_inc(s_r, 1)
            dve.wait_ge(s_bc, 1)
            for k in range(HT):
                dve.tensor_tensor(chunked(cv[:, k, :]), chunked(cv[:, k, :]), PS[:, 3:6, 0:CW], ALU.mult).then_inc(s_y, 1)
            dve.wait_ge(s_o, HT)
            dve.memset(core.M[:, HT:2 * HT, T:TP], 0.0)
            ada.finish(dve)

        @block.gpsimd
        def _(pool):
            for k in range(1, HT):
                pool.wait_ge(s_sq, k + 1)
                if k >= 2:
                    pool.wait_ge(s_sum, k - 1)
                pool.tensor_tensor(sq[:, 0, :], sq[:, 0, :], sq[:, k, :], ALU.add).then_inc(s_sum, 1)


def odd_mixer(nc, core, tag):
    with ExitStack() as es:
        sb = lambda name, shape: es.enter_context(nc.sbuf_tensor(f"{tag}_{name}", shape, F32))
        G = sb("glu", [P, HT, GX])
        cv = sb("conv", [P, HT, TP])
        U = sb("u", [P, HT, UX])
        odd_prepare(nc, core, tag + "_prep", U, G)
        odd_branches(nc, core, tag + "_branches", U, G, cv)
        odd_norm(nc, core, tag + "_norm", cv)


INPUTS = ["x_prompt", "x_sample", "c_prompt", "c_sample", "cache_sb_k", "cache_sb_v", "state_hgrn", "state_pool",
          "state_conv", "page_table", "norm_g", "ada_w", "ada_b", "even_w_in", "even_w_out", "sb_bias",
          "hgrn_lb_logits", "hgrn_norm_g", "odd_w_in", "odd_w_out", "pool_w", "pool_scale", "conv_w", "conv_b",
          "conv_ln_g", "conv_ln_b", "mlp_w1", "mlp_w2"]

OUTPUTS = [("y_prompt", (1, SEQ, D)), ("y_sample", (NSEQ, TQ, D)),
           ("sb_k_prompt", (1, 1, SEQ, SBH, SBD)), ("sb_v_prompt", (1, 1, SEQ, SBH, SBD)),
           ("sb_k_sample", (1, NSEQ, TQ, SBH, SBD)), ("sb_v_sample", (1, NSEQ, TQ, SBH, SBD)),
           ("hgrn_prompt", (1, 1, HGH, P, P)), ("hgrn_sample", (1, NSEQ, HGH, P, P)),
           ("pool_prompt", (1, 1, PH, HALF)), ("pool_sample", (1, NSEQ, PH, HALF)),
           ("conv_prompt", (1, 1, CHI, HALF)), ("conv_sample", (1, NSEQ, CHI, HALF))]


def open_core(nc, es, ins):
    c = Core()
    (c.x_prompt, c.x_sample, c.c_prompt, c.c_sample, c.cache_k, c.cache_v, c.state_hgrn, c.state_pool,
     c.state_conv, c.page_table, c.norm_g, c.ada_w, c.ada_b, c.even_w_in, c.even_w_out, c.sb_bias,
     c.hgrn_lb_logits, c.hgrn_norm_g, c.odd_w_in, c.odd_w_out, c.pool_w, c.pool_scale, c.conv_w, c.conv_b,
     c.conv_ln_g, c.conv_ln_b, c.mlp_w1, c.mlp_w2) = (ins[n] for n in INPUTS)
    c.even_w_in, c.even_w_out, c.odd_w_in, c.odd_w_out = (w[0] for w in (c.even_w_in, c.even_w_out, c.odd_w_in, c.odd_w_out))
    c.const_in = ins["consts"]
    sb = lambda n, s, d=F32: es.enter_context(nc.sbuf_tensor(n, s, d))
    c.const = sb("const", [P, NCONST])
    c.mod = sb("mod", [P, 2, N_MOD * KT * SEGP])
    c.coef = sb("coef", [P, 2, 4, KT * SEGP])
    c.ada_bT = sb("ada_bT", [P, 96])
    c.vec = sb("vec", [P, VP])
    c.convw = sb("convw", [P, CWID * HT])
    c.sb_bias_bc = sb("sb_bias_bc", [P, SBH])
    c.cT = sb("cT", [P, KT, SEGP])
    c.M = sb("M", [P, KT, TP])
    (c.o_y_p, c.o_y_s, c.o_k_p, c.o_v_p, c.o_k_s, c.o_v_s, c.o_S_p, c.o_S_s, c.o_pool_p, c.o_pool_s, c.o_conv_p,
     c.o_conv_s) = (ins[n] for n, _ in OUTPUTS)
    c.x_dram = nc.dram_tensor("x_scratch", [P, KT * TP], F32, kind="Internal").ap()
    c.PS = es.enter_context(nc.psum_tensor("PS", [P, 8, 512], F32))
    return c


def rows_out(nc, core, tag, X):
    with ExitStack() as es:
        sb, sem = scope(nc, es, tag)
        rows = sb("rows", [P, 2, D])
        s_T, s_cp = sem("turned"), sem("copied")
        s_out = [sem(f"stored{i}") for i in range(2)]
        PS = core.PS
        n_rows = lambda i: P if i < 8 else NS
        block = es.enter_context(nc.Block())

        @block.tensor
        def _(pe):
            for i in range(9):
                if i >= 2:
                    pe.wait_ge(s_cp, i - 1)
                n = n_rows(i)
                for k in range(KT):
                    q = pe.transpose(PS[0:n, 2 * (i % 2) + k // 4, (k % 4) * P:(k % 4 + 1) * P],
                                     X[:, k, i * P:i * P + n], cols(core, "ident"))
                q.then_inc(s_T, 1)

        @block.vector
        def _(dve):
            for i in range(9):
                dve.wait_ge(s_T, i + 1)
                if i >= 2:
                    dve.wait_ge(s_out[i % 2], 16 * (i // 2))
                n = n_rows(i)
                dve.tensor_copy(rows[0:n, i % 2, :], PS[0:n, 2 * (i % 2):2 * (i % 2) + 2, :].rearrange("p b c -> p (b c)"))\
                   .then_inc(s_cp, 1)

        @block.sync
        def _(sp):
            for i in range(9):
                sp.wait_ge(s_cp, i + 1)
                dst = core.o_y_p[0, i * P:(i + 1) * P, :] if i < 8 else core.o_y_s.rearrange("b t d -> (b t) d")
                sp.dma_start(dst, rows[0:n_rows(i), i % 2, :]).then_inc(s_out[i % 2], 16)
            sp.wait_ge(s_out[0], 16 * 5)
            sp.wait_ge(s_out[1], 16 * 4)


def flat(tiles):
    return tiles.rearrange("p a b -> p (a b)")


def step(nc, ins):
    with ExitStack() as top:
        core = open_core(nc, top, ins)
        M = core.M
        with nc.sbuf_tensor("big0", [P, 3 * HT, TP], F32) as big:
            core.BIG = big
            setup(nc, core, "setup", big[:, 0:KT, :])
            with ExitStack() as es:
                open_split(nc, es, core, "in0")
                residual_norm(nc, core, "norm00", big[:, 0:KT, :], False, None, None, (0, 0), (0, 0), True)
                KV = big[:, 0:KT, :]
                values = flat(big[:, KT:KT + HT, :])[:, 0:8 * HALF].rearrange("p (i f) -> p i f", f=HALF)
                sb_at = 4 * HALF
                dense(nc, core, "qkv", core.even_w_in, [(sb_at, HT, M[:, HT:2 * HT, :]), (sb_at + HALF, 2 * HT, KV)])
                sb_prompt(nc, core, "sb_prompt", KV, values, flat(M[:, 0:HT, :]))
                sb_sample(nc, core, "sb_sample", KV, flat(M[:, 0:HT, :]), flat(big[:, KT:KT + HT, :]))
                dense(nc, core, "qfig", core.even_w_in, [(0, HT, M[:, 0:HT, :]), (HALF, 3 * HT, big)])
            hgrn(nc, core, "hgrn")
        mlp_of_layer(nc, core, 0, core.even_w_out, M)
        with nc.sbuf_tensor("big1", [P, 3 * HT, TP], F32) as big:
            core.BIG = big
            with ExitStack() as es:
                open_split(nc, es, core, "in1")
                residual_norm(nc, core, "norm10", big[:, 0:KT, :], True, M, (0, 3), (1, 0), (1, 0), True)
                dense(nc, core, "odd_in", core.odd_w_in, [(0, 3 * HT, big)])
            odd_mixer(nc, core, "odd")
        mlp_of_layer(nc, core, 1, core.odd_w_out, M)
        with nc.sbuf_tensor("x_end", [P, KT, TP], F32) as X:
            residual_norm(nc, core, "norm_end", X, True, M, (1, 3), None, None, False, final=True)
            rows_out(nc, core, "rows", X)


def mlp_of_layer(nc, core, l, w_out, M):
    with ExitStack() as es:
        open_split(nc, es, core, f"mid{l}")
        dense(nc, core, f"out{l}", w_out, [(0, KT, M)], src=M)
        with nc.sbuf_tensor(f"x_mid{l}", [P, KT, TP], F32) as X:
            residual_norm(nc, core, f"norm{l}1", X, True, M, (l, 1), (l, 2), (l, 3 * KT), True)
        mlp(nc, core, f"mlp{l}", core.mlp_w1[l], core.mlp_w2[l], M)


def kernel(**inputs):
    import concourse.bacc as bacc
    from concourse.bass_utils import run_bass_kernel_spmd

    nc = bacc.Bacc("TRN2", target_bir_lowering=False, num_devices=1)
    arrays = {name: np.ascontiguousarray(inputs[name]) for name in INPUTS}
    arrays["consts"] = constants()
    aps = {name: nc.dram_tensor(name, a.shape, mybir.dt.from_np(a.dtype), kind="ExternalInput").ap()
           for name, a in arrays.items()}
    for name, shape in OUTPUTS:
        aps[name] = nc.dram_tensor(name, shape, F32, kind="ExternalOutput").ap()
    step(nc, aps)
    result = run_bass_kernel_spmd(nc, [arrays], core_ids=[0])
    return tuple(result.results[0][name] for name, _ in OUTPUTS)
```
